# Optimizing a Trainium2 kernel written in Bass

```python
import jax, jax.numpy as jnp
from jax import lax
import numpy as np

D_MODEL = 1024
BATCH = 1
SEQ = 256
DEPTH = 2

NSA_HEADS = 8
NSA_GROUPS = 2
NSA_HPG = NSA_HEADS // NSA_GROUPS
NSA_DK = 64
NSA_DV = 64
CMP_BLOCK = 32
CMP_STRIDE = 16
SLC_BLOCK = 64
N_SELECT = 16
WINDOW = 512
MLA_HEADS = 8
MLA_NOPE = 64
MLA_ROPE = 32
MLA_V = 64
MLA_Q_RANK = 384
MLA_KV_RANK = 256
ROPE_THETA = 10000.0
D_FF = 2816
N_MOD = 9
Q_BLOCK = 128
NORM_EPS = 1e-6

IN_SPLITS = (
    NSA_HEADS * NSA_DK,
    NSA_GROUPS * NSA_DK,
    NSA_GROUPS * NSA_DV,
    NSA_GROUPS * NSA_DK,
    NSA_GROUPS * NSA_DV,
    NSA_GROUPS * NSA_DK,
    NSA_GROUPS * NSA_DV,
    3 * NSA_HEADS,
    MLA_Q_RANK,
    MLA_KV_RANK,
    MLA_ROPE,
    2 * D_MODEL,
)
IN_TOTAL = sum(IN_SPLITS)


def rms_norm(x):
    xf = x.astype(jnp.float32)
    return (xf * lax.rsqrt(jnp.mean(xf * xf, -1, keepdims=True) + NORM_EPS)).astype(x.dtype)

def modulate(x, shift, scale):
    return rms_norm(x) * (1 + scale[:, None, :]) + shift[:, None, :]

def swiglu(u, w_gate, w_up, w_down):
    return (jax.nn.silu(u @ w_gate) * (u @ w_up)) @ w_down

def masked_softmax(scores, mask):
    s = jnp.where(mask, scores.astype(jnp.float32), -jnp.inf)
    m = jnp.max(s, -1, keepdims=True)
    m = jnp.where(jnp.isfinite(m), m, 0.0)
    p = jnp.exp(s - m)
    return p / jnp.maximum(jnp.sum(p, -1, keepdims=True), 1.0)

def rope(x, cos, sin):
    half = x.shape[-1] // 2
    x1, x2 = x[..., :half], x[..., half:]
    return jnp.concatenate([x1 * cos - x2 * sin, x1 * sin + x2 * cos], -1).astype(x.dtype)

def alibi_slopes(n):
    return 2.0 ** (-8.0 * jnp.arange(1, n + 1, dtype=jnp.float32) / n)

def compress(k, w1, w2, pe):
    B, G, S, d = k.shape
    n_chunks = S // CMP_STRIDE
    r = CMP_BLOCK // CMP_STRIDE
    n_cmp = n_chunks - r + 1
    chunks = k.reshape(B, G, n_chunks, CMP_STRIDE, d)
    blocks = jnp.concatenate([chunks[:, :, j:j + n_cmp] for j in range(r)], axis=3)
    blocks = (blocks + pe).reshape(B, G, n_cmp, CMP_BLOCK * d)
    return jax.nn.gelu(blocks @ w1) @ w2

def nsa_attention(q, k_c, v_c, k_s, v_s, k_w, v_w, gates):
    B, G, HPG, S, dk = q.shape
    dv = v_c.shape[-1]
    nq = S // Q_BLOCK
    n_slc = S // SLC_BLOCK
    n_top = min(N_SELECT, n_slc)
    n_cmp = k_c.shape[2]
    ratio = SLC_BLOCK // CMP_STRIDE
    r = CMP_BLOCK // CMP_STRIDE
    cmp_end = jnp.arange(n_cmp) * CMP_STRIDE + CMP_BLOCK - 1
    ks_blocks = k_s.reshape(B, G, n_slc, SLC_BLOCK, dk)
    vs_blocks = v_s.reshape(B, G, n_slc, SLC_BLOCK, dv)
    kw_pad = jnp.pad(k_w, ((0, 0), (0, 0), (WINDOW, 0), (0, 0)))
    vw_pad = jnp.pad(v_w, ((0, 0), (0, 0), (WINDOW, 0), (0, 0)))
    slope = alibi_slopes(NSA_HEADS).reshape(1, G, HPG, 1, 1)
    scale = dk ** -0.5
    b_ix = jnp.arange(B)[:, None, None, None]
    g_ix = jnp.arange(G)[None, :, None, None]
    blk = jnp.arange(n_slc)

    def block(i):
        q0 = i * Q_BLOCK
        qb = lax.dynamic_slice_in_dim(q, q0, Q_BLOCK, axis=3)
        gb = lax.dynamic_slice_in_dim(gates, q0, Q_BLOCK, axis=3)
        t = q0 + jnp.arange(Q_BLOCK)
        d_c = (t[:, None] - cmp_end[None, :]).astype(jnp.float32)
        s_c = jnp.einsum('bghqd,bgnd->bghqn', qb, k_c).astype(jnp.float32) * scale - slope * d_c
        p_c = masked_softmax(s_c, cmp_end[None, :] <= t[:, None])
        o_c = jnp.einsum('bghqn,bgnd->bghqd', p_c.astype(v_c.dtype), v_c)
        imp = jnp.pad(p_c.sum(axis=2), ((0, 0), (0, 0), (0, 0), (r - 1, n_slc * ratio - n_cmp)))
        imp_s = imp[..., 0:ratio * n_slc:ratio]
        for j in range(1, ratio + r - 1):
            imp_s = imp_s + imp[..., j:j + ratio * n_slc:ratio]
        cur = t // SLC_BLOCK
        forced = (blk[None, :] == 0) | (blk[None, :] == cur[:, None]) | (blk[None, :] == cur[:, None] - 1)
        valid = blk[None, :] * SLC_BLOCK <= t[:, None]
        imp_s = jnp.where(forced, jnp.inf, jnp.where(valid, imp_s, -jnp.inf))
        _, idx = lax.top_k(imp_s, n_top)
        ks = ks_blocks[b_ix, g_ix, idx].reshape(B, G, Q_BLOCK, n_top * SLC_BLOCK, dk)
        vs = vs_blocks[b_ix, g_ix, idx].reshape(B, G, Q_BLOCK, n_top * SLC_BLOCK, dv)
        pos_s = (idx[..., None] * SLC_BLOCK + jnp.arange(SLC_BLOCK)).reshape(B, G, Q_BLOCK, n_top * SLC_BLOCK)
        d_s = (t[:, None] - pos_s).astype(jnp.float32)[:, :, None]
        s_s = jnp.einsum('bghqd,bgqkd->bghqk', qb, ks).astype(jnp.float32) * scale - slope * d_s
        p_s = masked_softmax(s_s, (pos_s <= t[:, None])[:, :, None])
        o_s = jnp.einsum('bghqk,bgqkd->bghqd', p_s.astype(vs.dtype), vs)
        kw = lax.dynamic_slice_in_dim(kw_pad, q0, WINDOW + Q_BLOCK, axis=2)
        vw = lax.dynamic_slice_in_dim(vw_pad, q0, WINDOW + Q_BLOCK, axis=2)
        pos_w = q0 - WINDOW + jnp.arange(WINDOW + Q_BLOCK)
        d_w = t[:, None] - pos_w[None, :]
        mask_w = (d_w >= 0) & (d_w < WINDOW) & (pos_w[None, :] >= 0)
        s_w = jnp.einsum('bghqd,bgkd->bghqk', qb, kw).astype(jnp.float32) * scale - slope * d_w.astype(jnp.float32)
        p_w = masked_softmax(s_w, mask_w)
        o_w = jnp.einsum('bghqk,bgkd->bghqd', p_w.astype(vw.dtype), vw)
        return gb[..., 0:1] * o_c + gb[..., 1:2] * o_s + gb[..., 2:3] * o_w

    out = lax.map(block, jnp.arange(nq))
    return out.transpose(1, 0, 4, 2, 3, 5).reshape(B, S, G * HPG * dv)

def mla_attention(q_nope, q_rope, k_nope, k_rope, v):
    B, H, S, _ = q_nope.shape
    dv = v.shape[-1]
    nq = S // Q_BLOCK
    scale = (MLA_NOPE + MLA_ROPE) ** -0.5
    kpos = jnp.arange(S)

    def block(i):
        q0 = i * Q_BLOCK
        qn = lax.dynamic_slice_in_dim(q_nope, q0, Q_BLOCK, axis=2)
        qr = lax.dynamic_slice_in_dim(q_rope, q0, Q_BLOCK, axis=2)
        s = (jnp.einsum('bhqd,bhkd->bhqk', qn, k_nope)
             + jnp.einsum('bhqd,bkd->bhqk', qr, k_rope)).astype(jnp.float32) * scale
        qpos = q0 + jnp.arange(Q_BLOCK)
        p = masked_softmax(s, kpos[None, :] <= qpos[:, None])
        return jnp.einsum('bhqk,bhkd->bhqd', p.astype(v.dtype), v)

    out = lax.map(block, jnp.arange(nq))
    return out.transpose(1, 0, 3, 2, 4).reshape(B, S, H * dv)

def token_mix(u, cos, sin, w_in, cmpk_w1, cmpk_w2, cmpk_pe, cmpv_w1, cmpv_w2, cmpv_pe,
              mla_q_norm, mla_w_uq, mla_kv_norm, mla_w_uk, mla_w_uv,
              w_branch_a, w_branch_b, w_out):
    B, S, _ = u.shape
    points = np.cumsum(IN_SPLITS)[:-1].tolist()
    (q_a, kc, vc, ks, vs, kw, vw, g_nsa, cq, ckv, kr, g_merge) = jnp.split(u @ w_in, points, axis=-1)
    q_a = q_a.reshape(B, S, NSA_GROUPS, NSA_HPG, NSA_DK).transpose(0, 2, 3, 1, 4)
    grp = lambda t: t.reshape(B, S, NSA_GROUPS, -1).transpose(0, 2, 1, 3)
    g_nsa = jax.nn.sigmoid(g_nsa).reshape(B, S, NSA_GROUPS, NSA_HPG, 3).transpose(0, 2, 3, 1, 4)
    k_c = compress(grp(kc), cmpk_w1, cmpk_w2, cmpk_pe)
    v_c = compress(grp(vc), cmpv_w1, cmpv_w2, cmpv_pe)
    o_a = nsa_attention(q_a, k_c, v_c, grp(ks), grp(vs), grp(kw), grp(vw), g_nsa)
    q = (rms_norm(cq) * mla_q_norm) @ mla_w_uq
    q = q.reshape(B, S, MLA_HEADS, MLA_NOPE + MLA_ROPE)
    q_nope = q[..., :MLA_NOPE].transpose(0, 2, 1, 3)
    q_rope = rope(q[..., MLA_NOPE:], cos[:, None, :], sin[:, None, :]).transpose(0, 2, 1, 3)
    ckv = rms_norm(ckv) * mla_kv_norm
    k_nope = (ckv @ mla_w_uk).reshape(B, S, MLA_HEADS, MLA_NOPE).transpose(0, 2, 1, 3)
    v = (ckv @ mla_w_uv).reshape(B, S, MLA_HEADS, MLA_V).transpose(0, 2, 1, 3)
    k_rope = rope(kr, cos, sin)
    o_b = mla_attention(q_nope, q_rope, k_nope, k_rope, v)
    g_a, g_b = jnp.split(g_merge, 2, axis=-1)
    y = jax.nn.sigmoid(g_a) * (o_a @ w_branch_a) + jax.nn.sigmoid(g_b) * (o_b @ w_branch_b)
    return y @ w_out

def first_inputs(seed: int = 0) -> dict:
    key = jax.random.key(seed)
    keys = iter(jax.random.split(key, 40))
    nrm = lambda shape, s: jax.random.normal(next(keys), shape, jnp.float32) * s
    L, D = DEPTH, D_MODEL
    return {
        "x": nrm((BATCH, SEQ, D), 1.0),
        "c": nrm((BATCH, D), 1.0),
        "w_ada": nrm((L, D, N_MOD * D), D ** -0.5),
        "b_ada": nrm((L, N_MOD * D), 0.02),
        "ffn1_gate": nrm((L, D, D_FF), D ** -0.5),
        "ffn1_up": nrm((L, D, D_FF), D ** -0.5),
        "ffn1_down": nrm((L, D_FF, D), D_FF ** -0.5),
        "ffn2_gate": nrm((L, D, D_FF), D ** -0.5),
        "ffn2_up": nrm((L, D, D_FF), D ** -0.5),
        "ffn2_down": nrm((L, D_FF, D), D_FF ** -0.5),
        "w_in": nrm((L, D, IN_TOTAL), D ** -0.5),
        "cmpk_w1": nrm((L, CMP_BLOCK * NSA_DK, NSA_DK), (CMP_BLOCK * NSA_DK) ** -0.5),
        "cmpk_w2": nrm((L, NSA_DK, NSA_DK), NSA_DK ** -0.5),
        "cmpk_pe": nrm((L, CMP_BLOCK, NSA_DK), 0.5),
        "cmpv_w1": nrm((L, CMP_BLOCK * NSA_DV, NSA_DV), (CMP_BLOCK * NSA_DV) ** -0.5),
        "cmpv_w2": nrm((L, NSA_DV, NSA_DV), NSA_DV ** -0.5),
        "cmpv_pe": nrm((L, CMP_BLOCK, NSA_DV), 0.5),
        "mla_q_norm": 1.0 + nrm((L, MLA_Q_RANK), 0.02),
        "mla_w_uq": nrm((L, MLA_Q_RANK, MLA_HEADS * (MLA_NOPE + MLA_ROPE)), MLA_Q_RANK ** -0.5),
        "mla_kv_norm": 1.0 + nrm((L, MLA_KV_RANK), 0.02),
        "mla_w_uk": nrm((L, MLA_KV_RANK, MLA_HEADS * MLA_NOPE), MLA_KV_RANK ** -0.5),
        "mla_w_uv": nrm((L, MLA_KV_RANK, MLA_HEADS * MLA_V), MLA_KV_RANK ** -0.5),
        "w_branch_a": nrm((L, NSA_HEADS * NSA_DV, D), (NSA_HEADS * NSA_DV) ** -0.5),
        "w_branch_b": nrm((L, MLA_HEADS * MLA_V, D), (MLA_HEADS * MLA_V) ** -0.5),
        "w_out": nrm((L, D, D), D ** -0.5),
        "final_norm": 1.0 + nrm((D,), 0.02),
    }

def first_block(x, c, w_ada, b_ada, ffn1_gate, ffn1_up, ffn1_down, ffn2_gate, ffn2_up, ffn2_down,
              w_in, cmpk_w1, cmpk_w2, cmpk_pe, cmpv_w1, cmpv_w2, cmpv_pe,
              mla_q_norm, mla_w_uq, mla_kv_norm, mla_w_uk, mla_w_uv,
              w_branch_a, w_branch_b, w_out, final_norm):
    S = x.shape[1]
    half = MLA_ROPE // 2
    inv_freq = ROPE_THETA ** (-jnp.arange(half, dtype=jnp.float32) / half)
    ang = jnp.arange(S, dtype=jnp.float32)[:, None] * inv_freq[None, :]
    cos, sin = jnp.cos(ang).astype(x.dtype), jnp.sin(ang).astype(x.dtype)
    c_act = jax.nn.silu(c)
    for l in range(DEPTH):
        mod = c_act @ w_ada[l] + b_ada[l]
        sh1, sc1, g1, sh2, sc2, g2, sh3, sc3, g3 = jnp.split(mod, N_MOD, axis=-1)
        x = x + 0.5 * g1[:, None, :] * swiglu(modulate(x, sh1, sc1), ffn1_gate[l], ffn1_up[l], ffn1_down[l])
        x = x + g2[:, None, :] * token_mix(
            modulate(x, sh2, sc2), cos, sin, w_in[l],
            cmpk_w1[l], cmpk_w2[l], cmpk_pe[l], cmpv_w1[l], cmpv_w2[l], cmpv_pe[l],
            mla_q_norm[l], mla_w_uq[l], mla_kv_norm[l], mla_w_uk[l], mla_w_uv[l],
            w_branch_a[l], w_branch_b[l], w_out[l])
        x = x + 0.5 * g3[:, None, :] * swiglu(modulate(x, sh3, sc3), ffn2_gate[l], ffn2_up[l], ffn2_down[l])
    return rms_norm(x) * final_norm


N_MIXERS = 2
N_A_LAYERS = (DEPTH + 1) // 2
N_B_LAYERS = DEPTH // 2
RMS_EPS = 1e-6
LRU_WIDTH = D_MODEL
LRU_HEADS = 4
LRU_BLOCK = LRU_WIDTH // LRU_HEADS
CONV_WIDTH = 4
LRU_C = 8.0
RWKV_HEAD = 64
RWKV_HEADS = D_MODEL // RWKV_HEAD
DECAY_LORA = 64
AAA_LORA = 64
GATE_LORA = 128
RWKV_GN_EPS = 64e-5
MEM_LEN = 256
MEM_HEADS = 4
MEM_HEAD_DIM = D_MODEL // MEM_HEADS
D_FF_2 = 4 * D_MODEL


def rms_norm_2(x, g):
    xf = x.astype(jnp.float32)
    y = xf * lax.rsqrt(jnp.mean(xf * xf, axis=-1, keepdims=True) + RMS_EPS)
    return (y * g.astype(jnp.float32)).astype(x.dtype)

def _lru_combine(c1, c2):
    a1, b1 = c1
    a2, b2 = c2
    return a1 * a2, a2 * b1 + b2

def rglru_mixer(x, conv_w, conv_b, w_in, b_in, gate_w, gate_b, lam, w_out, b_out):
    B, S, _ = x.shape
    proj = x @ w_in + b_in
    y_branch, u = jnp.split(proj, 2, axis=-1)
    y_branch = jax.nn.gelu(y_branch, approximate=True)
    u_pad = jnp.pad(u, ((0, 0), (CONV_WIDTH - 1, 0), (0, 0)))
    conv = conv_b + u_pad[:, 0:S] * conv_w[0]
    for tap in range(1, CONV_WIDTH):
        conv = conv + u_pad[:, tap:tap + S] * conv_w[tap]
    ub = conv.reshape(B, S, LRU_HEADS, LRU_BLOCK)
    gates = jax.nn.sigmoid(jnp.einsum('bshi,ghij->gbshj', ub, gate_w) + gate_b[:, None, None])
    r_gate = gates[0].reshape(B, S, LRU_WIDTH).astype(jnp.float32)
    i_gate = gates[1].reshape(B, S, LRU_WIDTH).astype(jnp.float32)
    log_a = -LRU_C * r_gate * jax.nn.softplus(-lam.astype(jnp.float32))
    a = jnp.exp(log_a)
    mult = jnp.sqrt(-jnp.expm1(2.0 * log_a))
    b = mult * i_gate * conv.astype(jnp.float32)
    _, h = lax.associative_scan(_lru_combine, (a, b), axis=1)
    return (h.astype(x.dtype) * y_branch) @ w_out + b_out

def rwkv7_mixer(x, mu, w_rkv, w0, w1, w2, a0, a1, a2, g1, g2, k_k, k_a, r_k, gn_g, gn_b, w_o):
    B, S, D = x.shape
    H, N = RWKV_HEADS, RWKV_HEAD
    x_prev = jnp.pad(x, ((0, 0), (1, 0), (0, 0)))[:, :S]
    xx = x_prev - x
    r = (x + xx * mu[0]) @ w_rkv[0]
    xw = x + xx * mu[1]
    k = (x + xx * mu[2]) @ w_rkv[1]
    v = (x + xx * mu[3]) @ w_rkv[2]
    xa = x + xx * mu[4]
    xg = x + xx * mu[5]
    w_log = -jax.nn.softplus(-(w0 + jnp.tanh(xw @ w1) @ w2).astype(jnp.float32)) - 0.5
    decay = jnp.exp(-jnp.exp(w_log))
    a = jax.nn.sigmoid(a0 + (xa @ a1) @ a2)
    g = jax.nn.sigmoid(xg @ g1) @ g2
    kk = (k * k_k).reshape(B, S, H, N).astype(jnp.float32)
    kk = kk / jnp.maximum(jnp.linalg.norm(kk, axis=-1, keepdims=True), 1e-12)
    k = k * (1.0 + (a - 1.0) * k_a)

    rh = r.reshape(B, S, H, N).astype(jnp.float32)
    kh = k.reshape(B, S, H, N).astype(jnp.float32)
    vh = v.reshape(B, S, H, N).astype(jnp.float32)
    wh = decay.reshape(B, S, H, N)
    ah = a.reshape(B, S, H, N).astype(jnp.float32)
    rem_a = -kk
    rem_b = kk * ah

    def step(state, inp):
        r_t, w_t, k_t, v_t, a_t, b_t = inp
        sa = jnp.einsum('bhij,bhj->bhi', state, a_t)
        state = (state * w_t[:, :, None, :] + sa[..., None] * b_t[:, :, None, :]
                 + v_t[..., None] * k_t[:, :, None, :])
        y_t = jnp.einsum('bhij,bhj->bhi', state, r_t)
        return state, y_t

    seq_inputs = tuple(jnp.moveaxis(t, 1, 0) for t in (rh, wh, kh, vh, rem_a, rem_b))
    state0 = jnp.zeros((B, H, N, N), jnp.float32)
    _, ys = lax.scan(step, state0, seq_inputs)
    y = jnp.moveaxis(ys, 0, 1)
    mean = jnp.mean(y, axis=-1, keepdims=True)
    var = jnp.mean(jnp.square(y - mean), axis=-1, keepdims=True)
    yn = ((y - mean) * lax.rsqrt(var + RWKV_GN_EPS)).reshape(B, S, D)
    yn = yn * gn_g.astype(jnp.float32) + gn_b.astype(jnp.float32)
    bonus = jnp.sum(rh * kh * r_k.astype(jnp.float32), axis=-1, keepdims=True) * vh
    out = (yn + bonus.reshape(B, S, D)).astype(x.dtype)
    return (out * g) @ w_o

def mem_cross_attention(h, mem_n, w_q, w_kv, w_o):
    B, S, D = h.shape
    M = mem_n.shape[1]
    q = (h @ w_q).reshape(B, S, MEM_HEADS, MEM_HEAD_DIM)
    kv = (mem_n @ w_kv).reshape(B, M, 2, MEM_HEADS, MEM_HEAD_DIM)
    k, v = kv[:, :, 0], kv[:, :, 1]
    s = jnp.einsum('bqhd,bkhd->bhqk', q, k).astype(jnp.float32) * (MEM_HEAD_DIM ** -0.5)
    p = jax.nn.softmax(s, axis=-1).astype(h.dtype)
    o = jnp.einsum('bhqk,bkhd->bqhd', p, v).reshape(B, S, D)
    return o @ w_o

def sqrelu_mlp(h, w_up, w_down):
    return jnp.square(jax.nn.relu(h @ w_up)) @ w_down

def second_inputs(seed: int = 0) -> dict:
    key = jax.random.key(seed)
    ks = iter(jax.random.split(key, 48))
    f32 = jnp.float32

    def nrm(shape, scale):
        return jax.random.normal(next(ks), shape, f32) * scale

    def unif(shape, lo, hi):
        return jax.random.uniform(next(ks), shape, f32, lo, hi)

    D, NA, NB = D_MODEL, N_A_LAYERS, N_B_LAYERS
    x = nrm((BATCH, SEQ, D), 1.0)
    mem = nrm((BATCH, MEM_LEN, D), 1.0)
    ln_gains = 1.0 + nrm((DEPTH, 6, D), 0.05)
    mem_norm = 1.0 + nrm((D,), 0.05)
    a_conv_w = nrm((NA, CONV_WIDTH, LRU_WIDTH), CONV_WIDTH ** -0.5)
    a_conv_b = nrm((NA, LRU_WIDTH), 0.01)
    a_w_in = nrm((NA, D, 2 * LRU_WIDTH), D ** -0.5)
    a_b_in = nrm((NA, 2 * LRU_WIDTH), 0.01)
    a_gate_w = nrm((NA, 2, LRU_HEADS, LRU_BLOCK, LRU_BLOCK), LRU_BLOCK ** -0.5)
    a_gate_b = nrm((NA, 2, LRU_HEADS, LRU_BLOCK), 0.01)
    u = unif((NA, LRU_WIDTH), 0.81, 0.998)
    sp = -0.5 * jnp.log(u)
    a_lambda = -jnp.log(jnp.expm1(sp))
    a_w_out = nrm((NA, LRU_WIDTH, D), LRU_WIDTH ** -0.5)
    a_b_out = nrm((NA, D), 0.01)
    b_mu = unif((NB, 6, D), 0.0, 1.0)
    b_w_rkv = nrm((NB, 3, D, D), D ** -0.5)
    b_w0 = unif((NB, D), -6.0, -1.0)
    b_w1 = nrm((NB, D, DECAY_LORA), D ** -0.5)
    b_w2 = nrm((NB, DECAY_LORA, D), 0.1 * DECAY_LORA ** -0.5)
    b_a0 = nrm((NB, D), 0.1)
    b_a1 = nrm((NB, D, AAA_LORA), D ** -0.5)
    b_a2 = nrm((NB, AAA_LORA, D), 0.1 * AAA_LORA ** -0.5)
    b_g1 = nrm((NB, D, GATE_LORA), D ** -0.5)
    b_g2 = nrm((NB, GATE_LORA, D), GATE_LORA ** -0.5)
    b_k_k = 0.85 + nrm((NB, D), 0.05)
    b_k_a = 1.0 + nrm((NB, D), 0.05)
    b_r_k = nrm((NB, RWKV_HEADS, RWKV_HEAD), 0.1)
    b_gn_g = 1.0 + nrm((NB, D), 0.05)
    b_gn_b = nrm((NB, D), 0.01)
    b_w_o = nrm((NB, D, D), D ** -0.5)
    c_w_q = nrm((DEPTH, D, D), D ** -0.5)
    c_w_kv = nrm((DEPTH, D, 2 * D), D ** -0.5)
    c_w_o = nrm((DEPTH, D, D), D ** -0.5)
    m_w_up = nrm((DEPTH, D, D_FF_2), D ** -0.5)
    m_w_down = nrm((DEPTH, D_FF_2, D), D_FF_2 ** -0.5)
    return {"x": x, "mem": mem, "ln_gains": ln_gains, "mem_norm": mem_norm,
            "a_conv_w": a_conv_w, "a_conv_b": a_conv_b, "a_w_in": a_w_in, "a_b_in": a_b_in,
            "a_gate_w": a_gate_w, "a_gate_b": a_gate_b, "a_lambda": a_lambda,
            "a_w_out": a_w_out, "a_b_out": a_b_out,
            "b_mu": b_mu, "b_w_rkv": b_w_rkv, "b_w0": b_w0, "b_w1": b_w1, "b_w2": b_w2,
            "b_a0": b_a0, "b_a1": b_a1, "b_a2": b_a2, "b_g1": b_g1, "b_g2": b_g2,
            "b_k_k": b_k_k, "b_k_a": b_k_a, "b_r_k": b_r_k, "b_gn_g": b_gn_g, "b_gn_b": b_gn_b,
            "b_w_o": b_w_o,
            "c_w_q": c_w_q, "c_w_kv": c_w_kv, "c_w_o": c_w_o,
            "m_w_up": m_w_up, "m_w_down": m_w_down}

def second_block(x, mem, ln_gains, mem_norm,
              a_conv_w, a_conv_b, a_w_in, a_b_in, a_gate_w, a_gate_b, a_lambda, a_w_out, a_b_out,
              b_mu, b_w_rkv, b_w0, b_w1, b_w2, b_a0, b_a1, b_a2, b_g1, b_g2,
              b_k_k, b_k_a, b_r_k, b_gn_g, b_gn_b, b_w_o,
              c_w_q, c_w_kv, c_w_o, m_w_up, m_w_down):
    mem_n = rms_norm_2(mem, mem_norm)
    for i in range(DEPTH):
        g = ln_gains[i]
        j = i // N_MIXERS
        hn = rms_norm_2(x, g[0])
        if i % N_MIXERS == 0:
            t = rglru_mixer(hn, a_conv_w[j], a_conv_b[j], a_w_in[j], a_b_in[j], a_gate_w[j],
                            a_gate_b[j], a_lambda[j], a_w_out[j], a_b_out[j])
        else:
            t = rwkv7_mixer(hn, b_mu[j], b_w_rkv[j], b_w0[j], b_w1[j], b_w2[j], b_a0[j],
                            b_a1[j], b_a2[j], b_g1[j], b_g2[j], b_k_k[j], b_k_a[j], b_r_k[j],
                            b_gn_g[j], b_gn_b[j], b_w_o[j])
        x = x + rms_norm_2(t, g[1])
        c = mem_cross_attention(rms_norm_2(x, g[2]), mem_n, c_w_q[i], c_w_kv[i], c_w_o[i])
        x = x + rms_norm_2(c, g[3])
        m = sqrelu_mlp(rms_norm_2(x, g[4]), m_w_up[i], m_w_down[i])
        x = x + rms_norm_2(m, g[5])
    return x


def setup_inputs(seed=0):
    out = dict(first_inputs(seed))
    for name, value in second_inputs(seed + 1).items():
        if name != "x":
            out[name + "_2"] = value
    return out


def reference(
    x, c, w_ada, b_ada, ffn1_gate, ffn1_up, ffn1_down, ffn2_gate, ffn2_up, ffn2_down, w_in,
    cmpk_w1, cmpk_w2, cmpk_pe, cmpv_w1, cmpv_w2, cmpv_pe, mla_q_norm, mla_w_uq, mla_kv_norm,
    mla_w_uk, mla_w_uv, w_branch_a, w_branch_b, w_out, final_norm, mem_2, ln_gains_2,
    mem_norm_2, a_conv_w_2, a_conv_b_2, a_w_in_2, a_b_in_2, a_gate_w_2, a_gate_b_2, a_lambda_2,
    a_w_out_2, a_b_out_2, b_mu_2, b_w_rkv_2, b_w0_2, b_w1_2, b_w2_2, b_a0_2, b_a1_2, b_a2_2,
    b_g1_2, b_g2_2, b_k_k_2, b_k_a_2, b_r_k_2, b_gn_g_2, b_gn_b_2, b_w_o_2, c_w_q_2, c_w_kv_2,
    c_w_o_2, m_w_up_2, m_w_down_2,
):
    x = first_block(
        x, c, w_ada, b_ada, ffn1_gate, ffn1_up, ffn1_down, ffn2_gate, ffn2_up, ffn2_down, w_in,
        cmpk_w1, cmpk_w2, cmpk_pe, cmpv_w1, cmpv_w2, cmpv_pe, mla_q_norm, mla_w_uq, mla_kv_norm,
        mla_w_uk, mla_w_uv, w_branch_a, w_branch_b, w_out, final_norm,
    )
    return second_block(
        x, mem_2, ln_gains_2, mem_norm_2, a_conv_w_2, a_conv_b_2, a_w_in_2, a_b_in_2,
        a_gate_w_2, a_gate_b_2, a_lambda_2, a_w_out_2, a_b_out_2, b_mu_2, b_w_rkv_2, b_w0_2,
        b_w1_2, b_w2_2, b_a0_2, b_a1_2, b_a2_2, b_g1_2, b_g2_2, b_k_k_2, b_k_a_2, b_r_k_2,
        b_gn_g_2, b_gn_b_2, b_w_o_2, c_w_q_2, c_w_kv_2, c_w_o_2, m_w_up_2, m_w_down_2,
    )


_drawn_inputs = setup_inputs


def setup_inputs(seed=0):
    import zlib

    import numpy as np

    out = dict(_drawn_inputs(seed))
    spreads = {}
    factors = {'cmpk_pe': 3.374,
     'mla_q_norm': 8.0,
     'mla_kv_norm': 5.332,
     'a_conv_b_2': 2.81,
     'a_gate_b_2': 8.0,
     'b_w1_2': 8.0,
     'b_w2_2': 8.0,
     'b_a0_2': 2.907,
     'b_a1_2': 2.999,
     'b_a2_2': 3.08,
     'b_gn_b_2': 33.685,
     'a_b_in_2': 3.126,
     'b_gn_g_2': 2.667}
    for name, (base, spread) in spreads.items():
        noise = np.random.default_rng([zlib.crc32(name.encode()), seed]).standard_normal(out[name].shape)
        drawn = base * np.exp(spread * noise) if base else spread * noise
        out[name] = __import__('jax').numpy.asarray(drawn.astype(out[name].dtype))
    for name, factor in factors.items():
        out[name] = (out[name] * factor).astype(out[name].dtype)
    return out
```

```python
import numpy as np
import concourse.bass as bass
from concourse import mybir
from contextlib import ExitStack

F32 = mybir.dt.float32
ALU = mybir.AluOpType
ACT = mybir.ActivationFunctionType
AX = mybir.AxisListType

P = 128
D = 1024
S = 256
KD = D // P
QT = S // P
DEPTH = 2
DFF = 2816
KF = DFF // P
NMOD = 9
HEADS = 8
GROUPS = 2
HPG = HEADS // GROUPS
DK = 64
CMP_BLOCK, CMP_STRIDE = 32, 16
NCMP = S // CMP_STRIDE - CMP_BLOCK // CMP_STRIDE + 1
NOPE, ROPE = 64, 32
QH = NOPE + ROPE
QRANK, KVRANK = 384, 256
KQ, KKV = QRANK // P, KVRANK // P
MERGE = 2 * KD
EPS = 1e-6
MASKED = -1e30
MAX_CLAMP = 1e29
TOKW = 2 * 128 + 3 * HEADS + ROPE
LRU_HEADS, LRU_BLOCK = 4, 256
CONV = 4
RH, RN = 16, 64
CH = 64
NCH = S // CH
LEVELS = 6
MH = 4
FF2 = 4 * D
KF2 = FF2 // P
GN_EPS = 64e-5
E_HALF = float(np.exp(-0.5))

HEAP = 112 * 256
TILES = 8
CW = TILES * P
RING = 12


def constant_columns():
    t = np.arange(S)
    c = {}
    c["ident"] = np.eye(P)
    c["ones"] = np.ones((P, P))
    rot = np.zeros((P, ROPE))
    half = ROPE // 2
    for i in range(half):
        rot[NOPE + half + i, i] = -1.0
        rot[NOPE + i, half + i] = 1.0
    c["rot"] = rot
    inv = np.float32(10000.0) ** (-np.arange(half, dtype=np.float32) / np.float32(half))
    ang = np.arange(S, dtype=np.float32)[None, :] * inv[:, None].astype(np.float32)
    cs = np.zeros((P, S)); sn = np.zeros((P, S))
    cs[NOPE:QH] = np.concatenate([np.cos(ang), np.cos(ang)])
    sn[NOPE:QH] = np.concatenate([np.sin(ang), np.sin(ang)])
    c["cos"], c["sin"] = cs, sn
    slope = 2.0 ** (-8.0 * np.arange(1, HEADS + 1) / HEADS)
    for q in range(QT):
        tq = t[q * P:(q + 1) * P]
        keys = t[:(q + 1) * P]
        dist = (tq[:, None] - keys[None, :]).astype(np.float64)
        mask = np.where(dist >= 0, 0.0, MASKED)
        c[f"causal{q}"] = mask
        c[f"alibi{q}"] = np.stack([-s * dist + mask for s in slope], 1).reshape(P, -1)
        end = np.arange(NCMP) * CMP_STRIDE + CMP_BLOCK - 1
        dc = (tq[:, None] - end[None, :]).astype(np.float64)
        cm = np.where(dc >= 0, 0.0, MASKED)
        c[f"cmp{q}"] = np.stack([-s * dc + cm for s in slope], 1).reshape(P, -1)
    a, b = np.arange(CH)[:, None], np.arange(CH)[None, :]
    m = np.zeros((P, 4, CH))
    m[:CH] = np.stack([a < b, a <= b, a < b, a <= b], 1)
    c["earlier"] = m.reshape(P, -1)
    m = np.zeros((P, LEVELS, CH))
    for n in range(LEVELS):
        m[:CH, n] = (a >> n + 1 == b >> n + 1) & (a >> n & 1 == 0) & (b >> n & 1 == 1)
    c["levels"] = m.reshape(P, -1)
    c["within"] = np.tile((t % CH != 0).astype(float), (P, 1))
    c["head_of"] = np.kron(np.eye(2), np.ones((RN, 1)))
    return {k: v.astype(np.float32) for k, v in c.items()}


def packed(parts):
    at, n = {}, 0
    for k, w in parts:
        at[k] = (n, n + w)
        n += w
    return at, n


CONSTS = constant_columns()
CONST_AT, CONST_W = packed([(k, v.shape[1]) for k, v in CONSTS.items()])

VEC_COLS = [("b_ada", DEPTH * NMOD * KD), ("c", KD), ("final_norm", KD),
            ("mla_q_norm", DEPTH * KQ), ("mla_kv_norm", DEPTH * KKV), ("pe", DEPTH * 2 * CMP_BLOCK),
            ("ln", DEPTH * 6 * KD), ("mem_norm", KD), ("conv_w", CONV * KD), ("conv_b", KD),
            ("b_in", 2 * KD), ("gate_b", 2 * KD), ("lam", KD), ("b_out", KD), ("mu", 6 * KD),
            ("w0", KD), ("a0", KD), ("k_k", KD), ("k_a", KD), ("r_k", KD), ("gn_g", KD), ("gn_b", KD)]
VEC_AT, VEC_W = packed(VEC_COLS)


def bcast(x, n):
    return x.unsqueeze(len(x.shape)).broadcast_to((*x.shape, n))


def bcast_mid(x, n):
    return x.unsqueeze(1).broadcast_to((x.shape[0], n, x.shape[1]))


FILLED = ("square_sums", "rstd", "head_sums", "head_spread", "chunk_used")


class Ledger:

    def __init__(self, nc, ctx, seen):
        self.nc, self.ctx, self.seen = nc, ctx, seen
        self.counts, self.events, self.sems = {}, {}, {}

    def sem(self, name):
        if name not in self.sems:
            self.sems[name] = self.ctx.enter_context(self.nc.semaphore(name))
        return self.sems[name]

    def did(self, name, key, also=(), by=1):
        kind = "bank_filled" if name.endswith("_raw") or name in FILLED else name
        self.counts[kind] = self.counts.get(kind, 0) + by
        for event in ((name, key), *also):
            assert event not in self.events, event
            self.events[event] = (kind, self.counts[kind])
        return self.sem(kind), by

    def of(self, name, key):
        if self.seen is None:
            return self.sem("first_writing"), 1
        sem, count = self.seen[(name, key)]
        return self.sem(sem), count


def program(nc, dram, out, seen, stream):
    ctx = ExitStack()
    with ctx:
        led = Ledger(nc, ctx, seen)
        did, of = led.did, led.of
        order = []

        def sb(name, shape):
            return ctx.enter_context(nc.sbuf_tensor(name, shape, F32))

        ring = sb("weight_ring", [P, RING, CW])
        X = sb("x_t", [P, KD, S])
        xn = sb("xn_t", [P, KD, S])
        consts = sb("consts", [P, CONST_W])
        vecs = sb("vecs", [P, VEC_W])
        mod = sb("mod", [P, DEPTH * NMOD * KD])
        c_act = sb("c_act", [P, KD])
        silu = sb("silu", [P, 2, S])
        root = sb("root", [P, 4, 4])
        diag = sb("diag", [P, 4, P])
        nmax = sb("nmax", [P, 2, HPG])
        den = sb("den", [P, 2, HPG])
        stat = sb("stat", [P, 4, QT * RH])
        w_end = sb("w_end", [P, KD, NCH])
        lam = sb("lam", [P, 4, KD])
        w2 = sb("w2", [DK, DEPTH * 2, DK])
        heap = sb("heap", [P, HEAP])
        free = [0]

        def take(n):
            free[0] += n
            assert free[0] <= HEAP, free
            return heap[:, free[0] - n:free[0]]

        def tall(n=KD, w=S):
            return take(n * w).rearrange("p (k t) -> p k t", t=w)

        arena = take(32 * S)
        work = take(16 * S)
        scores = take(2 * HPG * S).rearrange("p (a b t) -> p a b t", a=2, b=HPG)
        q_t = tall(HPG)
        kv_t = tall(4)
        vsw = tall(QT, 2 * P)
        gates = tall(QT, 3 * HEADS)
        latent_n = tall(KQ + KKV)
        v_mla = tall(QT, HEADS * DK)
        oa_t = tall(HPG)
        ob_t = tall(HPG)
        cmp_h = take(GROUPS * 2 * CMP_STRIDE)[0:DK, :].rearrange("p (g v n) -> p g v n", g=GROUPS, v=2)
        kcc = take(CMP_STRIDE)
        vcc = take(P)[0:CMP_STRIDE, :]
        rope_tmp = take(2 * S)
        rope_k = take(S)
        bank = ctx.enter_context(nc.psum_tensor("banks", [P, 8, 512], F32))

        hid = arena.rearrange("p (k t) -> p k t", t=S)
        gm = hid[:, 0:MERGE, :]
        qh = hid[:, MERGE:MERGE + HEADS, :]
        kh = hid[:, MERGE + HEADS:MERGE + 2 * HEADS, :]
        wk = work.rearrange("p (k t) -> p k t", t=S)
        sq = wk[:, 0:KD, :]
        blocks_pe = work[:, KD * S:KD * S + 2 * CMP_BLOCK * NCMP].rearrange(
            "p (v i n) -> p v i n", v=2, i=CMP_BLOCK)
        prob_t = work.rearrange("p (u j k q) -> p u j k q", u=4, j=HPG, k=QT)
        latent = scores[:, :, :, :].rearrange("p a b t -> p (a b) t")[:, 0:KQ + KKV, :]

        free[0] = 0
        slot = [tall() for _ in range(HEAP // (KD * S))]

        def slots(a, n, off=0):
            return heap[:, a * KD * S + off:a * KD * S + off + n]

        mem_n = slot[0]
        t_out, t_sq = slot[11], slot[12]
        UW = S + CONV - 1
        y_br = slot[1]
        u_pad = slots(2, KD * UW).rearrange("p (k t) -> p k t", t=UW)
        conv, rg, ig, decay, th, lru_b, lru_h = slot[4:11]
        q2, o2, k2, v2 = slot[1], slot[4], slot[13], slot[5]
        v2 = slots(5, KD * S).rearrange("p (k c) -> p k c", k=QT)
        sc2 = slots(2, KD * S).rearrange("p (u h k) -> p u h k", u=QT, h=MH)
        pt2 = slots(3, KD * S).rearrange("p (u h k q) -> p u h k q", u=QT, h=MH, k=QT)
        hid2 = slots(1, KF2 * S).rearrange("p (k t) -> p k t", t=S)
        ar = slots(1, 2 * KD * S).rearrange("p (k m t) -> p k m t", k=KD, m=2)
        bt, kt_, v_t, g_t, bonus = slot[3:8]
        mats = slots(8, RH * 4 * CH)[0:CH, :].rearrange("p (h w) -> p h w", h=RH)
        inv = slots(10, 4 * RH * CH)[0:CH, :].rearrange("p (m h t) -> p m h t", m=4, h=RH)
        xi, xit, yi, mi = (inv[:, m] for m in range(4))
        tm = slots(12, 3 * D)[0:CH, :].rearrange("p (m c) -> p m c", m=3)
        state = slots(12, KD * RN, 3 * D).rearrange("p (k i) -> p k i", k=KD)
        r_t, k_t, kk_t, aa_t, sg_t = slot[8], slot[9], slot[10], slot[11], slot[12]
        xs_t = [slot[3], slot[4]]
        wide = {n: slots(i, QT * RH * RN) for n, i in (("kk", 7), ("bonus", 4), ("mean", 4), ("var", 5))}

        def const(name, rows=P):
            a, b = CONST_AT[name]
            return consts[0:rows, a:b]

        def vec(name, i=0, n=1):
            a = VEC_AT[name][0]
            return vecs[:, a + i:a + i + n]

        def mods(l, seg, k, n=1):
            a = (l * NMOD + seg) * KD + k
            return mod[:, a:a + n]

        def cols(b, w=S, at=0):
            return bank[:, b, at:at + w]

        ident, ones = const("ident"), const("ones")

        UNITS, PV = [], []
        for q in range(QT):
            for g in range(GROUPS):
                PV.append(("a", g, q, [len(UNITS) + i for i in range(3)]))
                UNITS += [("cmp", g, q), ("slc", g, q), ("win", g, q)]
        for q in range(QT):
            for g in range(GROUPS):
                PV.append(("b", g, q, [len(UNITS)]))
                UNITS.append(("mla", g, q))
        NU = len(UNITS)
        PV_OF = {u: i for i, pv in enumerate(PV) for u in pv[3]}

        def width(kind, q):
            return NCMP if kind == "cmp" else (q + 1) * P

        ADA = [(0, i) for i in range(NMOD * KD)] + [(1, i) for i in range(NMOD * KD)]
        ADA_PARTS = [(0, 2 * KD, 6), (2 * KD, NMOD * KD, 7), (NMOD * KD, 2 * NMOD * KD, 6)]

        held = {}

        block = ctx.enter_context(nc.Block())

        @block.sync
        def _(sp):
            sp.dma_start(vecs[:, :], dram["vecs"]).then_inc(*did("vecs_in", 0, by=16))
            for n, (name, i, w) in enumerate(stream):
                if n >= RING:
                    sp.wait_ge(*of("weights_used", n - RING))
                sp.dma_start(ring[:, n % RING, 0:w], dram[name][i][:, 0:w]).then_inc(
                    led.sem(f"weights_in_{n % RING}"), 16)
            sp.wait_ge(*of("x_final", ((DEPTH - 1, 5), KD - 1)))
            sp.dma_start(out, X[:, :, :]).then_inc(*did("out_stored", 0, by=16))
            sp.wait_ge(*of("out_stored", 0))

        @block.tensor
        def _(pe):
            readers = {}

            def refill(*banks):
                for b in banks:
                    for event in readers.pop(b, ()):
                        pe.wait_ge(*of(*event))

            def arrived(name, i, w=CW):
                n = len(order)
                order.append((name, i, w))
                pe.wait_ge(led.sem(f"weights_in_{n % RING}"), 16 * (n // RING + 1))
                return ring[:, n % RING, 0:w], ("weights_used", n)

            def mm(o, w, r, first, last):
                return nc.tensor.matmul(o, w, r, start=first, stop=last)

            ring_at = [0]

            def next_bank(n=4):
                ring_at[0] += 1
                b = (ring_at[0] - 1) % n
                refill(b)
                return b

            def ada(i0, i1):
                for i in range(i0, i1):
                    for part, (a, b, bk) in enumerate(ADA_PARTS):
                        if a <= i < b:
                            break
                    if i == a:
                        refill(bk)
                    if i == 0:
                        pe.wait_ge(*of("c_act", 0))
                    w, used = arrived("w_ada", i)
                    for k in range(KD):
                        mn = mm(bank[:, bk, i - a:i - a + 1], w[:, k * P:(k + 1) * P],
                                c_act[:, k:k + 1], k == 0, k == KD - 1)
                    mn.then_inc(*did("ada_raw", i, also=[used]))
                    if i == b - 1:
                        readers[bk] = [("mod_sum", part)]

            def squares_sum(n, k, kn, tts=range(QT)):
                if k == 0:
                    refill(4, 5)
                pe.wait_ge(*of("squares", (n, k)))
                src = sq if isinstance(n, int) else t_sq
                for t in tts:
                    mn = mm(bank[:, 4 + t, 0:1], src[:, k, t * P:(t + 1) * P], ones[:, 0:1],
                            k == 0, k == kn - 1)
                if k == kn - 1:
                    mn.then_inc(*did("square_sums", n))
                    readers[4] = readers[5] = [("mean_square", n)]

            def spread(n):
                refill(4)
                pe.wait_ge(*of("rstd_diag", n))
                for t in range(QT):
                    mn = mm(cols(4, P, t * P), ones, diag[:, t, :], True, True)
                mn.then_inc(*did("rstd", n))
                readers[4] = [("rstd_read", n)]

            def project(name, i, x, ready, done, readers_of, kn=KD, b=None):
                w, used = arrived(name, i)
                b = next_bank() if b is None else b
                for k in range(kn):
                    if ready is not None:
                        pe.wait_ge(*of(ready[0], (*ready[1:], k)))
                    mn = mm(cols(b), w[:, k * P:(k + 1) * P], x[:, k, :], k == 0, k == kn - 1)
                mn.then_inc(*did(*done, also=[used]))
                readers[b] = readers_of
                held[done] = b
                return b

            def down(name, i0, x, kt, hidden, s, norm, reader="residual"):
                wc = None
                for f in range(KD):
                    b = next_bank()
                    for k in range(kt):
                        m = f * kt + k
                        if m % TILES == 0:
                            wc, used = arrived(name, i0 + m // TILES)
                        if f == 0 and hidden is not None:
                            pe.wait_ge(*of(hidden, (s, k)))
                        j = m % TILES
                        mn = mm(cols(b), wc[:, j * P:(j + 1) * P], x[:, k, :], k == 0, k == kt - 1)
                        ends = [used] if m % TILES == TILES - 1 else []
                        if k == kt - 1:
                            mn.then_inc(*did("down_raw", (s, f), also=ends))
                        elif ends:
                            mn.then_inc(*did("chunk_used", (s, m), also=ends))
                    readers[b] = [(reader, (s, f))]
                    held["down_raw", (s, f)] = b
                    if norm is not None and f > 0:
                        squares_sum(norm, f - 1, KD)
                if norm is not None:
                    squares_sum(norm, KD - 1, KD)

            def ffn(s, l, which, norm, next_norm, ada_part):
                spread(norm)
                for f in range(KF):
                    first = ("normed", norm) if f == 0 else None
                    b = project(which + "_gate", l * KF + f, xn, first, ("gate_raw", (s, f)),
                                [("silu", (s, f))])
                    project(which + "_up", l * KF + f, xn, None, ("up_raw", (s, f)),
                            [("hidden", (s, f))])
                    if ada_part is not None:
                        a, b1 = ADA_PARTS[ada_part][0:2]
                        per = -(-(b1 - a) // KF)
                        ada(min(a + per * f, b1), min(a + per * f + per, b1))
                down(which + "_down", l * KF, hid, KF, "hidden", s, next_norm)

            def mix(l, s, norm, next_norm):
                spread(norm)
                done = "in_raw"
                for i in range(KQ + KKV):
                    project("w_in", l * 29 + i, xn, ("normed", norm) if i == 0 else None,
                            (done, (l, i)), [("latent", (l, i)), ("squares", (("m", l), i))])
                for i in range(4):
                    project("w_in", l * 29 + 5 + i, xn, None, (done, (l, 5 + i)),
                            [("kv" if i < 2 else "kv_attn", (l, i))])
                refill(4, 5)
                for t in range(QT):
                    for c, (a, b) in enumerate(((0, KQ), (KQ, KQ + KKV))):
                        for i in range(a, b):
                            pe.wait_ge(*of("squares", (("m", l), i)))
                            mn = mm(bank[:, 4 + t, c:c + 1], sq[:, i, t * P:(t + 1) * P],
                                    ones[:, 0:1], i == a, i == b - 1)
                mn.then_inc(*did("square_sums", ("m", l)))
                readers[4] = readers[5] = [("mean_square", ("m", l))]
                for i in range(4):
                    project("w_in", l * 29 + 9 + i, xn, None, (done, (l, 9 + i)), [("q", (l, i))])
                refill(4)
                pe.wait_ge(*of("rstd_diag", ("m", l)))
                for c in range(4):
                    mn = mm(cols(4, P, c * P), ones, diag[:, c, :], True, True)
                mn.then_inc(*did("rstd", ("m", l)))
                readers[4] = [("rstd_read", ("m", l))]
                b0, b1, b2 = next_bank(), next_bank(), next_bank()
                at = 0
                for c, n in enumerate((3, 3, 2)):
                    w, used = arrived("w_tok", l * 3 + c, n * TOKW)
                    for k in range(at, at + n):
                        wk_ = w[:, (k - at) * TOKW:(k - at + 1) * TOKW]
                        for t, b in ((0, b0), (1, b1)):
                            mm(cols(b, TOKW - ROPE), xn[:, k, t * P:(t + 1) * P],
                               wk_[:, 0:TOKW - ROPE], k == 0, k == KD - 1)
                        mn = mm(bank[NOPE:QH, b2, 0:S], wk_[:, TOKW - ROPE:TOKW], xn[:, k, :],
                                k == 0, k == KD - 1)
                    at += n
                    mn.then_inc(*did("tok_raw", (l, c), also=[used]))
                readers[b0] = [("vsw", (l, 0)), ("gate_exp", (l, 0))]
                readers[b1] = [("vsw", (l, 1)), ("gate_exp", (l, 1))]
                readers[b2] = [("rope_key", l)]
                held["tok_raw", (l, 0)], held["tok_raw", (l, 1)], held["tok_raw", (l, 2)] = b0, b1, b2
                refill(6, 7)
                if l == 0:
                    pe.wait_ge(*of("w2_in", 0))
                for v in range(2):
                    pe.wait_ge(*of("blocks_pe", (l, v)))
                    for c in range(2):
                        w, used = arrived("cmp_w1", (l * 2 + v) * 2 + c)
                        for g in range(GROUPS):
                            r = slice(DK * g, DK * g + DK)
                            for i in range(CMP_STRIDE):
                                mn = mm(bank[0:DK, 6 + g, v * CMP_STRIDE:v * CMP_STRIDE + NCMP],
                                        w[r, i * DK:(i + 1) * DK],
                                        blocks_pe[r, v, c * CMP_STRIDE + i, :],
                                        c == 0 and i == 0, c == 1 and i == CMP_STRIDE - 1)
                        mn.then_inc(*did("cmp_raw", (l, v, c), also=[used]))
                readers[6] = [("cmp_hidden", (l, 0))]
                readers[7] = [("cmp_hidden", (l, 1))]
                for k in range(KKV):
                    pe.wait_ge(*of("latent_n", (l, KQ + k)))
                w, used = arrived("w_uk", l)
                for p2 in range(HEADS // 2):
                    b = next_bank()
                    for e in range(2):
                        h = 2 * p2 + e
                        for k in range(KKV):
                            mn = mm(bank[0:DK, b, e * S:(e + 1) * S],
                                    w[:, k * 512 + h * DK:k * 512 + (h + 1) * DK],
                                    latent_n[:, KQ + k, :], k == 0, k == KKV - 1)
                    mn.then_inc(*did("uk_raw", (l, p2), also=[used] if p2 == 3 else []))
                    readers[b] = [("k_nope", (l, p2))]
                    held["uk_raw", (l, p2)] = b
                w, used = arrived("w_uv", l)
                for t in range(QT):
                    b = next_bank()
                    for k in range(KKV):
                        mn = mm(cols(b, 512), latent_n[:, KQ + k, t * P:(t + 1) * P],
                                w[:, k * 512:(k + 1) * 512], k == 0, k == KKV - 1)
                    mn.then_inc(*did("uv_raw", (l, t), also=[used] if t == 1 else []))
                    readers[b] = [("v_mla", (l, t))]
                    held["uv_raw", (l, t)] = b
                refill(5)
                for g in range(GROUPS):
                    pe.wait_ge(*of("cmp_hidden", (l, g)))
                    mm(bank[DK * g:DK * g + DK, 5, 0:NCMP], w2[:, l * 2, :], cmp_h[:, g, 0, 0:NCMP],
                       True, True)
                for g in range(GROUPS):
                    mn = mm(bank[0:NCMP, 5, (1 + g) * DK:(2 + g) * DK], cmp_h[:, g, 1, 0:NCMP],
                            w2[:, l * 2 + 1, :], True, True)
                mn.then_inc(*did("cmp_out_raw", l))
                readers[5] = [("kcc", l), ("vcc", l)]
                for k in range(KQ):
                    pe.wait_ge(*of("latent_n", (l, k)))
                m = 0
                for p2 in range(HEADS // 2):
                    b = next_bank()
                    for e in range(2):
                        for k in range(KQ):
                            if m % TILES == 0:
                                w, used = arrived("w_uq", l * 3 + m // TILES, TILES * QH)
                            j = m % TILES
                            mn = mm(bank[0:QH, b, e * S:(e + 1) * S], w[:, j * QH:(j + 1) * QH],
                                    latent_n[:, k, :], k == 0, k == KQ - 1)
                            m += 1
                            ends = [used] if m % TILES == 0 else []
                            if e == 1 and k == KQ - 1:
                                mn.then_inc(*did("uq_raw", (l, p2), also=ends))
                            elif ends:
                                mn.then_inc(*did("chunk_used", (l, "uq", m), also=ends))
                    readers[b] = [("q_mla_scaled", (l, p2))]
                    held["uq_raw", (l, p2)] = b
                rr = slice(NOPE, QH)
                b = next_bank()
                pe.wait_ge(*of("rope_key", l))
                mm(bank[rr, b, 0:S], const("rot")[rr, :], rope_k[rr, :], True, True).then_inc(
                    *did("rot_raw", (l, -1)))
                readers[b] = [("rot_sin", (l, -1))]
                held["rot_raw", (l, -1)] = b
                for p2 in range(HEADS // 2):
                    b = next_bank()
                    pe.wait_ge(*of("q_mla_scaled", (l, p2)))
                    mm(bank[rr, b, :], const("rot")[rr, :], qh[rr, 2 * p2:2 * p2 + 2, :],
                       True, True).then_inc(*did("rot_raw", (l, p2)))
                    readers[b] = [("rot_sin", (l, p2))]
                    held["rot_raw", (l, p2)] = b

                def unit_scores(u):
                    kind, g, q = UNITS[u]
                    w = width(kind, q)
                    refill(2 * (u % 2), 2 * (u % 2) + 1)
                    if u == 0:
                        pe.wait_ge(*of("kcc", l))
                        for i in range(HPG):
                            pe.wait_ge(*of("q", (l, i)))
                        for i in range(2, 4):
                            pe.wait_ge(*of("kv_attn", (l, i)))
                    if kind == "mla":
                        pe.wait_ge(*of("k_mla", l))
                        for p2 in (2 * g, 2 * g + 1):
                            pe.wait_ge(*of("q_mla", (l, p2)))
                            pe.wait_ge(*of("k_nope", (l, p2)))
                    r = slice(DK * g, DK * g + DK)
                    for j in range(HPG):
                        o = bank[:, 2 * (u % 2) + j // 2, (j % 2) * S:(j % 2) * S + w]
                        qs = slice(q * P, (q + 1) * P)
                        if kind == "mla":
                            h = g * HPG + j
                            mn = mm(o, qh[0:QH, h, qs], kh[0:QH, h, 0:w], True, True)
                        elif kind == "cmp":
                            mn = mm(o, q_t[r, j, qs], kcc[r, 0:w], True, True)
                        else:
                            mn = mm(o, q_t[r, j, qs], kv_t[r, 2 if kind == "slc" else 3, 0:w],
                                    True, True)
                    mn.then_inc(*did("scores_raw", (l, u)))
                    readers[2 * (u % 2)] = readers[2 * (u % 2) + 1] = [("biased", (l, u))]

                def unit_transpose(u):
                    kind, g, q = UNITS[u]
                    w = width(kind, q)
                    refill(4, 5)
                    pe.wait_ge(*of("probs", (l, u)))
                    for j in range(HPG):
                        for k in range(-(-w // P)):
                            n = min(P, w - k * P)
                            c = (j % 2) * S + k * P
                            mn = nc.tensor.transpose(bank[0:n, 4 + j // 2, c:c + P],
                                                     scores[:, u % 2, j, k * P:k * P + n], ident)
                    mn.then_inc(*did("prob_t_raw", (l, u)))
                    readers[4] = [("prob_t_a", (l, u))]
                    readers[5] = [("prob_t_b", (l, u))]

                def unit_values(i):
                    kind, g, q, us = PV[i]
                    b = 6 + i % 2
                    refill(b)
                    if i == 0:
                        pe.wait_ge(*of("vcc", l))
                        for t in range(QT):
                            pe.wait_ge(*of("vsw", (l, t)))
                    for u in us:
                        pe.wait_ge(*of("prob_t_a", (l, u)))
                        pe.wait_ge(*of("prob_t_b", (l, u)))
                    for j in range(HPG):
                        parts = []
                        for u in us:
                            for k in range(q + 1 if UNITS[u][0] != "cmp" else 1):
                                v = {"cmp": vcc[0:NCMP, g * DK:(g + 1) * DK],
                                     "slc": vsw[:, k, g * DK:(g + 1) * DK],
                                     "win": vsw[:, k, P + g * DK:P + (g + 1) * DK],
                                     "mla": v_mla[:, k, (g * HPG + j) * DK:(g * HPG + j + 1) * DK],
                                     }[UNITS[u][0]]
                                n = NCMP if UNITS[u][0] == "cmp" else P
                                parts.append((v, prob_t[0:n, u % 4, j, k, :]))
                        for n, (v, p) in enumerate(parts):
                            mn = mm(bank[DK * g:DK * g + DK, b, j * P:(j + 1) * P], v, p,
                                    n == 0, n == len(parts) - 1)
                    mn.then_inc(*did("attn_raw", (l, i)))
                    readers[b] = [("attn_out", (l, i))]

                unit_scores(0)
                unit_scores(1)
                todo = []
                for u in range(NU):
                    b = 7 - (PV_OF[u] % 2)
                    refill(b)
                    project("w_in", l * 29 + 13 + u, xn, None, ("merge_raw", (l, u)),
                            [("merge", (l, u))], b=b)
                    unit_transpose(u)
                    if u + 2 < NU:
                        unit_scores(u + 2)
                    if todo:
                        unit_values(todo.pop())
                    if u == PV[PV_OF[u]][3][-1]:
                        todo.append(PV_OF[u])
                unit_values(todo.pop())
                for c in range(4):
                    for name, x, first in (("w_a", oa_t, 0), ("w_b", ob_t, 4)):
                        w, used = arrived(name, l * 4 + c)
                        if c == 0:
                            for i in range(first, first + 4):
                                pe.wait_ge(*of("attn_out", (l, i)))
                        for e in range(2):
                            f = 2 * c + e
                            b = next_bank()
                            for k in range(4):
                                j = e * 4 + k
                                mn = mm(cols(b), w[:, j * P:(j + 1) * P], x[:, k, :], k == 0, k == 3)
                            mn.then_inc(*did(name + "_raw", (l, f), also=[used] if e else []))
                            readers[b] = [(name + "_gated", (l, f))]
                            held[name + "_raw", (l, f)] = b
                down("w_out", l * KD, xn, KD, "merged", s, next_norm)

            pe.wait_ge(*of("consts_in", 0))
            ada(0, 2 * KD)
            for k in range(KD):
                squares_sum(0, k, KD)
            for l in range(DEPTH):
                ffn(3 * l, l, "ffn1", 3 * l, 3 * l + 1, 1 if l == 0 else None)
                mix(l, 3 * l + 1, 3 * l + 1, 3 * l + 2)
                ffn(3 * l + 2, l, "ffn2", 3 * l + 2, 3 * l + 3, 2 if l == 0 else None)
            spread(6)
            for k in range(KD):
                squares_sum("mem", k, KD)
            spread("mem")
            for k in range(KD):
                squares_sum((0, 0), k, KD)

            def recurrent(i):
                spread((i, 0))
                for f in range(2 * KD):
                    project("a_w_in", f, xn, ("normed2", (i, 0)) if f == 0 else None, ("lru_in_raw", f),
                            [("lru_in", f)])
                for g in range(2):
                    for h in range(LRU_HEADS):
                        for e in range(2):
                            f = 2 * h + e
                            if f % 4 == 0:
                                w, used = arrived("a_gate_w", (g * KD + f) // 4)
                            b = next_bank()
                            for k in range(2):
                                if g == 0:
                                    pe.wait_ge(*of("conv", 2 * h + k))
                                j = (f % 4) * 2 + k
                                mn = mm(cols(b), w[:, j * P:(j + 1) * P], conv[:, 2 * h + k, :],
                                        k == 0, k == 1)
                            mn.then_inc(*did("lru_gate_raw", (g, f), also=[used] if f % 4 == 3 else []))
                            readers[b] = [("lru_gate", (g, f))]
                            held["lru_gate_raw", (g, f)] = b
                mem_keys(i)
                down("a_w_out", 0, lru_h, KD, "lru_gated", (i, 0), (i, 1), "mixed_sq")

            def mem_keys(i):
                for f in range(KD):
                    project("c_w_kv", i * 2 * KD + f, mem_n, ("normed2", "mem") if (i, f) == (0, 0) else None,
                            ("mem_k_raw", (i, f)), [("mem_k", (i, f))])

            def mem_values(i):
                for f in range(KD):
                    w, used = arrived("c_w_kv", i * 2 * KD + KD + f)
                    b = next_bank()
                    for t in range(QT):
                        for k in range(KD):
                            mn = mm(cols(b, P, t * P), mem_n[:, k, t * P:(t + 1) * P],
                                    w[:, k * P:(k + 1) * P], k == 0, k == KD - 1)
                    mn.then_inc(*did("mem_v_raw", (i, f), also=[used]))
                    readers[b] = [("mem_v", (i, f))]
                    held["mem_v_raw", (i, f)] = b

            def cross(i):
                spread((i, 2))
                for f in range(KD):
                    project("c_w_q", i * KD + f, xn, ("normed2", (i, 2)) if f == 0 else None,
                            ("mem_q_raw", (i, f)), [("mem_q", (i, f))])
                for k in range(KD):
                    pe.wait_ge(*of("mem_k", (i, k)))
                for q in range(QT):
                    refill(4 + 2 * q, 5 + 2 * q)
                    for h in range(MH):
                        for k in range(2):
                            pe.wait_ge(*of("mem_q", (i, 2 * h + k)))
                            mn = mm(bank[:, 4 + 2 * q + h // 2, (h % 2) * S:(h % 2 + 1) * S],
                                    q2[:, 2 * h + k, q * P:(q + 1) * P], k2[:, 2 * h + k, :],
                                    k == 0, k == 1)
                    mn.then_inc(*did("mem_scores_raw", (i, q)))
                    readers[4 + 2 * q] = readers[5 + 2 * q] = [("mem_exps", (i, q))]
                mem_values(i)
                for q in range(QT):
                    refill(4 + 2 * q, 5 + 2 * q)
                    pe.wait_ge(*of("mem_probs", (i, q)))
                    for h in range(MH):
                        for k in range(QT):
                            c = (h % 2) * S + k * P
                            mn = nc.tensor.transpose(bank[:, 4 + 2 * q + h // 2, c:c + P],
                                                     sc2[:, q, h, k * P:(k + 1) * P], ident)
                    mn.then_inc(*did("mem_prob_t_raw", (i, q)))
                    readers[4 + 2 * q] = [("mem_prob_t_a", (i, q))]
                    readers[5 + 2 * q] = [("mem_prob_t_b", (i, q))]
                for f in range(KD):
                    pe.wait_ge(*of("mem_v", (i, f)))
                for q in range(QT):
                    refill(2 * q, 2 * q + 1)
                    pe.wait_ge(*of("mem_prob_t_a", (i, q)))
                    pe.wait_ge(*of("mem_prob_t_b", (i, q)))
                    for f in range(KD):
                        for k in range(QT):
                            mn = mm(bank[:, 2 * q + f // 4, (f % 4) * P:(f % 4 + 1) * P],
                                    v2[:, k, f * P:(f + 1) * P], pt2[:, q, f // 2, k, :],
                                    k == 0, k == QT - 1)
                    mn.then_inc(*did("mem_out_raw", (i, q)))
                    readers[2 * q] = [("mem_out_a", (i, q))]
                    readers[2 * q + 1] = [("mem_out_b", (i, q))]
                for q in range(QT):
                    pe.wait_ge(*of("mem_out_a", (i, q)))
                    pe.wait_ge(*of("mem_out_b", (i, q)))
                down("c_w_o", i * KD, o2, KD, None, (i, 1), (i, 3), "mixed_sq")

            def mlp(i):
                spread((i, 4))
                for f in range(KF2):
                    project("m_w_up", i * KF2 + f, xn, ("normed2", (i, 4)) if f == 0 else None,
                            ("relu_raw", (i, f)), [("relu", (i, f))])
                down("m_w_down", i * KF2, hid2, KF2, "hidden2", (i, 2), (i, 5), "mixed_sq")

            def head_sums(name, src, ready):
                refill(6)
                for k in range(KD):
                    pe.wait_ge(*of(ready, k))
                    for t in range(QT):
                        mn = mm(bank[:, 6, t * RH + 2 * k:t * RH + 2 * k + 2],
                                src[:, k, t * P:(t + 1) * P], const("head_of"), True, True)
                mn.then_inc(*did("head_sums", name))
                readers[6] = [("head_sums_read", name)]

            def head_spread(name, m):
                pe.wait_ge(*of("head_stat", name))
                for k in range(KD):
                    b = k // 2
                    if k % 2 == 0:
                        refill(b)
                    for t in range(QT):
                        c = t * RH + 2 * k
                        mn = mm(cols(b, P, (k % 2) * S + t * P), wide[name][:, c * RN:(c + 2) * RN], ident,
                                True, True)
                    if k % 2:
                        mn.then_inc(*did("head_spread", (name, b)))
                        readers[b] = [("head_used", (name, b))]

            def delta_mixer(i):
                spread((i, 0))
                for j in range(3):
                    for f in range(KD):
                        project("b_w_rkv", j * KD + f, xs_t[j % 2], ("xs", j) if f == 0 else None,
                                ("rkv_raw", (j, f)), [("rkv", (j, f))])
                for j, wd in ((3, RN), (4, RN), (5, P)):
                    w, used = arrived("lora1", j - 3, KD * wd)
                    b = next_bank()
                    for k in range(KD):
                        pe.wait_ge(*of("xs", (j, k)))
                        mn = mm(bank[0:wd, b, 0:S], w[:, k * wd:(k + 1) * wd], xs_t[j % 2][:, k, :],
                                k == 0, k == KD - 1)
                    mn.then_inc(*did("rkv_raw", (j, KD - 1), also=[used]))
                    readers[b] = [("lora", j)]
                    held["rkv_raw", (j, KD - 1)] = b
                    w, used = arrived("lora2", j - 3)
                    pe.wait_ge(*of("lora", j))
                    for f in range(KD):
                        b = next_bank()
                        mm(cols(b), w[0:wd, f * P:(f + 1) * P], silu[0:wd, j % 2, :], True, True).then_inc(
                            *did("lora_raw", (j, f), also=[used] if f == KD - 1 else []))
                        readers[b] = [("lora_out", (j, f))]
                        held["lora_raw", (j, f)] = b
                head_sums("kk", bt, "kk_sq")
                head_spread("kk", 0)
                head_sums("bonus", bt, "rkr")
                head_spread("bonus", 1)
                pe.wait_ge(*of("delta_in", 0))
                for c in range(NCH):
                    chunk(c)
                head_sums("mean", xn, "y_all")
                head_spread("mean", 2)
                head_sums("var", slot[3], "yc_sq")
                head_spread("var", 3)
                mem_keys(i)
                down("b_w_o", 0, xn, KD, "delta_out", (i, 0), (i, 1), "mixed_sq")

            def chunk(c):
                ts = slice(c * CH, (c + 1) * CH)
                half = [slice(0, RN), slice(RN, 2 * RN)]
                lo = half[0]
                for r in range(4):
                    refill(6, 7)
                    for p in range(2):
                        for e in range(2):
                            k = 2 * r + e
                            for m, src in enumerate((bt, kt_)):
                                mn = mm(bank[lo, 6 + p, e * 256 + m * P:e * 256 + (m + 1) * P],
                                        src[half[p], k, ts], ar[half[p], k, :, ts], True, True)
                        mn.then_inc(*did("mats_raw", (c, r, p)))
                        readers[6 + p] = [("mats", (c, r, p))]
                for m, src in enumerate((bt, kt_, v_t)):
                    for e in range(2):
                        b = 2 * m + e
                        refill(b)
                        for k in range(4):
                            mn = nc.tensor.transpose(bank[lo, b, k * P:(k + 1) * P],
                                                     src[:, 4 * e + k, ts], ident)
                        mn.then_inc(*did("tm_raw", (c, m, e)))
                        readers[b] = [("tm", (c, m, e))]
                for n in range(LEVELS):
                    for p in range(2):
                        refill(p)
                        pe.wait_ge(*of("level", (c, n, p)))
                        if n:
                            pe.wait_ge(*of("inv", (c, n - 1, p)))
                        for h in range(8):
                            hh = p * 8 + h
                            rhs = xi[:, hh, :] if n else ident[lo, 0:CH]
                            mn = mm(bank[lo, p, h * CH:(h + 1) * CH], mi[:, hh, :], rhs, True, True)
                        mn.then_inc(*did("y_raw", (c, n, p)))
                        readers[p] = [("y_inv", (c, n, p))] if n else [("inv", (c, n, p))]
                    if n == 0:
                        continue
                    for p in range(2):
                        pe.wait_ge(*of("y_inv", (c, n, p)))
                        refill(2 + p, 4 + p)
                        pe.wait_ge(*of("inv_t", (c, n - 1, p)))
                        if n < LEVELS - 1:
                            for h in range(8):
                                hh = p * 8 + h
                                mn = mm(bank[lo, 2 + p, h * CH:(h + 1) * CH], xit[:, hh, :], yi[:, hh, :],
                                        True, True)
                            mn.then_inc(*did("inv_raw", (c, n, p)))
                            readers[2 + p] = [("inv", (c, n, p))]
                        for h in range(8):
                            hh = p * 8 + h
                            mn = mm(bank[lo, 4 + p, h * CH:(h + 1) * CH], yi[:, hh, :], xit[:, hh, :],
                                    True, True)
                        mn.then_inc(*did("inv_t_raw", (c, n, p)))
                        readers[4 + p] = [("inv_t", (c, n, p))]
                refill(0, 1, 2, 3)
                pe.wait_ge(*of("state", c - 1))
                for p in range(2):
                    for k in range(KD):
                        mn = mm(bank[lo, p, k * CH:(k + 1) * CH], ar[half[p], k, 0, ts], state[half[p], k, :],
                                True, True)
                mn.then_inc(*did("q_state_raw", c))
                readers[0] = readers[1] = [("q_state", c)]
                for e in range(2):
                    pe.wait_ge(*of("tm", (c, 2, e)))
                for p in range(2):
                    for k in range(KD):
                        h = 2 * k + p
                        mn = mm(bank[lo, 2 + p, k * CH:(k + 1) * CH], mats[:, p * 8 + k, 2 * CH:3 * CH],
                                tm[:, 2, h * RN:(h + 1) * RN], True, True)
                mn.then_inc(*did("q_value_raw", c))
                readers[2] = readers[3] = [("q_sum", c)]
                refill(4, 5)
                pe.wait_ge(*of("q_sum", c))
                for p in range(2):
                    pe.wait_ge(*of("inv_t", (c, LEVELS - 1, p)))
                    for k in range(KD):
                        mn = mm(bank[lo, 4 + p, k * CH:(k + 1) * CH], xit[:, p * 8 + k, :],
                                mi[:, p * 8 + k, :], True, True)
                mn.then_inc(*did("sa_raw", c))
                readers[4] = readers[5] = [("sa", c)]
                refill(6, 7)
                for p in range(2):
                    for k in range(KD):
                        mn = mm(bank[half[p], 6 + p, k * CH:(k + 1) * CH], state[half[p], k, :],
                                ar[half[p], k, 1, ts], True, True)
                mn.then_inc(*did("y_state_raw", c))
                readers[6] = readers[7] = [("y_state", c)]
                pe.wait_ge(*of("sa", c))
                for m in range(2):
                    for e in range(2):
                        pe.wait_ge(*of("tm", (c, m, e)))
                refill(1)
                for p in range(2):
                    for k in range(KD):
                        h = 2 * k + p
                        o = bank[half[p], 1, k * RN:(k + 1) * RN]
                        mm(o, tm[:, 0, h * RN:(h + 1) * RN], yi[:, p * 8 + k, :], True, False)
                        mn = mm(o, tm[:, 1, h * RN:(h + 1) * RN], tm[:, 2, h * RN:(h + 1) * RN], False, True)
                mn.then_inc(*did("state_raw", c))
                readers[1] = [("state_sum", c)]
                refill(0)
                for p in range(2):
                    for k in range(KD):
                        h = 2 * k + p
                        o = bank[half[p], 0, k * CH:(k + 1) * CH]
                        mm(o, yi[:, p * 8 + k, :], mats[:, p * 8 + k, CH:2 * CH], True, False)
                        mn = mm(o, tm[:, 2, h * RN:(h + 1) * RN], mats[:, p * 8 + k, 3 * CH:4 * CH],
                                False, True)
                mn.then_inc(*did("y_chunk_raw", c))
                readers[0] = [("y", c)]

            for i in range(DEPTH):
                if i == 0:
                    recurrent(i)
                else:
                    delta_mixer(i)
                spread((i, 1))
                for k in range(KD):
                    squares_sum((i, 2), k, KD)
                cross(i)
                spread((i, 3))
                for k in range(KD):
                    squares_sum((i, 4), k, KD)
                mlp(i)
                spread((i, 5))
                if i + 1 < DEPTH:
                    for k in range(KD):
                        squares_sum((i + 1, 0), k, KD)

        @block.vector
        def _(dve):
            V = nc.vector

            def mod_sum(part):
                a, b, bk = ADA_PARTS[part]
                dve.wait_ge(*of("ada_raw", b - 1))
                if part == 0:
                    dve.wait_ge(*of("vecs_in", 0))
                V.tensor_tensor(mod[:, a:b], bank[:, bk, 0:b - a], vec("b_ada", a, b - a),
                                ALU.add).then_inc(*did("mod_sum", part))
                dve.wait_ge(*of("mod_sum", part))
                l, s0, s1 = {0: (0, 0, 2), 1: (0, 2, NMOD), 2: (1, 0, NMOD)}[part]
                for seg in range(s0, s1):
                    m = mods(l, seg, 0, KD)
                    if seg % 3 == 1:
                        last = V.tensor_scalar(m, m, 1.0, None, ALU.add)
                    elif seg in (2, 8):
                        last = V.tensor_scalar(m, m, 0.5, None, ALU.mult)
                    else:
                        continue
                    last.then_inc(*did("mod_step", (part, seg), also=[("mod", part)] if seg == (1 if part == 0 else 8) else []))

            def rstd(n, cnt=D):
                dve.wait_ge(*of("square_sums", n))
                for t in range(QT):
                    last = V.tensor_scalar(root[:, 0, t:t + 1], bank[:, 4 + t, 0:1], 1.0 / cnt, EPS,
                                           ALU.mult, ALU.add)
                    last.then_inc(*did("mean", (n, t), also=[("mean_square", n)] if t else []))
                dve.wait_ge(*of("root", n))
                V.reciprocal(root[:, 2, 0:2], root[:, 1, 0:2]).then_inc(*did("rroot", n))
                dve.wait_ge(*of("rroot", n))
                for t in range(QT):
                    V.tensor_scalar(diag[:, t, :], ident, root[:, 2, t:t + 1], None,
                                    ALU.mult).then_inc(*did("diag", (n, t), also=[("rstd_diag", n)] if t else []))

            def normalise(n, out_t, gain, event, ready=None):
                dve.wait_ge(*of("rstd", n))
                for k in range(KD):
                    V.scalar_tensor_tensor(out_t[:, k, :], X[:, k, :], gain(k), cols(4), ALU.mult,
                                           ALU.mult).then_inc(
                        *did(event, (n, k), also=[("rstd_read", n)] if k == KD - 1 else []))

            def residual(s, gain, kt=KD):
                for f in range(KD):
                    dve.wait_ge(*of("down_raw", (s, f)))
                    b = held["down_raw", (s, f)]
                    V.scalar_tensor_tensor(X[:, f, :], cols(b), gain(f), X[:, f, :], ALU.mult,
                                           ALU.add).then_inc(*did("residual", (s, f)))

            def ffn(s, l, which, norm):
                for f in range(KF):
                    dve.wait_ge(*of("silu", (s, f)))
                    dve.wait_ge(*of("up_raw", (s, f)))
                    V.tensor_tensor(hid[:, f, :], silu[:, f % 2, :], cols(held["up_raw", (s, f)]),
                                    ALU.mult).then_inc(*did("hidden", (s, f)))

            def mix(l, s, norm):
                for i in range(2):
                    dve.wait_ge(*of("in_raw", (l, 5 + i)))
                    V.tensor_copy(kv_t[:, i, :], cols(held["in_raw", (l, 5 + i)])).then_inc(*did("kv", (l, i)))
                for v in range(2):
                    dve.wait_ge(*of("kv", (l, v)))
                    x = kv_t[:, v, :].rearrange("p (n i) -> p i n", i=CMP_STRIDE)
                    for c in range(2):
                        a = c * CMP_STRIDE
                        pe_ = vec("pe", (l * 2 + v) * CMP_BLOCK + a, CMP_STRIDE)
                        V.tensor_tensor(blocks_pe[:, v, a:a + CMP_STRIDE, :], x[:, :, c:c + NCMP],
                                        bcast(pe_, NCMP), ALU.add).then_inc(
                            *did("blocks", (l, v, c), also=[("blocks_pe", (l, v))] if c else []))
                n = ("m", l)
                dve.wait_ge(*of("square_sums", n))
                for t in range(QT):
                    for c, cnt in enumerate((QRANK, KVRANK)):
                        last = V.tensor_scalar(root[:, 0, 2 * c + t:2 * c + t + 1],
                                               bank[:, 4 + t, c:c + 1], 1.0 / cnt, EPS, ALU.mult, ALU.add)
                        last.then_inc(*did("mean", (n, t, c), also=[("mean_square", n)] if t + c == 2 else []))
                dve.wait_ge(*of("root", n))
                V.reciprocal(root[:, 2, :], root[:, 1, :]).then_inc(*did("rroot", n))
                dve.wait_ge(*of("rroot", n))
                for c in range(4):
                    V.tensor_scalar(diag[:, c, :], ident, root[:, 2, c:c + 1], None, ALU.mult).then_inc(
                        *did("diag", (n, c), also=[("rstd_diag", n)] if c == 3 else []))
                dve.wait_ge(*of("rstd", n))
                for i in list(range(KQ, KQ + KKV)) + list(range(KQ)):
                    dve.wait_ge(*of("latent", (l, i)))
                    q = i < KQ
                    gain = vec("mla_q_norm", l * KQ + i) if q else vec("mla_kv_norm", l * KKV + i - KQ)
                    V.scalar_tensor_tensor(latent_n[:, i, :], latent[:, i, :], gain,
                                           cols(4, S, 0 if q else S), ALU.mult, ALU.mult).then_inc(
                        *did("latent_n", (l, i), also=[("rstd_read", n)] if i == KQ - 1 else []))
                dve.wait_ge(*of("gate_exp", (l, 1)))
                V.tensor_scalar(gates[:, :, :], gates[:, :, :], 1.0, None, ALU.add).then_inc(*did("gate_den", l))
                dve.wait_ge(*of("gate_den", l))
                V.reciprocal(gates[:, :, :], gates[:, :, :]).then_inc(*did("gates", l))
                for t in range(QT):
                    dve.wait_ge(*of("uv_raw", (l, t)))
                    V.tensor_copy(v_mla[:, t, :], cols(held["uv_raw", (l, t)], 512)).then_inc(*did("v_mla", (l, t)))
                dve.wait_ge(*of("cmp_out_raw", l))
                V.tensor_copy(kcc[:, 0:NCMP], bank[:, 5, 0:NCMP]).then_inc(*did("kcc", l))
                V.tensor_copy(vcc[0:NCMP, :], bank[0:NCMP, 5, DK:3 * DK]).then_inc(*did("vcc", l))
                rr = slice(NOPE, QH)
                for p2 in range(-1, HEADS // 2):
                    w = 1 if p2 < 0 else 2
                    dve.wait_ge(*of("rot_raw", (l, p2)))
                    if p2 >= 0:
                        dve.wait_ge(*of("roped", (l, p2 - 1)))
                    tmp = rope_tmp[rr, 0:w * S].rearrange("p (h t) -> p h t", t=S)
                    V.tensor_tensor(tmp, bank[rr, held["rot_raw", (l, p2)], 0:w * S].rearrange("p (h t) -> p h t", t=S),
                                    bcast_mid(const("sin")[rr, :], w), ALU.mult).then_inc(*did("rot_sin", (l, p2)))
                    dve.wait_ge(*of("rot_sin", (l, p2)))
                    dve.wait_ge(*of("rope_cos", (l, p2)))
                    x = rope_k[rr, :].rearrange("p (h t) -> p h t", h=1) if p2 < 0 else qh[rr, 2 * p2:2 * p2 + 2, :]
                    V.tensor_tensor(x, x, tmp, ALU.add).then_inc(
                        *did("roped", (l, p2), also=[("rope_k", l)] if p2 < 0 else [("q_mla", (l, p2))]))

                def front(u):
                    kind, g, q = UNITS[u]
                    w = width(kind, q)
                    dve.wait_ge(*of("scores_raw", (l, u)))
                    if u >= 2:
                        dve.wait_ge(*of("prob_t_raw", (l, u - 2)))
                    ps = bank[:, 2 * (u % 2):2 * (u % 2) + 2, :].rearrange("p b (j k) -> p (b j) k", k=S)[:, :, 0:w]
                    if kind == "mla":
                        bias = bcast_mid(const(f"causal{q}"), HPG)
                    else:
                        name = ("cmp" if kind == "cmp" else "alibi") + str(q)
                        bias = const(name).rearrange("p (h k) -> p h k", k=w)[:, g * HPG:(g + 1) * HPG, :]
                    s_ = scores[:, u % 2, :, 0:w]
                    V.tensor_tensor(s_, ps, bias, ALU.add).then_inc(*did("biased", (l, u)))
                    dve.wait_ge(*of("biased", (l, u)))
                    V.tensor_reduce(nmax[:, u % 2, :], s_, AX.X, ALU.max, negate=True).then_inc(
                        *did("row_max", (l, u)))
                    dve.wait_ge(*of("row_max", (l, u)))
                    V.tensor_scalar(nmax[:, u % 2, :], nmax[:, u % 2, :], MAX_CLAMP, None, ALU.min).then_inc(
                        *did("neg_max", (l, u)))

                def scale(u):
                    kind, g, q = UNITS[u]
                    dve.wait_ge(*of("exps", (l, u)))
                    d = den[:, u % 2, :]
                    V.tensor_scalar(d, d, 1.0, None, ALU.max).then_inc(*did("den", (l, u)))
                    dve.wait_ge(*of("den", (l, u)))
                    V.reciprocal(d, d).then_inc(*did("rden", (l, u), also=[("prob_scale", (l, u))] if kind == "mla" else []))
                    if kind != "mla":
                        dve.wait_ge(*of("rden", (l, u)))
                        br = ("cmp", "slc", "win").index(kind)
                        gt = gates[:, q, :].rearrange("p (h b) -> p h b", b=3)[:, g * HPG:(g + 1) * HPG, br]
                        V.tensor_tensor(d, d, gt, ALU.mult).then_inc(*did("gden", (l, u), also=[("prob_scale", (l, u))]))

                def back(u):
                    kind, g, q = UNITS[u]
                    w = width(kind, q)
                    n, kk = (NCMP, 1) if kind == "cmp" else (P, q + 1)
                    dve.wait_ge(*of("prob_t_raw", (l, u)))
                    if u >= 4:
                        dve.wait_ge(*of("attn_raw", (l, PV_OF[u - 4])))
                    V.tensor_copy(prob_t[0:n, u % 4, 2:4, 0:kk, :],
                                  bank[0:n, 5, :].rearrange("p (j k q) -> p j k q", j=2, k=2)[:, :, 0:kk, :]
                                  ).then_inc(*did("prob_t_b", (l, u)))

                front(0)
                front(1)
                scale(0)
                for u in range(NU):
                    if u + 1 < NU:
                        scale(u + 1)
                    back(u)
                    if u + 2 < NU:
                        front(u + 2)
                for c in range(4):
                    for name in ("w_a", "w_b"):
                        for e in range(2):
                            f = 2 * c + e
                            dve.wait_ge(*of(name + "_raw", (l, f)))
                            if f == 0:
                                dve.wait_ge(*of("merge_gate", (l, 0 if name == "w_a" else 1)))
                            if name == "w_a":
                                if f >= 2:
                                    dve.wait_ge(*of("merged", (s, f - 2)))
                                V.tensor_tensor(silu[:, e, :], gm[:, f, :], cols(held[name + "_raw", (l, f)]), ALU.mult
                                                ).then_inc(*did("w_a_gated", (l, f)))
                            else:
                                V.tensor_tensor(xn[:, f, :], gm[:, KD + f, :], cols(held[name + "_raw", (l, f)]), ALU.mult
                                                ).then_inc(*did("w_b_gated", (l, f)))
                                dve.wait_ge(*of("w_b_gated", (l, f)))
                                V.tensor_tensor(xn[:, f, :], xn[:, f, :], silu[:, e, :], ALU.add).then_inc(
                                    *did("merged", (s, f)))

            mod_sum(0)
            rstd(0)
            for l in range(DEPTH):
                for s3 in range(3):
                    n = 3 * l + s3
                    if s3 == 0:
                        dve.wait_ge(*of("mod", 0 if l == 0 else 2))
                    normalise(n, xn, lambda k: mods(l, 3 * s3 + 1, k), "scaled")
                    if s3 == 1:
                        mix(l, n, n)
                    else:
                        ffn(n, l, "", n)
                        if l == 0:
                            mod_sum(1 if s3 == 0 else 2)
                    if l == 0 and s3 == 0:
                        dve.wait_ge(*of("mod", 1))
                    residual(n, lambda f: mods(l, 3 * s3 + 2, f))
                    rstd(n + 1)
            normalise(6, X, lambda k: vec("final_norm", k), "x_second")
            rstd("mem")

            def gained(n, src, dst, gain):
                dve.wait_ge(*of("rstd", n))
                for k in range(KD):
                    V.scalar_tensor_tensor(dst[:, k, :], src[:, k, :], gain(k), cols(4), ALU.mult,
                                           ALU.mult).then_inc(
                        *did("normed2", (n, k), also=[("rstd_read", n)] if k == KD - 1 else []))

            def added(n, gain, event="x_added"):
                dve.wait_ge(*of("rstd", n))
                for k in range(KD):
                    V.scalar_tensor_tensor(t_out[:, k, :], t_out[:, k, :], gain(k), cols(4), ALU.mult,
                                           ALU.mult).then_inc(
                        *did("mixed_n", (n, k), also=[("rstd_read", n)] if k == KD - 1 else []))
                for k in range(KD):
                    dve.wait_ge(*of("mixed_n", (n, k)))
                    V.tensor_tensor(X[:, k, :], X[:, k, :], t_out[:, k, :], ALU.add).then_inc(
                        *did(event, (n, k)))

            def ln(i, j):
                return lambda k: vec("ln", (i * 6 + j) * KD + k)

            link = [0]

            def step(ins, also=()):
                link[0] += 1
                ins.then_inc(*did("dve_chain", link[0], also=also))
                dve.wait_ge(*of("dve_chain", link[0]))

            def recurrent(i):
                lv = vec("lam", 0, KD)
                step(V.tensor_scalar(lam[:, 0, :], lv, -1.0, None, ALU.mult))
                step(V.tensor_tensor(lam[:, 1, :], lv, lam[:, 0, :], ALU.max), [("lam_abs", 0)])
                step(V.tensor_scalar(lam[:, 0, :], lam[:, 0, :], 0.0, None, ALU.max))
                dve.wait_ge(*of("lam_ln", 0))
                step(V.tensor_tensor(lam[:, 0, :], lam[:, 0, :], lam[:, 2, :], ALU.add))
                step(V.tensor_scalar(lam[:, 2, :], lam[:, 0, :], 8.0, None, ALU.mult))
                step(V.tensor_scalar(lam[:, 3, :], lam[:, 0, :], -8.0, None, ALU.mult), [("lam", 0)])
                step(V.memset(u_pad[:, :, 0:CONV - 1], 0.0))
                for k in range(KD):
                    dve.wait_ge(*of("lru_in", KD + k))
                    step(V.tensor_scalar(conv[:, k, :], u_pad[:, k, 0:S], vec("conv_w", k),
                                         vec("conv_b", k), ALU.mult, ALU.add))
                    for tap in range(1, CONV):
                        step(V.scalar_tensor_tensor(conv[:, k, :], u_pad[:, k, tap:tap + S],
                                                    vec("conv_w", tap * KD + k), conv[:, k, :],
                                                    ALU.mult, ALU.add),
                             [("conv", k)] if tap == CONV - 1 else [])
                for k in range(KD):
                    dve.wait_ge(*of("lru_gate", (1, k)))
                    V.tensor_tensor(ig[:, k, :], ig[:, k, :], conv[:, k, :], ALU.mult).then_inc(
                        *did("i_conv", k))
                for k in range(KD):
                    dve.wait_ge(*of("lru_tanh", k))
                    step(V.tensor_tensor(lru_b[:, k, :], decay[:, k, :], decay[:, k, :], ALU.mult))
                    step(V.scalar_tensor_tensor(lru_b[:, k, :], lru_b[:, k, :], 1.0, th[:, k, :],
                                                ALU.add, ALU.mult), [("lru_mult_sq", k)])
                for k in range(KD):
                    dve.wait_ge(*of("lru_mult", k))
                    step(V.tensor_tensor(lru_b[:, k, :], lru_b[:, k, :], ig[:, k, :], ALU.mult))
                    step(V.tensor_tensor_scan(lru_h[:, k, :], decay[:, k, :], lru_b[:, k, :], 0.0,
                                              ALU.mult, ALU.add))
                    V.tensor_tensor(lru_h[:, k, :], lru_h[:, k, :], y_br[:, k, :], ALU.mult).then_inc(
                        *did("lru_gated", ((i, 0), k)))

            def cross(i):
                for q in range(QT):
                    dve.wait_ge(*of("mem_scores_raw", (i, q)))
                    ps = bank[:, 4 + 2 * q:6 + 2 * q, :].rearrange("p b (j k) -> p (b j) k", k=S)
                    V.tensor_reduce(nmax[:, q, :], ps, AX.X, ALU.max, negate=True).then_inc(
                        *did("mem_neg_max", (i, q)))
                for q in range(QT):
                    dve.wait_ge(*of("mem_exps", (i, q)))
                    V.reciprocal(den[:, q, :], den[:, q, :]).then_inc(*did("mem_rden", (i, q)))
                for q in range(QT):
                    dve.wait_ge(*of("mem_prob_t_raw", (i, q)))
                    V.tensor_copy(pt2[:, q, 2:4, :, :],
                                  bank[:, 5 + 2 * q, :].rearrange("p (j k q) -> p j k q", j=2, k=2)).then_inc(
                        *did("mem_prob_t_b", (i, q)))
                for q in range(QT):
                    dve.wait_ge(*of("mem_out_raw", (i, q)))
                    V.tensor_copy(o2[:, 4:8, q * P:(q + 1) * P],
                                  bank[:, 2 * q + 1, :].rearrange("p (f q) -> p f q", f=4)).then_inc(
                        *did("mem_out_b", (i, q)))

            def mlp(i):
                for f in range(KF2):
                    dve.wait_ge(*of("relu", (i, f)))
                    V.tensor_tensor(hid2[:, f, :], silu[:, f % 2, :], silu[:, f % 2, :], ALU.mult).then_inc(
                        *did("hidden2", ((i, 2), f)))

            def pair(b):
                return slice(2 * b, 2 * b + 2), bank[:, b, :].rearrange("p (k t) -> p k t", k=2)

            def widen(name, m):
                w = wide[name].rearrange("p (h n) -> p h n", n=RN)
                step(V.tensor_copy(w, bcast(stat[:, m, :], RN)), [("head_stat", name)])

            def delta_mixer(i):
                xx = slot[10]
                for k in range(KD):
                    dve.wait_ge(*of("normed2", ((i, 0), k)))
                    V.tensor_tensor(xx[:, k, 1:S], xn[:, k, 0:S - 1], xn[:, k, 1:S], ALU.subtract).then_inc(
                        *did("xx_rest", k))
                    V.tensor_scalar(xx[:, k, 0:1], xn[:, k, 0:1], -1.0, None, ALU.mult).then_inc(
                        *did("xx", k))
                for j, mu in enumerate((0, 2, 3, 1, 4, 5)):
                    if j >= 2:
                        dve.wait_ge(*of("rkv_raw", (j - 2, KD - 1)))
                    for k in range(KD):
                        dve.wait_ge(*of("xx", k))
                        V.scalar_tensor_tensor(xs_t[j % 2][:, k, :], xx[:, k, :], vec("mu", mu * KD + k),
                                               xn[:, k, :], ALU.mult, ALU.add).then_inc(*did("xs", (j, k)))
                dve.wait_ge(*of("rkv_raw", (5, KD - 1)))
                for k in range(KD):
                    dve.wait_ge(*of("rkv", (1, k)))
                    V.tensor_scalar(kk_t[:, k, :], k_t[:, k, :], vec("k_k", k), None, ALU.mult).then_inc(
                        *did("kk", k))
                for k in range(KD):
                    dve.wait_ge(*of("lora_out", (4, k)))
                    step(V.tensor_scalar(kt_[:, k, :], aa_t[:, k, :], 1.0, vec("k_a", k), ALU.subtract,
                                         ALU.mult))
                    step(V.scalar_tensor_tensor(k_t[:, k, :], kt_[:, k, :], 1.0, k_t[:, k, :], ALU.add,
                                                ALU.mult))
                for k in range(KD):
                    dve.wait_ge(*of("lora_out", (3, k)))
                    V.tensor_tensor_scan(xn[:, k, :], const("within"), sg_t[:, k, :], 0.0, ALU.mult,
                                         ALU.add).then_inc(*did("decay_sum", k))
                dve.wait_ge(*of("head_root", "kk"))
                step(V.tensor_scalar(stat[:, 0, :], stat[:, 0, :], 1e-12, None, ALU.max))
                step(V.reciprocal(stat[:, 0, :], stat[:, 0, :]))
                widen("kk", 0)
                for b in range(4):
                    dve.wait_ge(*of("head_spread", ("kk", b)))
                    ks, ps = pair(b)
                    V.tensor_tensor(kk_t[:, ks, :], kk_t[:, ks, :], ps, ALU.mult).then_inc(
                        *did("head_used", ("kk", b)))
                for k in range(KD):
                    dve.wait_ge(*of("rkv", (0, k)))
                    V.scalar_tensor_tensor(bt[:, k, :], r_t[:, k, :], vec("r_k", k), k_t[:, k, :],
                                           ALU.mult, ALU.mult).then_inc(*did("rkr", k))
                dve.wait_ge(*of("head_sums", "bonus"))
                step(V.tensor_copy(stat[:, 1, :], bank[:, 6, 0:QT * RH]), [("head_sums_read", "bonus")])
                widen("bonus", 1)
                for b in range(4):
                    dve.wait_ge(*of("head_spread", ("bonus", b)))
                    ks, ps = pair(b)
                    V.tensor_tensor(bonus[:, ks, :], v_t[:, ks, :], ps, ALU.mult).then_inc(
                        *did("head_used", ("bonus", b)))
                dve.wait_ge(*of("exp_plus", 0))
                step(V.tensor_tensor(ar[:, :, 1, :], r_t, kt_, ALU.mult), [("r_scaled", 0)])
                step(V.tensor_copy(w_end[:, :, :], kt_.rearrange("p k (c t) -> p k c t", t=CH)[:, :, :, CH - 1]),
                     [("w_end", 0)])
                step(V.tensor_tensor(bt, kk_t, aa_t, ALU.mult))
                dve.wait_ge(*of("exp_minus", 0))
                step(V.tensor_tensor(bt, bt, kt_, ALU.mult))
                step(V.tensor_tensor(kt_, kt_, k_t, ALU.mult))
                step(V.tensor_tensor(xn[:, :, :], xn[:, :, :], sg_t, ALU.subtract), [("before_sum", 0)])
                dve.wait_ge(*of("exp_before", 0))
                for k in range(KD):
                    step(V.scalar_tensor_tensor(ar[:, k, 0, :], kk_t[:, k, :], -1.0, r_t[:, k, :], ALU.mult,
                                                ALU.mult), [("delta_in", 0)] if k == KD - 1 else [])
                step(V.memset(state, 0.0), [("state", -1)])
                for c in range(NCH):
                    chunk(c)
                def used(name, m, out_t, src, op):
                    for b in range(4):
                        dve.wait_ge(*of("head_spread", (name, b)))
                        ks, ps = pair(b)
                        V.tensor_tensor(out_t[:, ks, :], src[:, ks, :], ps, op).then_inc(
                            *did("head_used", (name, b)))

                dve.wait_ge(*of("head_sums", "mean"))
                step(V.tensor_scalar(stat[:, 2, :], bank[:, 6, 0:QT * RH], 1.0 / RN, None, ALU.mult),
                     [("head_sums_read", "mean")])
                widen("mean", 2)
                used("mean", 2, xn, xn, ALU.subtract)
                dve.wait_ge(*of("head_sums", "var"))
                step(V.tensor_scalar(stat[:, 3, :], bank[:, 6, 0:QT * RH], 1.0 / RN, GN_EPS, ALU.mult, ALU.add),
                     [("head_var", 0), ("head_sums_read", "var")])
                dve.wait_ge(*of("head_root", "var"))
                step(V.reciprocal(stat[:, 3, :], stat[:, 3, :]))
                widen("var", 3)
                used("var", 3, xn, xn, ALU.mult)
                for k in range(KD):
                    if k % 2 == 0:
                        dve.wait_ge(*of("head_used", ("var", k // 2)))
                    step(V.scalar_tensor_tensor(xn[:, k, :], xn[:, k, :], vec("gn_g", k), bonus[:, k, :],
                                                ALU.mult, ALU.add))
                    V.scalar_tensor_tensor(xn[:, k, :], xn[:, k, :], vec("gn_b", k), g_t[:, k, :],
                                           ALU.add, ALU.mult).then_inc(*did("delta_out", ((i, 0), k)))

            def chunk(c):
                lo = slice(0, CH)
                ts = slice(c * CH, (c + 1) * CH)
                for r in range(4):
                    for p in range(2):
                        dve.wait_ge(*of("mats_raw", (c, r, p)))
                        V.tensor_tensor(mats[:, p * 8 + 2 * r:p * 8 + 2 * r + 2, :],
                                        bank[lo, 6 + p, :].rearrange("p (h w) -> p h w", h=2),
                                        bcast_mid(const("earlier")[lo, :], 2), ALU.mult).then_inc(
                            *did("mats", (c, r, p)))
                eye = bcast_mid(ident[lo, 0:CH], 8)
                for n in range(LEVELS):
                    for p in range(2):
                        hs = slice(p * 8, p * 8 + 8)
                        if n == 0:
                            dve.wait_ge(*of("level", (c, 0, p)))
                            V.tensor_tensor(xit[:, hs, :], mi[:, hs, :], eye, ALU.add).then_inc(
                                *did("inv_t", (c, 0, p)))
                            dve.wait_ge(*of("y_raw", (c, 0, p)))
                            V.tensor_tensor(xi[:, hs, :], bank[lo, p, :].rearrange("p (h t) -> p h t", h=8),
                                            eye, ALU.add).then_inc(*did("inv", (c, 0, p)))
                            continue
                        if n < LEVELS - 1:
                            dve.wait_ge(*of("inv_raw", (c, n, p)))
                            V.tensor_tensor(xi[:, hs, :], bank[lo, 2 + p, :].rearrange("p (h t) -> p h t", h=8),
                                            xi[:, hs, :], ALU.add).then_inc(*did("inv", (c, n, p)))
                        dve.wait_ge(*of("inv_t_raw", (c, n, p)))
                        V.tensor_tensor(xit[:, hs, :], bank[lo, 4 + p, :].rearrange("p (h t) -> p h t", h=8),
                                        xit[:, hs, :], ALU.add).then_inc(*did("inv_t", (c, n, p)))
                dve.wait_ge(*of("q_value_raw", c))
                dve.wait_ge(*of("q_state", c))
                V.tensor_tensor(mi, bank[lo, 2:4, :].rearrange("p b (k t) -> p (b k) t", t=CH), mi,
                                ALU.add).then_inc(*did("q_sum", c))
                dve.wait_ge(*of("state_raw", c))
                ps = bank[:, 1, :].rearrange("p (k i) -> p k i", k=KD)
                step(V.tensor_tensor(state, ps, state, ALU.add), [("state_sum", c)])
                step(V.tensor_tensor(state, state, bcast(w_end[:, :, c], RN), ALU.mult), [("state", c)])
                dve.wait_ge(*of("y_chunk_raw", c))
                dve.wait_ge(*of("y_state", c))
                ps = bank[:, 0, :].rearrange("p (k t) -> p k t", k=KD)
                last = c == NCH - 1
                step(V.tensor_tensor(xn[:, :, ts], ps, xn[:, :, ts], ALU.add),
                     [("y", c)] + [("y_all", k) for k in range(KD)] * last)

            gained("mem", slot[10], mem_n, lambda k: vec("mem_norm", k))
            rstd((0, 0))
            for i in range(DEPTH):
                gained((i, 0), X, xn, ln(i, 0))
                if i == 0:
                    recurrent(i)
                else:
                    delta_mixer(i)
                rstd((i, 1))
                added((i, 1), ln(i, 1))
                rstd((i, 2))
                gained((i, 2), X, xn, ln(i, 2))
                cross(i)
                rstd((i, 3))
                added((i, 3), ln(i, 3))
                rstd((i, 4))
                gained((i, 4), X, xn, ln(i, 4))
                mlp(i)
                rstd((i, 5))
                added((i, 5), ln(i, 5), "x_added" if i + 1 < DEPTH else "x_final")
                if i + 1 < DEPTH:
                    rstd((i + 1, 0))

        @block.scalar
        def _(act):
            A = nc.scalar

            def squares(n, ready):
                for k in range(KD):
                    if ready is not None:
                        act.wait_ge(*of(*ready(k)))
                    A.activation(sq[:, k, :], X[:, k, :], ACT.Square).then_inc(*did("squares", (n, k)))

            def root_of(n, w=2):
                act.wait_ge(*of("mean_square", n))
                A.activation(root[:, 1, 0:w], root[:, 0, 0:w], ACT.Sqrt).then_inc(*did("root", n))

            def shift(n, sh):
                for k in range(KD):
                    act.wait_ge(*of("scaled", (n, k)))
                    A.activation(xn[:, k, :], xn[:, k, :], ACT.Identity, bias=sh(k)).then_inc(
                        *did("normed", (n, k)))

            def ffn(s):
                for f in range(KF):
                    act.wait_ge(*of("gate_raw", (s, f)))
                    if f >= 2:
                        act.wait_ge(*of("hidden", (s, f - 2)))
                    A.activation(silu[:, f % 2, :], cols(held["gate_raw", (s, f)]), ACT.Silu).then_inc(
                        *did("silu", (s, f)))

            def mix(l, s):
                for i in range(KQ + KKV):
                    act.wait_ge(*of("in_raw", (l, i)))
                    A.activation(latent[:, i, :], cols(held["in_raw", (l, i)]), ACT.Copy).then_inc(*did("latent", (l, i)))
                    A.activation(sq[:, i, :], cols(held["in_raw", (l, i)]), ACT.Square).then_inc(*did("squares", (("m", l), i)))
                for i in range(2, 4):
                    act.wait_ge(*of("in_raw", (l, 5 + i)))
                    A.activation(kv_t[:, i, :], cols(held["in_raw", (l, 5 + i)]), ACT.Copy).then_inc(*did("kv_attn", (l, i)))
                root_of(("m", l), 4)
                for i in range(HPG):
                    act.wait_ge(*of("in_raw", (l, 9 + i)))
                    A.activation(q_t[:, i, :], cols(held["in_raw", (l, 9 + i)]), ACT.Copy, scale=DK ** -0.5).then_inc(
                        *did("q", (l, i)))
                act.wait_ge(*of("tok_raw", (l, 2)))
                A.activation(rope_k[NOPE:QH, :], bank[NOPE:QH, held["tok_raw", (l, 2)], 0:S], ACT.Copy).then_inc(
                    *did("rope_key", l))
                for t in range(QT):
                    A.activation(vsw[:, t, :], cols(held["tok_raw", (l, t)], 2 * P), ACT.Copy).then_inc(
                        *did("vsw", (l, t)))
                    A.activation(gates[:, t, :], cols(held["tok_raw", (l, t)], 3 * HEADS, 2 * P), ACT.Exp, scale=-1.0
                                 ).then_inc(*did("gate_exp", (l, t)))
                act.wait_ge(*of("cmp_raw", (l, 1, 1)))
                for g in range(GROUPS):
                    A.activation(cmp_h[:, g, :, 0:NCMP],
                                 bank[0:DK, 6 + g, 0:2 * CMP_STRIDE].rearrange("p (v n) -> p v n", v=2)[:, :, 0:NCMP],
                                 ACT.Gelu_apprx_tanh).then_inc(*did("cmp_hidden", (l, g)))
                for p2 in range(HEADS // 2):
                    act.wait_ge(*of("uk_raw", (l, p2)))
                    A.activation(kh[0:DK, 2 * p2:2 * p2 + 2, :],
                                 bank[0:DK, held["uk_raw", (l, p2)], :].rearrange("p (h t) -> p h t", h=2), ACT.Copy
                                 ).then_inc(*did("k_nope", (l, p2)))
                for p2 in range(HEADS // 2):
                    act.wait_ge(*of("uq_raw", (l, p2)))
                    A.activation(qh[0:QH, 2 * p2:2 * p2 + 2, :],
                                 bank[0:QH, held["uq_raw", (l, p2)], :].rearrange("p (h t) -> p h t", h=2), ACT.Copy,
                                 scale=QH ** -0.5).then_inc(*did("q_mla_scaled", (l, p2)))

                def exps(u):
                    kind, g, q = UNITS[u]
                    w = width(kind, q)
                    act.wait_ge(*of("neg_max", (l, u)))
                    if u >= 2:
                        act.wait_ge(*of("probs", (l, u - 2)))
                    for j in range(HPG):
                        s_ = scores[:, u % 2, j, 0:w]
                        A.activation(s_, s_, ACT.Exp, bias=nmax[:, u % 2, j:j + 1],
                                     accum_out=den[:, u % 2, j:j + 1]).then_inc(
                            *did("exp", (l, u, j), also=[("exps", (l, u))] if j == HPG - 1 else []))

                def merge(u):
                    act.wait_ge(*of("merge_raw", (l, u)))
                    A.activation(gm[:, u, :], cols(7 - (PV_OF[u] % 2)), ACT.Copy).then_inc(*did("merge", (l, u)))

                def back(u):
                    kind, g, q = UNITS[u]
                    n, kk = (NCMP, 1) if kind == "cmp" else (P, q + 1)
                    act.wait_ge(*of("prob_t_raw", (l, u)))
                    if u >= 4:
                        act.wait_ge(*of("attn_raw", (l, PV_OF[u - 4])))
                    A.activation(prob_t[0:n, u % 4, 0:2, 0:kk, :],
                                 bank[0:n, 4, :].rearrange("p (j k q) -> p j k q", j=2, k=2)[:, :, 0:kk, :],
                                 ACT.Copy).then_inc(*did("prob_t_a", (l, u)))

                def out_t(i):
                    kind, g, q, us = PV[i]
                    act.wait_ge(*of("attn_raw", (l, i)))
                    o = oa_t if kind == "a" else ob_t
                    r = slice(DK * g, DK * g + DK)
                    A.activation(o[r, :, q * P:(q + 1) * P],
                                 bank[r, 6 + i % 2, :].rearrange("p (j q) -> p j q", j=HPG), ACT.Copy).then_inc(
                        *did("attn_out", (l, i)))

                exps(0)
                todo = []
                for u in range(NU):
                    if u + 1 < NU:
                        exps(u + 1)
                    merge(u)
                    back(u)
                    if todo:
                        out_t(todo.pop())
                    if u == PV[PV_OF[u]][3][-1]:
                        todo.append(PV_OF[u])
                out_t(todo.pop())
                for e in range(2):
                    act.wait_ge(*of("merge", (l, NU - 1)))
                    a = gm[:, e * KD:(e + 1) * KD, :]
                    A.activation(a, a, ACT.Sigmoid).then_inc(*did("merge_gate", (l, e)))

            act.dma_start(X[:, :, :], dram["x"]).then_inc(*did("x_in", 0, by=16))
            act.dma_start(consts[:, :], dram["consts"]).then_inc(*did("consts_in", 0, by=16))
            act.dma_start(w2[:, :, :], dram["w2"]).then_inc(*did("w2_in", 0, by=16))
            act.wait_ge(*of("vecs_in", 0))
            A.activation(c_act[:, :], vec("c", 0, KD), ACT.Silu).then_inc(*did("c_act", 0))
            act.wait_ge(*of("x_in", 0))
            squares(0, None)
            root_of(0)
            for l in range(DEPTH):
                for s3 in range(3):
                    n = 3 * l + s3
                    shift(n, lambda k: mods(l, 3 * s3, k))
                    if s3 == 1:
                        mix(l, n)
                    else:
                        ffn(n)
                    squares(n + 1, lambda k: ("residual", (n, k)))
                    root_of(n + 1)
            def squares2(n, src, ready):
                for k in range(KD):
                    if ready is not None:
                        act.wait_ge(*of(*ready(k)))
                    A.activation(t_sq[:, k, :], src[:, k, :], ACT.Square).then_inc(*did("squares", (n, k)))

            def evac(raw, key, dst, done, func=ACT.Copy, ps=None, **more):
                act.wait_ge(*of(raw, key))
                A.activation(dst, cols(held[raw, key]) if ps is None else ps, func, **more).then_inc(
                    *did(done, key))

            def mixed(s, n, bias=None):
                for f in range(KD):
                    act.wait_ge(*of("down_raw", (s, f)))
                    more = {"bias": bias(f)} if bias else {}
                    ps = cols(held["down_raw", (s, f)])
                    A.activation(t_out[:, f, :], ps, ACT.Identity, **more).then_inc(*did("mixed", (s, f)))
                    A.activation(t_sq[:, f, :], ps, ACT.Square, **more).then_inc(
                        *did("squares", (n, f), also=[("mixed_sq", (s, f))]))
                root_of(n)

            def recurrent(i):
                act.wait_ge(*of("lam_abs", 0))
                A.activation(lam[:, 2, :], lam[:, 1, :], ACT.Exp, scale=-1.0).then_inc(*did("lam_exp", 0))
                act.wait_ge(*of("lam_exp", 0))
                A.activation(lam[:, 2, :], lam[:, 2, :], ACT.Ln, bias=1.0).then_inc(*did("lam_ln", 0))
                for f in range(KD):
                    evac("lru_in_raw", f, y_br[:, f, :], "lru_in", ACT.Gelu_apprx_tanh, bias=vec("b_in", f))
                for f in range(KD, 2 * KD):
                    evac("lru_in_raw", f, u_pad[:, f - KD, CONV - 1:], "lru_in", ACT.Identity,
                         bias=vec("b_in", f))
                for g, dst in ((0, rg), (1, ig)):
                    for f in range(KD):
                        evac("lru_gate_raw", (g, f), dst[:, f, :], "lru_gate", ACT.Sigmoid,
                             bias=vec("gate_b", g * KD + f))
                keys(i)
                act.wait_ge(*of("lam", 0))
                act.wait_ge(*of("lru_gate", (0, KD - 1)))
                for k in range(KD):
                    A.activation(decay[:, k, :], rg[:, k, :], ACT.Exp, scale=lam[:, 3, k:k + 1]).then_inc(
                        *did("lru_decay", k))
                    A.activation(th[:, k, :], rg[:, k, :], ACT.Tanh, scale=lam[:, 2, k:k + 1]).then_inc(
                        *did("lru_tanh", k))
                for k in range(KD):
                    act.wait_ge(*of("lru_mult_sq", k))
                    A.activation(lru_b[:, k, :], lru_b[:, k, :], ACT.Sqrt).then_inc(*did("lru_mult", k))
                mixed((i, 0), (i, 1), lambda f: vec("b_out", f))

            def keys(i):
                for f in range(KD):
                    evac("mem_k_raw", (i, f), k2[:, f, :], "mem_k")

            def cross(i):
                for f in range(KD):
                    evac("mem_q_raw", (i, f), q2[:, f, :], "mem_q", scale=256 ** -0.5)
                for q in range(QT):
                    act.wait_ge(*of("mem_neg_max", (i, q)))
                    for h in range(MH):
                        A.activation(sc2[:, q, h, :],
                                     bank[:, 4 + 2 * q + h // 2, (h % 2) * S:(h % 2 + 1) * S], ACT.Exp,
                                     bias=nmax[:, q, h:h + 1], accum_out=den[:, q, h:h + 1]).then_inc(
                            *did("mem_exp", (i, q, h), also=[("mem_exps", (i, q))] if h == MH - 1 else []))
                for f in range(KD):
                    act.wait_ge(*of("mem_v_raw", (i, f)))
                    A.activation(v2[:, :, f * P:(f + 1) * P],
                                 cols(held["mem_v_raw", (i, f)]).rearrange("p (t c) -> p t c", t=QT),
                                 ACT.Copy).then_inc(*did("mem_v", (i, f)))
                for q in range(QT):
                    act.wait_ge(*of("mem_prob_t_raw", (i, q)))
                    A.activation(pt2[:, q, 0:2, :, :],
                                 bank[:, 4 + 2 * q, :].rearrange("p (j k q) -> p j k q", j=2, k=2),
                                 ACT.Copy).then_inc(*did("mem_prob_t_a", (i, q)))
                for q in range(QT):
                    act.wait_ge(*of("mem_out_raw", (i, q)))
                    A.activation(o2[:, 0:4, q * P:(q + 1) * P],
                                 bank[:, 2 * q, :].rearrange("p (f q) -> p f q", f=4), ACT.Copy).then_inc(
                        *did("mem_out_a", (i, q)))
                mixed((i, 1), (i, 3))

            def mlp(i):
                for f in range(KF2):
                    act.wait_ge(*of("relu_raw", (i, f)))
                    if f >= 2:
                        act.wait_ge(*of("hidden2", ((i, 2), f - 2)))
                    A.activation(silu[:, f % 2, :], cols(held["relu_raw", (i, f)]), ACT.Relu).then_inc(
                        *did("relu", (i, f)))
                mixed((i, 2), (i, 5))

            def delta_mixer(i):
                for j, dst in enumerate((r_t, k_t, v_t)):
                    for f in range(KD):
                        evac("rkv_raw", (j, f), dst[:, f, :], "rkv")
                for j, wd, fn, dst, fn2, b in ((3, RN, ACT.Tanh, sg_t, ACT.Sigmoid, "w0"),
                                               (4, RN, ACT.Copy, aa_t, ACT.Sigmoid, "a0"),
                                               (5, P, ACT.Sigmoid, g_t, ACT.Copy, None)):
                    act.wait_ge(*of("rkv_raw", (j, KD - 1)))
                    if j == 5:
                        act.wait_ge(*of("lora_raw", (3, KD - 1)))
                    A.activation(silu[0:wd, j % 2, :], bank[0:wd, held["rkv_raw", (j, KD - 1)], 0:S],
                                 fn).then_inc(*did("lora", j))
                    for f in range(KD):
                        more = {"bias": vec(b, f)} if b else {}
                        evac("lora_raw", (j, f), dst[:, f, :], "lora_out", fn2, **more)
                for k in range(KD):
                    act.wait_ge(*of("kk", k))
                    A.activation(bt[:, k, :], kk_t[:, k, :], ACT.Square).then_inc(*did("kk_sq", k))
                act.wait_ge(*of("head_sums", "kk"))
                A.activation(stat[:, 0, :], bank[:, 6, 0:QT * RH], ACT.Sqrt).then_inc(
                    *did("head_root", "kk", also=[("head_sums_read", "kk")]))
                act.wait_ge(*of("head_used", ("bonus", 3)))
                act.wait_ge(*of("decay_sum", KD - 1))
                A.activation(kt_, xn[:, :, :], ACT.Exp, scale=-E_HALF).then_inc(*did("exp_plus", 0))
                act.wait_ge(*of("w_end", 0))
                A.activation(kt_, xn[:, :, :], ACT.Exp, scale=E_HALF).then_inc(*did("exp_minus", 0))
                act.wait_ge(*of("before_sum", 0))
                A.activation(r_t, xn[:, :, :], ACT.Exp, scale=-E_HALF).then_inc(*did("exp_before", 0))
                for c in range(NCH):
                    chunk(c)
                for b in range(4):
                    act.wait_ge(*of("head_used", ("mean", b)))
                    A.activation(slot[3][:, 2 * b:2 * b + 2, :], xn[:, 2 * b:2 * b + 2, :], ACT.Square
                                 ).then_inc(*did("yc_sqs", b, also=[("yc_sq", 2 * b), ("yc_sq", 2 * b + 1)]))
                act.wait_ge(*of("head_var", 0))
                A.activation(stat[:, 3, :], stat[:, 3, :], ACT.Sqrt).then_inc(*did("head_root", "var"))
                keys(i)
                mixed((i, 0), (i, 1))

            def chunk(c):
                lo = slice(0, CH)
                ts = slice(c * CH, (c + 1) * CH)
                for m in range(3):
                    for e in range(2):
                        act.wait_ge(*of("tm_raw", (c, m, e)))
                        if c:
                            act.wait_ge(*of("y_chunk_raw", c - 1))
                        A.activation(tm[:, m, e * 512:(e + 1) * 512], bank[lo, 2 * m + e, :], ACT.Copy
                                     ).then_inc(*did("tm", (c, m, e)))
                for n in range(1, LEVELS):
                    for p in range(2):
                        act.wait_ge(*of("y_raw", (c, n, p)))
                        A.activation(yi[:, p * 8:p * 8 + 8, :],
                                     bank[lo, p, :].rearrange("p (h t) -> p h t", h=8), ACT.Copy).then_inc(
                            *did("y_inv", (c, n, p)))
                act.wait_ge(*of("q_state_raw", c))
                A.activation(mi, bank[lo, 0:2, :].rearrange("p b (k t) -> p (b k) t", t=CH), ACT.Copy
                             ).then_inc(*did("q_state", c))
                act.wait_ge(*of("sa_raw", c))
                A.activation(yi, bank[lo, 4:6, :].rearrange("p b (k t) -> p (b k) t", t=CH), ACT.Copy
                             ).then_inc(*did("sa", c))
                act.wait_ge(*of("y_state_raw", c))
                for p in range(2):
                    r = slice(RN * p, RN * p + RN)
                    A.activation(xn[r, :, ts], bank[r, 6 + p, :].rearrange("p (k t) -> p k t", k=KD),
                                 ACT.Copy).then_inc(*did("y_half", (c, p), also=[("y_state", c)] if p else []))

            act.dma_start(slot[10], dram["mem"]).then_inc(*did("mem_in", 0, by=16))
            act.wait_ge(*of("mem_in", 0))
            squares2("mem", slot[10], None)
            root_of("mem")
            squares2((0, 0), X, lambda k: ("x_second", (6, k)))
            root_of((0, 0))
            for i in range(DEPTH):
                if i == 0:
                    recurrent(i)
                else:
                    delta_mixer(i)
                squares2((i, 2), X, lambda k: ("x_added", ((i, 1), k)))
                root_of((i, 2))
                cross(i)
                squares2((i, 4), X, lambda k: ("x_added", ((i, 3), k)))
                root_of((i, 4))
                mlp(i)
                if i + 1 < DEPTH:
                    squares2((i + 1, 0), X, lambda k: ("x_added", ((i, 5), k)))
                    root_of((i + 1, 0))

        @block.gpsimd
        def _(pool):
            G = nc.gpsimd
            pool.wait_ge(*of("consts_in", 0))
            rr = slice(NOPE, QH)
            for l in range(DEPTH):
                for p2 in range(-1, HEADS // 2):
                    w = 1 if p2 < 0 else 2
                    pool.wait_ge(*of("rot_raw", (l, p2)))
                    x = rope_k[rr, :].rearrange("p (h t) -> p h t", h=1) if p2 < 0 else qh[rr, 2 * p2:2 * p2 + 2, :]
                    G.tensor_tensor(x, x, bcast_mid(const("cos")[rr, :], w), ALU.mult).then_inc(
                        *did("rope_cos", (l, p2)))
                    if p2 == 0:
                        pool.wait_ge(*of("rope_k", l))
                        G.tensor_copy(kh[rr, :, :], bcast_mid(rope_k[rr, :], HEADS)).then_inc(*did("k_mla", l))
                for u in range(NU):
                    kind, g, q = UNITS[u]
                    w = width(kind, q)
                    pool.wait_ge(*of("prob_scale", (l, u)))
                    s_ = scores[:, u % 2, :, 0:w]
                    G.tensor_tensor(s_, s_, bcast(den[:, u % 2, :], w), ALU.mult).then_inc(*did("probs", (l, u)))
            for i in range(DEPTH):
                if i == 1:
                    for c in range(NCH):
                        for n in range(LEVELS):
                            for p in range(2):
                                if n == 0:
                                    for r in range(4):
                                        pool.wait_ge(*of("mats", (c, r, p)))
                                    if c:
                                        pool.wait_ge(*of("sa_raw", c - 1))
                                else:
                                    pool.wait_ge(*of("y_raw", (c, n - 1, p)))
                                    pool.wait_ge(*of("inv_t", (c, 0, p)))
                                lv = const("levels")[0:CH, n * CH:(n + 1) * CH]
                                G.tensor_tensor(mi[:, p * 8:p * 8 + 8, :], mats[:, p * 8:p * 8 + 8, 0:CH],
                                                bcast_mid(lv, 8), ALU.mult).then_inc(*did("level", (c, n, p)))
                for q in range(QT):
                    pool.wait_ge(*of("mem_rden", (i, q)))
                    G.tensor_tensor(sc2[:, q], sc2[:, q], bcast(den[:, q, :], S), ALU.mult).then_inc(
                        *did("mem_probs", (i, q)))

    return led.events, order


def tiles(w):
    k, f = w.shape
    t = w.reshape(k // P, P, f // P, P).transpose(2, 0, 1, 3)
    return np.ascontiguousarray(t.reshape(-1, TILES, P, P).transpose(0, 2, 1, 3)).reshape(-1, P, CW)


def columns(v):
    return v.reshape(-1, P).T


def laid_out(x):
    a = {k: np.asarray(v) for k, v in x.items()}
    L = range(DEPTH)
    cut = np.cumsum([0, 512, 128, 128, 128, 128, 128, 128, 24, QRANK, KVRANK, ROPE, 2 * D])
    q, kc, vc, ks, vs, kw, vw, gn, cq, ckv, kr, gm = (slice(cut[i], cut[i + 1]) for i in range(12))
    pair = np.concatenate([np.arange((g * HPG + j) * DK, (g * HPG + j + 1) * DK)
                           for j in range(HPG) for g in range(GROUPS)])
    d = {}
    d["x"] = a["x"][0].T.reshape(KD, P, S).transpose(1, 0, 2)
    d["consts"] = np.concatenate([CONSTS[k] for k in CONSTS], 1)
    pe = np.stack([np.concatenate([a[n][l].T] * 2, 0) for l in L for n in ("cmpk_pe", "cmpv_pe")], 1)
    d["vecs"] = np.concatenate(
        [columns(a["b_ada"].reshape(-1)), columns(a["c"][0]), columns(a["final_norm"]),
         columns(a["mla_q_norm"].reshape(-1)), columns(a["mla_kv_norm"].reshape(-1)),
         pe.reshape(P, -1), columns(a["ln_gains_2"].reshape(-1)),
         *(columns(a[n].reshape(-1)) for n in (
             "mem_norm_2", "a_conv_w_2", "a_conv_b_2", "a_b_in_2", "a_gate_b_2", "a_lambda_2",
             "a_b_out_2", "b_mu_2", "b_w0_2", "b_a0_2", "b_k_k_2", "b_k_a_2", "b_r_k_2",
             "b_gn_g_2", "b_gn_b_2"))], 1)
    d["w2"] = np.stack([a[n][l] for l in L for n in ("cmpk_w2", "cmpv_w2")], 1)
    each = lambda f: np.concatenate([f(l) for l in L])
    d["w_ada"] = each(lambda l: tiles(a["w_ada"][l]))
    for n in ("ffn1_gate", "ffn1_up", "ffn1_down", "ffn2_gate", "ffn2_up", "ffn2_down", "w_out"):
        d[n] = each(lambda l: tiles(a[n][l]))
    w = a["w_in"]
    d["w_in"] = each(lambda l: tiles(np.concatenate(
        [w[l][:, cq], w[l][:, ckv], w[l][:, kc], w[l][:, vc], w[l][:, ks], w[l][:, kw],
         w[l][:, q][:, pair], w[l][:, gm]], 1)))
    tok = [np.concatenate([w[l][:, s] for s in (vs, vw, gn, kr)], 1).reshape(KD, P, TOKW) for l in L]
    pad = np.zeros((1, P, TOKW), np.float32)
    d["w_tok"] = np.stack([np.concatenate([t, pad])[3 * c:3 * c + 3].transpose(1, 0, 2).reshape(P, -1)
                           for t in tok for c in range(3)])
    w1 = [a[n][l].reshape(2, CMP_STRIDE, DK, DK).transpose(0, 2, 1, 3).reshape(2, DK, -1)
          for l in L for n in ("cmpk_w1", "cmpv_w1")]
    d["cmp_w1"] = np.concatenate([np.concatenate([v, v], 1) for v in w1])
    for n in ("w_uk", "w_uv"):
        d[n] = a["mla_" + n].reshape(DEPTH, KKV, P, 512).transpose(0, 2, 1, 3).reshape(DEPTH, P, -1)
    uq = a["mla_w_uq"].reshape(DEPTH, KQ, P, HEADS, QH).transpose(0, 3, 1, 2, 4)
    d["w_uq"] = uq.reshape(DEPTH * 3, TILES, P, QH).transpose(0, 2, 1, 3).reshape(DEPTH * 3, P, -1)
    d["w_a"] = each(lambda l: tiles(a["w_branch_a"][l][pair]))
    d["w_b"] = each(lambda l: tiles(a["w_branch_b"][l][pair]))
    d["mem"] = a["mem_2"][0].T.reshape(KD, P, S).transpose(1, 0, 2)
    d["a_w_in"] = tiles(a["a_w_in_2"][0])
    gw = a["a_gate_w_2"][0].reshape(2 * LRU_HEADS, 2, P, 2, P).transpose(0, 3, 1, 2, 4)
    d["a_gate_w"] = gw.reshape(-1, TILES, P, P).transpose(0, 2, 1, 3).reshape(-1, P, CW)
    d["a_w_out"] = tiles(a["a_w_out_2"][0])
    d["b_w_rkv"] = np.concatenate([tiles(a["b_w_rkv_2"][0][j]) for j in range(3)])
    d["b_w_o"] = tiles(a["b_w_o_2"][0])
    lora = [a[n][0].reshape(KD, P, -1).transpose(1, 0, 2).reshape(P, -1)
            for n in ("b_w1_2", "b_a1_2", "b_g1_2")]
    d["lora1"] = np.stack([np.pad(v, ((0, 0), (0, CW - v.shape[1]))) for v in lora])
    lora = [a[n][0] for n in ("b_w2_2", "b_a2_2", "b_g2_2")]
    d["lora2"] = np.stack([np.pad(v, ((0, P - v.shape[0]), (0, 0))) for v in lora])
    for n in ("c_w_q", "c_w_kv", "c_w_o", "m_w_up", "m_w_down"):
        d[n] = each(lambda l: tiles(a[n + "_2"][l]))
    return {k: np.ascontiguousarray(v) for k, v in d.items()}


def build(scrap, nc, shapes):
    seen, stream = None, []
    for target in (scrap, nc):
        dram = {k: target.dram_tensor(k + "_dram", s, F32, kind="ExternalInput").ap()
                for k, s in shapes.items()}
        out = target.dram_tensor("out_dram", (P, KD, S), F32, kind="ExternalOutput").ap()
        seen, stream = program(target, dram, out, seen, stream)
    return nc


def kernel(**inputs):
    import concourse.bacc as bacc
    from concourse.bass_utils import run_bass_kernel_spmd as run

    arrays = laid_out(inputs)
    scrap, nc = (bacc.Bacc("TRN2", target_bir_lowering=False, num_devices=1) for _ in range(2))
    build(scrap, nc, {k: v.shape for k, v in arrays.items()})
    r = run(nc, [{k + "_dram": v for k, v in arrays.items()}], core_ids=[0])
    y = r.results[0]["out_dram"]
    return y.transpose(1, 0, 2).reshape(D, S).T.reshape(1, S, D).copy()
```

```python
import numpy as np
import concourse.bass as bass
from concourse import mybir
from contextlib import ExitStack

F32 = mybir.dt.float32
F32R = mybir.dt.float32r
ALU = mybir.AluOpType
ACT = mybir.ActivationFunctionType
AX = mybir.AxisListType

P = 128
D = 1024
S = 256
KD = D // P
QT = S // P
DEPTH = 2
DFF = 2816
KF = DFF // P
NMOD = 9
HEADS = 8
GROUPS = 2
HPG = HEADS // GROUPS
DK = 64
CMP_BLOCK, CMP_STRIDE = 32, 16
NCMP = S // CMP_STRIDE - CMP_BLOCK // CMP_STRIDE + 1
NOPE, ROPE = 64, 32
QH = NOPE + ROPE
QRANK, KVRANK = 384, 256
KQ, KKV = QRANK // P, KVRANK // P
MERGE = 2 * KD
EPS = 1e-6
MASKED = -1e30
MAX_CLAMP = 1e29
TOKW = 2 * 128 + 3 * HEADS + ROPE
LRU_HEADS, LRU_BLOCK = 4, 256
CONV = 4
RH, RN = 16, 64
CH = 64
NCH = S // CH
LEVELS = 6
MH = 4
FF2 = 4 * D
KF2 = FF2 // P
GN_EPS = 64e-5
E_HALF = float(np.exp(-0.5))

HEAP = 112 * 256
TILES = 8
CW = TILES * P
RING = 9
SPLITS = 4
FIRST = 3
LAG = 2
AHEAD = SPLITS - 1


def constant_columns():
    t = np.arange(S)
    c = {}
    c["ident"] = np.eye(P)
    c["ones"] = np.ones((P, P))
    rot = np.zeros((P, ROPE))
    half = ROPE // 2
    for i in range(half):
        rot[NOPE + half + i, i] = -1.0
        rot[NOPE + i, half + i] = 1.0
    c["rot"] = rot
    inv = np.float32(10000.0) ** (-np.arange(half, dtype=np.float32) / np.float32(half))
    ang = np.arange(S, dtype=np.float32)[None, :] * inv[:, None].astype(np.float32)
    cs = np.zeros((P, S)); sn = np.zeros((P, S))
    cs[NOPE:QH] = np.concatenate([np.cos(ang), np.cos(ang)])
    sn[NOPE:QH] = np.concatenate([np.sin(ang), np.sin(ang)])
    c["cos"], c["sin"] = cs, sn
    slope = 2.0 ** (-8.0 * np.arange(1, HEADS + 1) / HEADS)
    for q in range(QT):
        tq = t[q * P:(q + 1) * P]
        keys = t[:(q + 1) * P]
        dist = (tq[:, None] - keys[None, :]).astype(np.float64)
        mask = np.where(dist >= 0, 0.0, MASKED)
        c[f"causal{q}"] = mask
        c[f"alibi{q}"] = np.stack([-s * dist + mask for s in slope], 1).reshape(P, -1)
        end = np.arange(NCMP) * CMP_STRIDE + CMP_BLOCK - 1
        dc = (tq[:, None] - end[None, :]).astype(np.float64)
        cm = np.where(dc >= 0, 0.0, MASKED)
        c[f"cmp{q}"] = np.stack([-s * dc + cm for s in slope], 1).reshape(P, -1)
    a, b = np.arange(CH)[:, None], np.arange(CH)[None, :]
    m = np.zeros((P, 4, CH))
    m[:CH] = np.stack([a < b, a <= b, a < b, a <= b], 1)
    c["earlier"] = m.reshape(P, -1)
    m = np.zeros((P, LEVELS, CH))
    for n in range(LEVELS):
        m[:CH, n] = (a >> n + 1 == b >> n + 1) & (a >> n & 1 == 0) & (b >> n & 1 == 1)
    c["levels"] = m.reshape(P, -1)
    c["within"] = np.tile((t % CH != 0).astype(float), (P, 1))
    c["head_of"] = np.kron(np.eye(2), np.ones((RN, 1)))
    return {k: v.astype(np.float32) for k, v in c.items()}


def packed(parts):
    at, n = {}, 0
    for k, w in parts:
        at[k] = (n, n + w)
        n += w
    return at, n


CONSTS = constant_columns()
ATTN = [k for k in CONSTS if k in ("cos", "sin") or k.startswith(("causal", "alibi", "cmp"))]
DELTA = ["earlier", "levels", "within"]
CONST_AT, CONST_W = packed([(k, v.shape[1]) for k, v in CONSTS.items() if k not in ATTN + DELTA])
ATTN_AT, ATTN_W = packed([(k, CONSTS[k].shape[1]) for k in ATTN])
DELTA_AT, DELTA_W = packed([(k, CONSTS[k].shape[1]) for k in DELTA])

VEC_COLS = [("b_ada", DEPTH * NMOD * KD), ("c", KD), ("final_norm", KD),
            ("mla_q_norm", DEPTH * KQ), ("mla_kv_norm", DEPTH * KKV), ("pe", DEPTH * 2 * CMP_BLOCK),
            ("ln", DEPTH * 6 * KD), ("mem_norm", KD), ("conv_w", CONV * KD), ("conv_b", KD),
            ("b_in", 2 * KD), ("gate_b", 2 * KD), ("lam", KD), ("b_out", KD), ("mu", 6 * KD),
            ("w0", KD), ("a0", KD), ("k_k", KD), ("k_a", KD), ("r_k", KD), ("gn_g", KD), ("gn_b", KD)]
VEC_AT, VEC_W = packed(VEC_COLS)


def bcast(x, n):
    return x.unsqueeze(len(x.shape)).broadcast_to((*x.shape, n))


def bcast_mid(x, n):
    return x.unsqueeze(1).broadcast_to((x.shape[0], n, x.shape[1]))


FILLED = ("square_sums", "rstd", "head_sums", "head_spread", "chunk_used")


class Ledger:

    def __init__(self, nc, ctx, seen):
        self.nc, self.ctx, self.seen = nc, ctx, seen
        self.counts, self.events, self.sems = {}, {}, {}
        self.fixed = False
        self.taken = 0

    def sem(self, name):
        if name not in self.sems:
            self.sems[name] = self.ctx.enter_context(self.nc.semaphore(name))
        return self.sems[name]

    def did(self, name, key, also=(), by=1):
        kind = "bank_filled" if name.endswith("_raw") or name in FILLED else name
        self.counts[kind] = self.counts.get(kind, 0) + by
        for event in ((name, key), *also):
            assert event not in self.events, event
            self.events[event] = (kind, self.counts[kind], self.taken)
        return self.sem(kind), by

    def of(self, name, key):
        if self.seen is None:
            return self.sem("first_writing"), 1
        sem, count, taken = self.seen[(name, key)]
        if (name, key) in self.events:
            taken = self.events[(name, key)][2]
        if not self.fixed:
            self.taken = max(self.taken, taken)
        return self.sem(sem), count


def program(nc, dram, out, seen, stream):
    ctx = ExitStack()
    with ctx:
        led = Ledger(nc, ctx, seen)
        did, of = led.did, led.of
        order = []

        kinds, split_no = [], {}

        def ahead(taken):
            last, n, cut = None, max(taken - 1, 0), 0
            while n < len(kinds):
                if n >= taken and (cut == AHEAD or last is not None and n - last >= RING):
                    break
                if last is None and kinds[n] != "ada":
                    last = n
                cut += n >= taken and kinds[n] == "cut"
                n += 1
            return n

        def sb(name, shape, dtype=F32):
            return ctx.enter_context(nc.sbuf_tensor(name, shape, dtype))

        def next_place():
            return -(-nc.sbuf_base // 32) * 32

        ring_at = next_place()
        ring = sb("weight_ring", [P, RING, CW])
        w_lo = nc.alloc_sbuf_tensor_at("weight_lower", [P, RING, CW], F32R, offset=ring_at)
        w_hi = sb("weight_upper", [P, SPLITS, CW], F32R)
        X = sb("x_t", [P, KD, S])
        xn = sb("xn_t", [P, KD, S])
        xn_hi = sb("xn_upper", [P, KD, S], F32R)
        delta_consts = nc.alloc_sbuf_tensor_at("delta_consts", [P, DELTA_W], F32, offset=next_place())
        xn_hl = [xn_hi, sb("xn_lower", [P, KD, S], F32R)]
        consts = sb("consts", [P, CONST_W])
        vecs = sb("vecs", [P, VEC_W])
        mod = sb("mod", [P, DEPTH * NMOD * KD])
        c_act = sb("c_act", [P, KD])
        silu = sb("silu", [P, 2, S])
        root = sb("root", [P, 4, 4])
        diag = sb("diag", [P, 4, P])
        nmax = sb("nmax", [P, 2, HPG])
        den = sb("den", [P, 2, HPG])
        stat = sb("stat", [P, 4, QT * RH])
        w_end = sb("w_end", [P, KD, NCH])
        lam = sb("lam", [P, 4, KD])
        w2 = sb("w2", [DK, DEPTH * 2, DK])
        heap_at = next_place()
        heap = sb("heap", [P, HEAP])
        free = [0]

        def take(n):
            free[0] += n
            assert free[0] <= HEAP, free
            return heap[:, free[0] - n:free[0]]

        def tall(n=KD, w=S):
            return take(n * w).rearrange("p (k t) -> p k t", t=w)

        def parts(name, *starts, n=KD):
            return [nc.alloc_sbuf_tensor_at(name + which, [P, n, S], F32R, offset=heap_at + 4 * a)
                    for which, a in zip(("_upper", "_lower"), starts)]

        arena = take(32 * S)
        work = take(16 * S)
        scores = take(2 * HPG * S).rearrange("p (a b t) -> p a b t", a=2, b=HPG)
        sq = tall()
        q_t = sq[:, 0:HPG, :]
        kv_t = sq[:, HPG:, :]
        vsw = tall(QT, 2 * P)
        gates = tall(QT, 3 * HEADS)
        latent_n = tall(KQ + KKV)
        v_mla = tall(QT, HEADS * DK)
        oa_hl = parts("branch_a", free[0], free[0] + HPG * S, n=HPG)
        take(2 * HPG * S)
        ob_hl = parts("branch_b", free[0], free[0] + HPG * S, n=HPG)
        take(2 * HPG * S)
        cmp_h = take(GROUPS * 2 * CMP_STRIDE)[0:DK, :].rearrange("p (g v n) -> p g v n", g=GROUPS, v=2)
        kcc = take(CMP_STRIDE)
        vcc = take(P)[0:CMP_STRIDE, :]
        rope_tmp = take(2 * S)
        rope_k = take(S)
        attn_consts = take(ATTN_W)
        bank = ctx.enter_context(nc.psum_tensor("banks", [P, 8, 512], F32))

        ada_part = v_mla[:, :, :].rearrange("p a (b c) -> p (a b) c", c=P)
        hid = arena.rearrange("p (k t) -> p k t", t=S)
        hid_hl = parts("hidden", 0, KF * S, n=KF)
        gm = hid[:, 0:MERGE, :]
        qh = hid[:, MERGE:MERGE + HEADS, :]
        kh = hid[:, MERGE + HEADS:MERGE + 2 * HEADS, :]
        wk = work.rearrange("p (k t) -> p k t", t=S)
        blocks_pe = work[:, KD * S:KD * S + 2 * CMP_BLOCK * NCMP].rearrange(
            "p (v i n) -> p v i n", v=2, i=CMP_BLOCK)
        prob_t = work.rearrange("p (u j k q) -> p u j k q", u=4, j=HPG, k=QT)
        latent = scores[:, :, :, :].rearrange("p a b t -> p (a b) t")[:, 0:KQ + KKV, :]

        free[0] = 0
        slot = [tall() for _ in range(HEAP // (KD * S))]

        def slots(a, n, off=0):
            return heap[:, a * KD * S + off:a * KD * S + off + n]

        mem_n = slot[0]
        t_out, t_sq = slot[11], slot[12]
        UW = S + CONV - 1
        y_br = slot[1]
        u_pad = slots(2, KD * UW).rearrange("p (k t) -> p k t", t=UW)
        conv, rg, ig, decay, th, lru_b, lru_h = slot[4:11]
        conv_hl = parts("conv", 9 * KD * S, 10 * KD * S)
        lru_hl = parts("lru", 5 * KD * S, 6 * KD * S)
        q2, k2 = slot[1], slot[13]
        o2_hl = parts("memory_read", 9 * KD * S, 10 * KD * S)
        v2 = slots(5, KD * S).rearrange("p (k c) -> p k c", k=QT)
        sc2 = slots(2, KD * S).rearrange("p (u h k) -> p u h k", u=QT, h=MH)
        pt2 = slots(3, KD * S).rearrange("p (u h k q) -> p u h k q", u=QT, h=MH, k=QT)
        hid2_hl = parts("hidden2", KD * S, 5 * KD * S, n=KF2)
        ar = slots(1, 2 * KD * S).rearrange("p (k m t) -> p k m t", k=KD, m=2)
        bt, kt_, v_t, g_t, bonus = slot[3:8]
        mats = slots(8, RH * 4 * CH)[0:CH, :].rearrange("p (h w) -> p h w", h=RH)
        inv = slots(10, 4 * RH * CH)[0:CH, :].rearrange("p (m h t) -> p m h t", m=4, h=RH)
        xi, xit, yi, mi = (inv[:, m] for m in range(4))
        tm = slots(12, 3 * D)[0:CH, :].rearrange("p (m c) -> p m c", m=3)
        state = slots(12, KD * RN, 3 * D).rearrange("p (k i) -> p k i", k=KD)
        r_t, k_t, kk_t, aa_t, sg_t = slot[8], slot[9], slot[10], slot[11], slot[12]
        xs_t = [slot[3], slot[4]]
        xs_hl = [parts(f"shifted_{i}", a * KD * S, b * KD * S) for i, (a, b) in enumerate(((1, 2), (7, 13)))]
        wide = {n: slots(i, QT * RH * RN) for n, i in (("kk", 7), ("bonus", 1), ("mean", 4), ("var", 5))}
        rkr_t, exp_plus = slot[2], slot[13]

        def const(name, rows=P):
            if name in ATTN_AT:
                a, b = ATTN_AT[name]
                return attn_consts[0:rows, a:b]
            if name in DELTA_AT:
                a, b = DELTA_AT[name]
                return delta_consts[0:rows, a:b]
            a, b = CONST_AT[name]
            return consts[0:rows, a:b]

        def vec(name, i=0, n=1):
            a = VEC_AT[name][0]
            return vecs[:, a + i:a + i + n]

        def mods(l, seg, k, n=1):
            a = (l * NMOD + seg) * KD + k
            return mod[:, a:a + n]

        def cols(b, w=S, at=0):
            return bank[:, b, at:at + w]

        ident, ones = const("ident"), const("ones")

        UNITS, PV = [], []
        for q in range(QT):
            for g in range(GROUPS):
                PV.append(("a", g, q, [len(UNITS) + i for i in range(3)]))
                UNITS += [("cmp", g, q), ("slc", g, q), ("win", g, q)]
        for q in range(QT):
            for g in range(GROUPS):
                PV.append(("b", g, q, [len(UNITS)]))
                UNITS.append(("mla", g, q))
        NU = len(UNITS)
        PV_OF = {u: i for i, pv in enumerate(PV) for u in pv[3]}

        MERGES_FIRST = 4

        def merge_bank(m):
            return 4 + m if m < MERGES_FIRST else 7 - PV_OF[m - MERGES_FIRST] % 2

        def width(kind, q):
            return NCMP if kind == "cmp" else (q + 1) * P

        ADA = [(0, i) for i in range(NMOD * KD)] + [(1, i) for i in range(NMOD * KD)]
        ADA_PARTS = [(a * KD, b * KD, bk) for a, b, bk in (
            (0, 2, 6), (2, 3, 7), (3, 8, 6), (8, 9, 7), (9, 12, 6), (12, 18, 7))]
        ADA_AT = {0: (1, 2), 2: (3, 4), 3: (5,)}
        FFN_STEPS = KF + KD - 2

        def ada_chunks(s, step):
            if s not in ADA_AT:
                return []
            a, b = ADA_PARTS[ADA_AT[s][0]][0], ADA_PARTS[ADA_AT[s][-1]][1]
            at = [min(a + (b - a) * n // FFN_STEPS, b) for n in (step, step + 1)]
            return [(i, part) for i in range(*at) for part in ADA_AT[s]
                    if ADA_PARTS[part][0] <= i < ADA_PARTS[part][1]]

        slot_of = {}
        beside = [i for i in range(2 * NMOD * KD) if i >= ADA_PARTS[0][1] or i % 2]
        beside_no = {i: n for n, i in enumerate(beside)}

        held = {}

        block = ctx.enter_context(nc.Block())

        @block.sync
        def _(sp):
            led.taken = 0
            sp.dma_start(vecs[:, :], dram["vecs"]).then_inc(*did("vecs_in", 0, by=16))
            for n, (name, i, w) in enumerate(stream):
                if n >= RING:
                    sp.wait_ge(*of("weights_used", n - RING))
                sp.dma_start(ring[:, n % RING, 0:w], dram[name][i][:, 0:w]).then_inc(
                    led.sem(f"weights_in_{n % RING}"), 16)
            sp.wait_ge(*of("x_final", ((DEPTH - 1, 5), KD - 1)))
            sp.dma_start(out, X[:, :, :]).then_inc(*did("out_stored", 0, by=16))
            sp.wait_ge(*of("out_stored", 0))

        @block.tensor
        def _(pe):
            led.taken, led.fixed = 0, True
            readers = {}

            def refill(*banks):
                for b in banks:
                    for event in readers.pop(b, ()):
                        pe.wait_ge(*of(*event))

            def take_chunk(name, i, w, kind):
                order.append((name, i, w))
                kinds.append(kind)
                led.taken = len(order)
                return len(order) - 1

            def cut(name, i):
                n = take_chunk(name, i, CW, "cut")
                j = split_no[n] = len(split_no)
                pe.wait_ge(*of("weight_lower", j))
                return (w_hi[:, j % SPLITS, :], w_lo[:, n % RING, :]), ("cut_used", j), ("weights_used", n)

            def mm3(o, w, j, x, first, last):
                (wh, wl), (xh, xl) = w, x
                ks = slice(j * P, (j + 1) * P)
                mm(o, wl[:, ks], xh, first, False)
                mm(o, wh[:, ks], xl, False, False)
                return mm(o, wh[:, ks], xh, False, last)

            def arrived(name, i, w=CW):
                n = take_chunk(name, i, w, "whole")
                pe.wait_ge(led.sem(f"weights_in_{n % RING}"), 16 * (n // RING + 1))
                return ring[:, n % RING, 0:w], ("weights_used", n)

            def mm(o, w, r, first, last):
                return nc.tensor.matmul(o, w, r, start=first, stop=last)

            turn = [0]

            def next_bank(n=4):
                turn[0] += 1
                b = (turn[0] - 1) % n
                refill(b)
                return b

            def ada_first():
                a, b, bk = ADA_PARTS[0]
                pe.wait_ge(*of("c_act", 0))
                for i in range(a, b + 1):
                    if i < b and i not in beside_no:
                        w, used = arrived("w_ada", i)
                        for k in range(KD):
                            mn = mm(bank[:, bk, i - a:i - a + 1], w[:, k * P:(k + 1) * P],
                                    c_act[:, k:k + 1], k == 0, k == KD - 1)
                        mn.then_inc(*did("ada_raw", i, also=[used]))
                    elif i < b:
                        slot_of[i] = take_chunk("w_ada", i, CW, "ada")
                    if i == 2:
                        pe.wait_ge(*of("consts_in", 0))
                    if i - 3 in beside_no or i == b:
                        for n in [i - 3] if i < b else [i - 3, i - 1]:
                            ada_column(n, a, bk)
                readers[bk] = [("mod_sum", 0)]

            def ada_column(i, a, bk):
                pe.wait_ge(*of("ada_part", i))
                mm(bank[:, bk, i - a:i - a + 1], ada_part[:, beside_no[i] % 8, :], ones[:, 0:1], True, True
                   ).then_inc(*did("ada_raw", i))

            def ada_take(s, step):
                for i, _ in ada_chunks(s, step):
                    slot_of[i] = take_chunk("w_ada", i, CW, "ada")

            def ada_sum(s, step):
                for i, part in ada_chunks(s, step):
                    a, b, bk = ADA_PARTS[part]
                    if i == a:
                        refill(bk)
                    ada_column(i, a, bk)
                    if i == b - 1:
                        readers[bk] = [("mod_sum", part)]

            def squares_sum(n, k, kn, tts=range(QT)):
                if k == 0:
                    refill(4, 5)
                pe.wait_ge(*of("squares", (n, k)))
                src = sq if isinstance(n, int) else t_sq
                for t in tts:
                    mn = mm(bank[:, 4 + t, 0:1], src[:, k, t * P:(t + 1) * P], ones[:, 0:1],
                            k == 0, k == kn - 1)
                if k == kn - 1:
                    mn.then_inc(*did("square_sums", n))
                    readers[4] = readers[5] = [("mean_square", n)]

            def squares_of_two(n):
                pe.wait_ge(*of("squares_added", (n, KD - 2)))
                squares_sum(n, 0, KD)
                squares_sum(n, KD - 1, KD)

            def spread(n):
                refill(4)
                pe.wait_ge(*of("rstd_diag", n))
                for t in range(QT):
                    mn = mm(cols(4, P, t * P), ones, diag[:, t, :], True, True)
                mn.then_inc(*did("rstd", n))
                readers[4] = [("rstd_read", n)]

            def project(name, i, x, done, readers_of, b=None):
                w, *used = cut(name, i)
                b = next_bank() if b is None else b
                for k in range(KD):
                    mn = mm3(cols(b), w, k, [part[:, k, :] for part in x], k == 0, k == KD - 1)
                mn.then_inc(*did(*done, also=used))
                readers[b] = readers_of
                held[done] = b

            def project_first(items, x, ready):
                took = [(*cut(name, i), next_bank(), done, readers_of) for name, i, done, readers_of in items]
                for k in range(KD):
                    pe.wait_ge(*of(ready[0], (ready[1], k)))
                    for w, *used, b, done, readers_of in took:
                        mn = mm3(cols(b), w, k, [part[:, k, :] for part in x], k == 0, k == KD - 1)
                        if k == KD - 1:
                            mn.then_inc(*did(*done, also=used))
                            readers[b] = readers_of
                            held[done] = b

            def project_all(items, x, ready):
                project_first(items[:FIRST], x, ready)
                for name, i, done, readers_of in items[FIRST:]:
                    project(name, i, x, done, readers_of)

            def down(name, i0, x, kt, hidden, s, norm, reader="residual", ffn=None):
                wc = None
                for f in range(KD):
                    ada_take(ffn, KF + f)
                    b = next_bank()
                    for k in range(kt):
                        m = f * kt + k
                        if m % TILES == 0:
                            wc, *used = cut(name, i0 + m // TILES)
                        if f == 0 and hidden is not None:
                            pe.wait_ge(*of(hidden, (s, k)))
                        j = m % TILES
                        mn = mm3(cols(b), wc, j, [part[:, k, :] for part in x], k == 0, k == kt - 1)
                        ends = used if m % TILES == TILES - 1 else []
                        if k == kt - 1:
                            mn.then_inc(*did("down_raw", (s, f), also=ends))
                        elif ends:
                            mn.then_inc(*did("chunk_used", (s, m), also=ends))
                    readers[b] = [(reader, (s, f))]
                    held["down_raw", (s, f)] = b
                    ada_sum(ffn, KF + f - 1)
                ada_sum(ffn, KF + KD - 1)
                squares_of_two(norm)

            def ffn(s, l, which, norm, next_norm):
                spread(norm)
                def items(f):
                    return [(which + "_gate", l * KF + f, ("gate_raw", (s, f)), [("silu", (s, f))]),
                            (which + "_up", l * KF + f, ("up_raw", (s, f)), [("hidden", (s, f))])]

                ada_take(s, 0)
                ada_take(s, 1)
                project_first(items(0) + items(1)[0:1], xn_hl, ("normed_lower", norm))
                for f in range(1, KF):
                    if f > 1:
                        ada_take(s, f)
                    for name, i, done, readers_of in items(f)[f == 1:]:
                        project(name, i, xn_hl, done, readers_of)
                    ada_sum(s, f - 1)
                down(which + "_down", l * KF, hid_hl, KF, "hidden_lower", s, next_norm, ffn=s)

            def mix(l, s, norm, next_norm):
                spread(norm)
                done = "in_raw"
                items = [("w_in", l * 29 + i, (done, (l, i)), [("latent", (l, i)), ("squares", (("m", l), i))])
                         for i in range(KQ + KKV)]
                items += [("w_in", l * 29 + 5 + i, (done, (l, 5 + i)), [("kv" if i < 2 else "kv_attn", (l, i))])
                          for i in range(4)]
                project_all(items, xn_hl, ("normed_lower", norm))
                refill(4, 5)
                for t in range(QT):
                    for c, (a, b) in enumerate(((0, KQ), (KQ, KQ + KKV))):
                        for i in range(a, b):
                            pe.wait_ge(*of("squares", (("m", l), i)))
                            mn = mm(bank[:, 4 + t, c:c + 1], wk[:, i, t * P:(t + 1) * P],
                                    ones[:, 0:1], i == a, i == b - 1)
                mn.then_inc(*did("square_sums", ("m", l)))
                readers[4] = readers[5] = [("mean_square", ("m", l))]
                for i in range(4):
                    project("w_in", l * 29 + 9 + i, xn_hl, (done, (l, 9 + i)), [("q", (l, i))])
                refill(4)
                pe.wait_ge(*of("rstd_diag", ("m", l)))
                for c in range(4):
                    mn = mm(cols(4, P, c * P), ones, diag[:, c, :], True, True)
                mn.then_inc(*did("rstd", ("m", l)))
                readers[4] = [("rstd_read", ("m", l))]
                b0, b1, b2 = next_bank(), next_bank(), next_bank()
                at = 0
                for c, n in enumerate((3, 3, 2)):
                    w, used = arrived("w_tok", l * 3 + c, n * TOKW)
                    for k in range(at, at + n):
                        wk_ = w[:, (k - at) * TOKW:(k - at + 1) * TOKW]
                        for t, b in ((0, b0), (1, b1)):
                            mm(cols(b, TOKW - ROPE), xn[:, k, t * P:(t + 1) * P],
                               wk_[:, 0:TOKW - ROPE], k == 0, k == KD - 1)
                        mn = mm(bank[NOPE:QH, b2, 0:S], wk_[:, TOKW - ROPE:TOKW], xn[:, k, :],
                                k == 0, k == KD - 1)
                    at += n
                    mn.then_inc(*did("tok_raw", (l, c), also=[used]))
                readers[b0] = [("vsw", (l, 0)), ("gate_exp", (l, 0))]
                readers[b1] = [("vsw", (l, 1)), ("gate_exp", (l, 1))]
                readers[b2] = [("rope_key", l)]
                held["tok_raw", (l, 0)], held["tok_raw", (l, 1)], held["tok_raw", (l, 2)] = b0, b1, b2
                refill(6, 7)
                if l == 0:
                    pe.wait_ge(*of("w2_in", 0))
                for v in range(2):
                    pe.wait_ge(*of("blocks_pe", (l, v)))
                    for c in range(2):
                        w, used = arrived("cmp_w1", (l * 2 + v) * 2 + c)
                        for g in range(GROUPS):
                            r = slice(DK * g, DK * g + DK)
                            for i in range(CMP_STRIDE):
                                mn = mm(bank[0:DK, 6 + g, v * CMP_STRIDE:v * CMP_STRIDE + NCMP],
                                        w[r, i * DK:(i + 1) * DK],
                                        blocks_pe[r, v, c * CMP_STRIDE + i, :],
                                        c == 0 and i == 0, c == 1 and i == CMP_STRIDE - 1)
                        mn.then_inc(*did("cmp_raw", (l, v, c), also=[used]))
                readers[6] = [("cmp_hidden", (l, 0))]
                readers[7] = [("cmp_hidden", (l, 1))]
                for k in range(KKV):
                    pe.wait_ge(*of("latent_n", (l, KQ + k)))
                w, used = arrived("w_uk", l)
                for p2 in range(HEADS // 2):
                    b = next_bank()
                    for e in range(2):
                        h = 2 * p2 + e
                        for k in range(KKV):
                            mn = mm(bank[0:DK, b, e * S:(e + 1) * S],
                                    w[:, k * 512 + h * DK:k * 512 + (h + 1) * DK],
                                    latent_n[:, KQ + k, :], k == 0, k == KKV - 1)
                    mn.then_inc(*did("uk_raw", (l, p2), also=[used] if p2 == 3 else []))
                    readers[b] = [("k_nope", (l, p2))]
                    held["uk_raw", (l, p2)] = b
                w, used = arrived("w_uv", l)
                for t in range(QT):
                    b = next_bank()
                    for k in range(KKV):
                        mn = mm(cols(b, 512), latent_n[:, KQ + k, t * P:(t + 1) * P],
                                w[:, k * 512:(k + 1) * 512], k == 0, k == KKV - 1)
                    mn.then_inc(*did("uv_raw", (l, t), also=[used] if t == 1 else []))
                    readers[b] = [("v_mla", (l, t))]
                    held["uv_raw", (l, t)] = b
                refill(5)
                for g in range(GROUPS):
                    pe.wait_ge(*of("cmp_hidden", (l, g)))
                    mm(bank[DK * g:DK * g + DK, 5, 0:NCMP], w2[:, l * 2, :], cmp_h[:, g, 0, 0:NCMP],
                       True, True)
                for g in range(GROUPS):
                    mn = mm(bank[0:NCMP, 5, (1 + g) * DK:(2 + g) * DK], cmp_h[:, g, 1, 0:NCMP],
                            w2[:, l * 2 + 1, :], True, True)
                mn.then_inc(*did("cmp_out_raw", l))
                readers[5] = [("kcc", l), ("vcc", l)]
                for k in range(KQ):
                    pe.wait_ge(*of("latent_n", (l, k)))
                m = 0
                for p2 in range(HEADS // 2):
                    b = next_bank()
                    for e in range(2):
                        for k in range(KQ):
                            if m % TILES == 0:
                                w, used = arrived("w_uq", l * 3 + m // TILES, TILES * QH)
                            j = m % TILES
                            mn = mm(bank[0:QH, b, e * S:(e + 1) * S], w[:, j * QH:(j + 1) * QH],
                                    latent_n[:, k, :], k == 0, k == KQ - 1)
                            m += 1
                            ends = [used] if m % TILES == 0 else []
                            if e == 1 and k == KQ - 1:
                                mn.then_inc(*did("uq_raw", (l, p2), also=ends))
                            elif ends:
                                mn.then_inc(*did("chunk_used", (l, "uq", m), also=ends))
                    readers[b] = [("q_mla_scaled", (l, p2))]
                    held["uq_raw", (l, p2)] = b
                rr = slice(NOPE, QH)
                b = next_bank()
                pe.wait_ge(*of("rope_key", l))
                mm(bank[rr, b, 0:S], const("rot")[rr, :], rope_k[rr, :], True, True).then_inc(
                    *did("rot_raw", (l, -1)))
                readers[b] = [("rot_sin", (l, -1))]
                held["rot_raw", (l, -1)] = b
                for p2 in range(HEADS // 2):
                    b = next_bank()
                    pe.wait_ge(*of("q_mla_scaled", (l, p2)))
                    mm(bank[rr, b, :], const("rot")[rr, :], qh[rr, 2 * p2:2 * p2 + 2, :],
                       True, True).then_inc(*did("rot_raw", (l, p2)))
                    readers[b] = [("rot_sin", (l, p2))]
                    held["rot_raw", (l, p2)] = b

                def unit_scores(u):
                    kind, g, q = UNITS[u]
                    w = width(kind, q)
                    refill(2 * (u % 2), 2 * (u % 2) + 1)
                    if u == 0:
                        pe.wait_ge(*of("kcc", l))
                        for i in range(HPG):
                            pe.wait_ge(*of("q", (l, i)))
                        for i in range(2, 4):
                            pe.wait_ge(*of("kv_attn", (l, i)))
                    if kind == "mla":
                        pe.wait_ge(*of("k_mla", l))
                        for p2 in (2 * g, 2 * g + 1):
                            pe.wait_ge(*of("q_mla", (l, p2)))
                            pe.wait_ge(*of("k_nope", (l, p2)))
                    r = slice(DK * g, DK * g + DK)
                    for j in range(HPG):
                        o = bank[:, 2 * (u % 2) + j // 2, (j % 2) * S:(j % 2) * S + w]
                        qs = slice(q * P, (q + 1) * P)
                        if kind == "mla":
                            h = g * HPG + j
                            mn = mm(o, qh[0:QH, h, qs], kh[0:QH, h, 0:w], True, True)
                        elif kind == "cmp":
                            mn = mm(o, q_t[r, j, qs], kcc[r, 0:w], True, True)
                        else:
                            mn = mm(o, q_t[r, j, qs], kv_t[r, 2 if kind == "slc" else 3, 0:w],
                                    True, True)
                    mn.then_inc(*did("scores_raw", (l, u)))
                    readers[2 * (u % 2)] = readers[2 * (u % 2) + 1] = [("biased", (l, u))]

                def unit_transpose(u):
                    kind, g, q = UNITS[u]
                    w = width(kind, q)
                    refill(4, 5)
                    pe.wait_ge(*of("probs", (l, u)))
                    for j in range(HPG):
                        for k in range(-(-w // P)):
                            n = min(P, w - k * P)
                            c = (j % 2) * S + k * P
                            mn = nc.tensor.transpose(bank[0:n, 4 + j // 2, c:c + P],
                                                     scores[:, u % 2, j, k * P:k * P + n], ident)
                    mn.then_inc(*did("prob_t_raw", (l, u)))
                    readers[4] = [("prob_t_a", (l, u))]
                    readers[5] = [("prob_t_b", (l, u))]

                def unit_values(i):
                    kind, g, q, us = PV[i]
                    b = 6 + i % 2
                    refill(b)
                    if i == 0:
                        pe.wait_ge(*of("vcc", l))
                        for t in range(QT):
                            pe.wait_ge(*of("vsw", (l, t)))
                    for u in us:
                        pe.wait_ge(*of("prob_t_a", (l, u)))
                        pe.wait_ge(*of("prob_t_b", (l, u)))
                    for j in range(HPG):
                        parts = []
                        for u in us:
                            for k in range(q + 1 if UNITS[u][0] != "cmp" else 1):
                                v = {"cmp": vcc[0:NCMP, g * DK:(g + 1) * DK],
                                     "slc": vsw[:, k, g * DK:(g + 1) * DK],
                                     "win": vsw[:, k, P + g * DK:P + (g + 1) * DK],
                                     "mla": v_mla[:, k, (g * HPG + j) * DK:(g * HPG + j + 1) * DK],
                                     }[UNITS[u][0]]
                                n = NCMP if UNITS[u][0] == "cmp" else P
                                parts.append((v, prob_t[0:n, u % 4, j, k, :]))
                        for n, (v, p) in enumerate(parts):
                            mn = mm(bank[DK * g:DK * g + DK, b, j * P:(j + 1) * P], v, p,
                                    n == 0, n == len(parts) - 1)
                    mn.then_inc(*did("attn_raw", (l, i)))
                    readers[b] = [("attn_lower", (l, i))]

                def merge(m):
                    b = merge_bank(m)
                    refill(b)
                    project("w_in", l * 29 + 13 + m, xn_hl, ("merge_raw", (l, m)),
                            [("merge", (l, m))], b=b)

                for m in range(MERGES_FIRST):
                    merge(m)
                unit_scores(0)
                unit_scores(1)
                todo = []
                for u in range(NU):
                    if u + MERGES_FIRST < MERGE:
                        merge(u + MERGES_FIRST)
                    unit_transpose(u)
                    if u + 2 < NU:
                        unit_scores(u + 2)
                    if todo:
                        unit_values(todo.pop())
                    if u == PV[PV_OF[u]][3][-1]:
                        todo.append(PV_OF[u])
                unit_values(todo.pop())
                for c in range(4):
                    for name, x, first in (("w_a", oa_hl, 0), ("w_b", ob_hl, 4)):
                        w, *used = cut(name, l * 4 + c)
                        if c == 0:
                            for i in range(first, first + 4):
                                pe.wait_ge(*of("attn_lower", (l, i)))
                        for e in range(2):
                            f = 2 * c + e
                            b = next_bank()
                            for k in range(4):
                                j = e * 4 + k
                                mn = mm3(cols(b), w, j, [part[:, k, :] for part in x], k == 0, k == 3)
                            mn.then_inc(*did(name + "_raw", (l, f), also=used if e else []))
                            readers[b] = [(name + "_gated", (l, f))]
                            held[name + "_raw", (l, f)] = b
                down("w_out", l * KD, xn_hl, KD, "merged_lower", s, next_norm)

            ada_first()
            for k in range(KD):
                squares_sum(0, k, KD)
            for l in range(DEPTH):
                ffn(3 * l, l, "ffn1", 3 * l, 3 * l + 1)
                mix(l, 3 * l + 1, 3 * l + 1, 3 * l + 2)
                ffn(3 * l + 2, l, "ffn2", 3 * l + 2, 3 * l + 3)
            spread(6)
            for k in range(KD):
                squares_sum("mem", k, KD)
            spread("mem")
            for k in range(KD):
                squares_sum((0, 0), k, KD)

            def recurrent(i):
                spread((i, 0))
                project_all([("a_w_in", f, ("lru_in_raw", f), [("lru_in", f)])
                             for f in (*range(KD, 2 * KD), *range(KD))],
                            xn_hl, ("normed_lower", (i, 0)))
                for g in range(2):
                    for h in range(LRU_HEADS):
                        for e in range(2):
                            f = 2 * h + e
                            if f % 4 == 0:
                                w, *used = cut("a_gate_w", (g * KD + f) // 4)
                            b = next_bank()
                            for k in range(2):
                                if g == 0:
                                    pe.wait_ge(*of("conv_lower", 2 * h + k))
                                j = (f % 4) * 2 + k
                                mn = mm3(cols(b), w, j, [part[:, 2 * h + k, :] for part in conv_hl],
                                         k == 0, k == 1)
                            mn.then_inc(*did("lru_gate_raw", (g, f), also=used if f % 4 == 3 else []))
                            readers[b] = [("lru_gate", (g, f))]
                            held["lru_gate_raw", (g, f)] = b
                mem_keys(i)
                down("a_w_out", 0, lru_hl, KD, "lru_lower", (i, 0), (i, 1), "mixed_sq")

            def mem_keys(i):
                for f in range(KD):
                    w, used = arrived("c_w_kv", i * KD + f)
                    b = next_bank()
                    for k in range(KD):
                        if (i, f) == (0, 0):
                            pe.wait_ge(*of("normed2", ("mem", k)))
                        mn = mm(cols(b), w[:, k * P:(k + 1) * P], mem_n[:, k, :], k == 0, k == KD - 1)
                    mn.then_inc(*did("mem_k_raw", (i, f), also=[used]))
                    readers[b] = [("mem_k", (i, f))]
                    held["mem_k_raw", (i, f)] = b

            def mem_values(i):
                for e in range(2):
                    bs = [2 * e, 2 * e + 1]
                    refill(*bs)
                    for k in range(KD):
                        if k % 2 == 0:
                            w, used = arrived("c_w_v", (i * 2 + e) * KD // 2 + k // 2)
                        for t in range(QT):
                            mn = mm(cols(bs[t], 512), mem_n[:, k, t * P:(t + 1) * P],
                                    w[:, k % 2 * 512:(k % 2 + 1) * 512], k == 0, k == KD - 1)
                        if k == KD - 1:
                            mn.then_inc(*did("mem_v_raw", (i, e), also=[used]))
                        elif k % 2:
                            mn.then_inc(*did("chunk_used", (i, "v", e, k), also=[used]))
                    readers[bs[0]] = readers[bs[1]] = [("mem_v", (i, e))]
                    held["mem_v_raw", (i, e)] = bs[0]

            def cross(i):
                spread((i, 2))
                project_all([("c_w_q", i * KD + f, ("mem_q_raw", (i, f)), [("mem_q", (i, f))])
                             for f in range(KD)], xn_hl, ("normed_lower", (i, 2)))
                for k in range(KD):
                    pe.wait_ge(*of("mem_k", (i, k)))
                for q in range(QT):
                    refill(4 + 2 * q, 5 + 2 * q)
                    for h in range(MH):
                        for k in range(2):
                            pe.wait_ge(*of("mem_q", (i, 2 * h + k)))
                            mn = mm(bank[:, 4 + 2 * q + h // 2, (h % 2) * S:(h % 2 + 1) * S],
                                    q2[:, 2 * h + k, q * P:(q + 1) * P], k2[:, 2 * h + k, :],
                                    k == 0, k == 1)
                    mn.then_inc(*did("mem_scores_raw", (i, q)))
                    readers[4 + 2 * q] = readers[5 + 2 * q] = [("mem_exps", (i, q))]
                mem_values(i)
                for q in range(QT):
                    refill(4 + 2 * q, 5 + 2 * q)
                    pe.wait_ge(*of("mem_probs", (i, q)))
                    for h in range(MH):
                        for k in range(QT):
                            c = (h % 2) * S + k * P
                            mn = nc.tensor.transpose(bank[:, 4 + 2 * q + h // 2, c:c + P],
                                                     sc2[:, q, h, k * P:(k + 1) * P], ident)
                    mn.then_inc(*did("mem_prob_t_raw", (i, q)))
                    readers[4 + 2 * q] = [("mem_prob_t_a", (i, q))]
                    readers[5 + 2 * q] = [("mem_prob_t_b", (i, q))]
                for e in range(2):
                    pe.wait_ge(*of("mem_v", (i, e)))
                for q in range(QT):
                    refill(2 * q, 2 * q + 1)
                    pe.wait_ge(*of("mem_prob_t_a", (i, q)))
                    pe.wait_ge(*of("mem_prob_t_b", (i, q)))
                    for f in range(KD):
                        for k in range(QT):
                            mn = mm(bank[:, 2 * q + f // 4, (f % 4) * P:(f % 4 + 1) * P],
                                    v2[:, k, f * P:(f + 1) * P], pt2[:, q, f // 2, k, :],
                                    k == 0, k == QT - 1)
                    mn.then_inc(*did("mem_out_raw", (i, q)))
                    readers[2 * q] = readers[2 * q + 1] = [("mem_out_lower", (i, q))]
                for q in range(QT):
                    pe.wait_ge(*of("mem_out_lower", (i, q)))
                down("c_w_o", i * KD, o2_hl, KD, None, (i, 1), (i, 3), "mixed_sq")

            def mlp(i):
                spread((i, 4))
                project_all([("m_w_up", i * KF2 + f, ("relu_raw", (i, f)), [("relu", (i, f))])
                             for f in range(KF2)], xn_hl, ("normed_lower", (i, 4)))
                down("m_w_down", i * KF2, hid2_hl, KF2, "hidden2_lower", (i, 2), (i, 5), "mixed_sq")

            def head_sums(name, src, ready):
                refill(6)
                for k in range(KD):
                    pe.wait_ge(*of(ready, k))
                    for t in range(QT):
                        mn = mm(bank[:, 6, t * RH + 2 * k:t * RH + 2 * k + 2],
                                src[:, k, t * P:(t + 1) * P], const("head_of"), True, True)
                mn.then_inc(*did("head_sums", name))
                readers[6] = [("head_sums_read", name)]

            def head_spread(name, m):
                pe.wait_ge(*of("head_stat", name))
                for k in range(KD):
                    b = k // 2
                    if k % 2 == 0:
                        refill(b)
                    for t in range(QT):
                        c = t * RH + 2 * k
                        mn = mm(cols(b, P, (k % 2) * S + t * P), wide[name][:, c * RN:(c + 2) * RN], ident,
                                True, True)
                    if k % 2:
                        mn.then_inc(*did("head_spread", (name, b)))
                        readers[b] = [("head_used", (name, b))]

            def delta_mixer(i):
                spread((i, 0))
                for j in range(3):
                    project_all([("b_w_rkv", j * KD + f, ("rkv_raw", (j, f)), [("rkv", (j, f))])
                                 for f in range(KD)], xs_hl[j % 2], ("xs_lower", j))
                for j, wd in ((3, RN), (4, RN), (5, P)):
                    w, used = arrived("lora1", j - 3, KD * wd)
                    b = next_bank()
                    for k in range(KD):
                        pe.wait_ge(*of("xs", (j, k)))
                        mn = mm(bank[0:wd, b, 0:S], w[:, k * wd:(k + 1) * wd], xs_t[j % 2][:, k, :],
                                k == 0, k == KD - 1)
                    mn.then_inc(*did("rkv_raw", (j, KD - 1), also=[used]))
                    readers[b] = [("lora", j)]
                    held["rkv_raw", (j, KD - 1)] = b
                    w, used = arrived("lora2", j - 3)
                    pe.wait_ge(*of("lora", j))
                    for f in range(KD):
                        b = next_bank()
                        mm(cols(b), w[0:wd, f * P:(f + 1) * P], silu[0:wd, j % 2, :], True, True).then_inc(
                            *did("lora_raw", (j, f), also=[used] if f == KD - 1 else []))
                        readers[b] = [("lora_out", (j, f))]
                        held["lora_raw", (j, f)] = b
                head_sums("kk", bt, "kk_sq")
                head_spread("kk", 0)
                head_sums("bonus", rkr_t, "rkr")
                head_spread("bonus", 1)
                pe.wait_ge(*of("delta_in", 0))
                for c in range(NCH):
                    chunk(c)
                head_sums("mean", xn, "y_all")
                head_spread("mean", 2)
                head_sums("var", slot[3], "yc_sq")
                head_spread("var", 3)
                mem_keys(i)
                down("b_w_o", 0, xn_hl, KD, "delta_lower", (i, 0), (i, 1), "mixed_sq")

            def chunk(c):
                ts = slice(c * CH, (c + 1) * CH)
                half = [slice(0, RN), slice(RN, 2 * RN)]
                lo = half[0]
                for r in range(4):
                    refill(6, 7)
                    for p in range(2):
                        for e in range(2):
                            k = 2 * r + e
                            for m, src in enumerate((bt, kt_)):
                                mn = mm(bank[lo, 6 + p, e * 256 + m * P:e * 256 + (m + 1) * P],
                                        src[half[p], k, ts], ar[half[p], k, :, ts], True, True)
                        mn.then_inc(*did("mats_raw", (c, r, p)))
                        readers[6 + p] = [("mats", (c, r, p))]
                for m, src in enumerate((bt, kt_, v_t)):
                    for e in range(2):
                        b = 2 * m + e
                        refill(b)
                        for k in range(4):
                            mn = nc.tensor.transpose(bank[lo, b, k * P:(k + 1) * P],
                                                     src[:, 4 * e + k, ts], ident)
                        mn.then_inc(*did("tm_raw", (c, m, e)))
                        readers[b] = [("tm", (c, m, e))]
                for n in range(LEVELS):
                    for p in range(2):
                        refill(p)
                        pe.wait_ge(*of("level", (c, n, p)))
                        if n:
                            pe.wait_ge(*of("inv", (c, n - 1, p)))
                        for h in range(8):
                            hh = p * 8 + h
                            rhs = xi[:, hh, :] if n else ident[lo, 0:CH]
                            mn = mm(bank[lo, p, h * CH:(h + 1) * CH], mi[:, hh, :], rhs, True, True)
                        mn.then_inc(*did("y_raw", (c, n, p)))
                        readers[p] = [("y_inv", (c, n, p))] if n else [("inv", (c, n, p))]
                    if n == 0:
                        continue
                    for p in range(2):
                        pe.wait_ge(*of("y_inv", (c, n, p)))
                        refill(2 + p, 4 + p)
                        pe.wait_ge(*of("inv_t", (c, n - 1, p)))
                        if n < LEVELS - 1:
                            for h in range(8):
                                hh = p * 8 + h
                                mn = mm(bank[lo, 2 + p, h * CH:(h + 1) * CH], xit[:, hh, :], yi[:, hh, :],
                                        True, True)
                            mn.then_inc(*did("inv_raw", (c, n, p)))
                            readers[2 + p] = [("inv", (c, n, p))]
                        for h in range(8):
                            hh = p * 8 + h
                            mn = mm(bank[lo, 4 + p, h * CH:(h + 1) * CH], yi[:, hh, :], xit[:, hh, :],
                                    True, True)
                        mn.then_inc(*did("inv_t_raw", (c, n, p)))
                        readers[4 + p] = [("inv_t", (c, n, p))]
                refill(0, 1, 2, 3)
                pe.wait_ge(*of("state", c - 1))
                for p in range(2):
                    for k in range(KD):
                        mn = mm(bank[lo, p, k * CH:(k + 1) * CH], ar[half[p], k, 0, ts], state[half[p], k, :],
                                True, True)
                mn.then_inc(*did("q_state_raw", c))
                readers[0] = readers[1] = [("q_state", c)]
                for e in range(2):
                    pe.wait_ge(*of("tm", (c, 2, e)))
                for p in range(2):
                    for k in range(KD):
                        h = 2 * k + p
                        mn = mm(bank[lo, 2 + p, k * CH:(k + 1) * CH], mats[:, p * 8 + k, 2 * CH:3 * CH],
                                tm[:, 2, h * RN:(h + 1) * RN], True, True)
                mn.then_inc(*did("q_value_raw", c))
                readers[2] = readers[3] = [("q_sum", c)]
                refill(4, 5)
                pe.wait_ge(*of("q_sum", c))
                for p in range(2):
                    pe.wait_ge(*of("inv_t", (c, LEVELS - 1, p)))
                    for k in range(KD):
                        mn = mm(bank[lo, 4 + p, k * CH:(k + 1) * CH], xit[:, p * 8 + k, :],
                                mi[:, p * 8 + k, :], True, True)
                mn.then_inc(*did("sa_raw", c))
                readers[4] = readers[5] = [("sa", c)]
                refill(6, 7)
                for p in range(2):
                    for k in range(KD):
                        mn = mm(bank[half[p], 6 + p, k * CH:(k + 1) * CH], state[half[p], k, :],
                                ar[half[p], k, 1, ts], True, True)
                mn.then_inc(*did("y_state_raw", c))
                readers[6] = readers[7] = [("y_state", c)]
                pe.wait_ge(*of("sa", c))
                for m in range(2):
                    for e in range(2):
                        pe.wait_ge(*of("tm", (c, m, e)))
                refill(1)
                for p in range(2):
                    for k in range(KD):
                        h = 2 * k + p
                        o = bank[half[p], 1, k * RN:(k + 1) * RN]
                        mm(o, tm[:, 0, h * RN:(h + 1) * RN], yi[:, p * 8 + k, :], True, False)
                        mn = mm(o, tm[:, 1, h * RN:(h + 1) * RN], tm[:, 2, h * RN:(h + 1) * RN], False, True)
                mn.then_inc(*did("state_raw", c))
                readers[1] = [("state_sum", c)]
                refill(0)
                for p in range(2):
                    for k in range(KD):
                        h = 2 * k + p
                        o = bank[half[p], 0, k * CH:(k + 1) * CH]
                        mm(o, yi[:, p * 8 + k, :], mats[:, p * 8 + k, CH:2 * CH], True, False)
                        mn = mm(o, tm[:, 2, h * RN:(h + 1) * RN], mats[:, p * 8 + k, 3 * CH:4 * CH],
                                False, True)
                mn.then_inc(*did("y_chunk_raw", c))
                readers[0] = [("y", c)]

            for i in range(DEPTH):
                if i == 0:
                    recurrent(i)
                else:
                    delta_mixer(i)
                spread((i, 1))
                squares_of_two((i, 2))
                cross(i)
                spread((i, 3))
                squares_of_two((i, 4))
                mlp(i)
                spread((i, 5))
                if i + 1 < DEPTH:
                    squares_of_two((i + 1, 0))

        @block.vector
        def _(dve):
            led.taken, led.fixed = 0, False
            V = nc.vector

            worked = [0]

            def work_ahead(upto):
                led.fixed = True
                for n in range(worked[0], upto):
                    worked[0] = n + 1
                    if kinds[n] == "cut":
                        j = split_no[n]
                        dve.wait_ge(*of("weight_upper", j))
                        V.tensor_tensor(w_lo[:, n % RING, :], ring[:, n % RING, :],
                                        w_hi[:, j % SPLITS, :].bitcast(F32), ALU.subtract).then_inc(
                            *did("weight_lower", j))
                    elif kinds[n] == "ada":
                        i = order[n][1]
                        dve.wait_ge(*of("ada_product", i))
                        m = beside_no[i]
                        if m >= 8:
                            dve.wait_ge(*of("ada_raw", beside[m - 8]))
                        w = ring[:, n % RING, :].rearrange("p (k c) -> p c k", k=KD)
                        V.tensor_reduce(ada_part[:, m % 8, :], w, AX.X, ALU.add).then_inc(
                            *did("ada_part", i, also=[("weights_used", n)]))
                led.fixed = False

            def due(name, key):
                event = of(name, key)
                work_ahead(ahead(led.taken))
                return event

            def lower(dst, k, src, upper, done, also=()):
                dve.wait_ge(*due(*upper))
                V.tensor_tensor(dst[1][:, k, :], src, dst[0][:, k, :].bitcast(F32), ALU.subtract
                                ).then_inc(*did(*done, also=also))

            def mod_sum(part):
                a, b, bk = ADA_PARTS[part]
                dve.wait_ge(*due("ada_raw", b - 1))
                if part == 0:
                    dve.wait_ge(*due("vecs_in", 0))
                V.tensor_tensor(mod[:, a:b], bank[:, bk, 0:b - a], vec("b_ada", a, b - a),
                                ALU.add).then_inc(*did("mod_sum", part))
                dve.wait_ge(*due("mod_sum", part))
                segs = [i for i in range(a // KD, b // KD) if i % NMOD % 3 == 1 or i % NMOD in (2, 8)]
                for seg in segs:
                    m = mod[:, seg * KD:(seg + 1) * KD]
                    one = seg % NMOD % 3 == 1
                    V.tensor_scalar(m, m, 1.0 if one else 0.5, None, ALU.add if one else ALU.mult).then_inc(
                        *did("mod_step", seg, also=[("mod", part)] if seg == segs[-1] else []))

            def rstd(n, cnt=D):
                dve.wait_ge(*due("square_sums", n))
                for t in range(QT):
                    last = V.tensor_scalar(root[:, 0, t:t + 1], bank[:, 4 + t, 0:1], 1.0 / cnt, EPS,
                                           ALU.mult, ALU.add)
                    last.then_inc(*did("mean", (n, t), also=[("mean_square", n)] if t else []))
                dve.wait_ge(*due("root", n))
                V.reciprocal(root[:, 2, 0:2], root[:, 1, 0:2]).then_inc(*did("rroot", n))
                dve.wait_ge(*due("rroot", n))
                for t in range(QT):
                    V.tensor_scalar(diag[:, t, :], ident, root[:, 2, t:t + 1], None,
                                    ALU.mult).then_inc(*did("diag", (n, t), also=[("rstd_diag", n)] if t else []))

            def normalise(n, out_t, gain, event, ready=None):
                dve.wait_ge(*due("rstd", n))
                for k in range(KD + LAG):
                    if k < KD:
                        V.scalar_tensor_tensor(out_t[:, k, :], X[:, k, :], gain(k), cols(4), ALU.mult,
                                               ALU.mult).then_inc(
                            *did(event, (n, k), also=[("rstd_read", n)] if k == KD - 1 else []))
                    if k >= LAG and event == "scaled":
                        lower(xn_hl, k - LAG, xn[:, k - LAG, :], ("normed_upper", (n, k - LAG)),
                              ("normed_lower", (n, k - LAG)))

            def squares_add(n, k):
                src = sq if isinstance(n, int) else t_sq
                dve.wait_ge(*due("squares", (n, k)))
                if k > 1:
                    dve.wait_ge(*due("squares_added", (n, k - 1)))
                V.tensor_tensor(src[:, 0, :], src[:, 0, :], src[:, k, :], ALU.add).then_inc(
                    *did("squares_added", (n, k)))

            def residual(s, gain, n):
                for f in range(KD):
                    dve.wait_ge(*due("down_raw", (s, f)))
                    b = held["down_raw", (s, f)]
                    V.scalar_tensor_tensor(X[:, f, :], cols(b), gain(f), X[:, f, :], ALU.mult,
                                           ALU.add).then_inc(*did("residual", (s, f)))
                    if f >= 2:
                        squares_add(n, f - 1)

            def ffn(s, l, which, norm):
                for f in range(KF + 1):
                    if f < KF:
                        dve.wait_ge(*due("silu", (s, f)))
                        dve.wait_ge(*due("up_raw", (s, f)))
                        V.tensor_tensor(silu[:, f % 2, :], silu[:, f % 2, :],
                                        cols(held["up_raw", (s, f)]), ALU.mult).then_inc(
                            *did("hidden", (s, f)))
                    if f:
                        lower(hid_hl, f - 1, silu[:, (f - 1) % 2, :], ("hidden_upper", (s, f - 1)),
                              ("hidden_lower", (s, f - 1)))

            def mix(l, s, norm):
                for i in range(2):
                    dve.wait_ge(*due("in_raw", (l, 5 + i)))
                    V.tensor_copy(kv_t[:, i, :], cols(held["in_raw", (l, 5 + i)])).then_inc(*did("kv", (l, i)))
                for v in range(2):
                    dve.wait_ge(*due("kv", (l, v)))
                    x = kv_t[:, v, :].rearrange("p (n i) -> p i n", i=CMP_STRIDE)
                    for c in range(2):
                        a = c * CMP_STRIDE
                        pe_ = vec("pe", (l * 2 + v) * CMP_BLOCK + a, CMP_STRIDE)
                        V.tensor_tensor(blocks_pe[:, v, a:a + CMP_STRIDE, :], x[:, :, c:c + NCMP],
                                        bcast(pe_, NCMP), ALU.add).then_inc(
                            *did("blocks", (l, v, c), also=[("blocks_pe", (l, v))] if c else []))
                n = ("m", l)
                dve.wait_ge(*due("square_sums", n))
                for t in range(QT):
                    for c, cnt in enumerate((QRANK, KVRANK)):
                        last = V.tensor_scalar(root[:, 0, 2 * c + t:2 * c + t + 1],
                                               bank[:, 4 + t, c:c + 1], 1.0 / cnt, EPS, ALU.mult, ALU.add)
                        last.then_inc(*did("mean", (n, t, c), also=[("mean_square", n)] if t + c == 2 else []))
                dve.wait_ge(*due("root", n))
                V.reciprocal(root[:, 2, :], root[:, 1, :]).then_inc(*did("rroot", n))
                dve.wait_ge(*due("rroot", n))
                for c in range(4):
                    V.tensor_scalar(diag[:, c, :], ident, root[:, 2, c:c + 1], None, ALU.mult).then_inc(
                        *did("diag", (n, c), also=[("rstd_diag", n)] if c == 3 else []))
                dve.wait_ge(*due("rstd", n))
                for i in list(range(KQ, KQ + KKV)) + list(range(KQ)):
                    dve.wait_ge(*due("latent", (l, i)))
                    q = i < KQ
                    gain = vec("mla_q_norm", l * KQ + i) if q else vec("mla_kv_norm", l * KKV + i - KQ)
                    V.scalar_tensor_tensor(latent_n[:, i, :], latent[:, i, :], gain,
                                           cols(4, S, 0 if q else S), ALU.mult, ALU.mult).then_inc(
                        *did("latent_n", (l, i), also=[("rstd_read", n)] if i == KQ - 1 else []))
                dve.wait_ge(*due("gate_exp", (l, 1)))
                V.tensor_scalar(gates[:, :, :], gates[:, :, :], 1.0, None, ALU.add).then_inc(*did("gate_den", l))
                dve.wait_ge(*due("gate_den", l))
                V.reciprocal(gates[:, :, :], gates[:, :, :]).then_inc(*did("gates", l))
                for t in range(QT):
                    dve.wait_ge(*due("uv_raw", (l, t)))
                    V.tensor_copy(v_mla[:, t, :], cols(held["uv_raw", (l, t)], 512)).then_inc(*did("v_mla", (l, t)))
                dve.wait_ge(*due("cmp_out_raw", l))
                V.tensor_copy(kcc[:, 0:NCMP], bank[:, 5, 0:NCMP]).then_inc(*did("kcc", l))
                V.tensor_copy(vcc[0:NCMP, :], bank[0:NCMP, 5, DK:3 * DK]).then_inc(*did("vcc", l))
                rr = slice(NOPE, QH)
                if l == 0:
                    dve.wait_ge(*due("attn_consts_in", 0))
                for p2 in range(-1, HEADS // 2):
                    w = 1 if p2 < 0 else 2
                    dve.wait_ge(*due("rot_raw", (l, p2)))
                    if p2 >= 0:
                        dve.wait_ge(*due("roped", (l, p2 - 1)))
                    tmp = rope_tmp[rr, 0:w * S].rearrange("p (h t) -> p h t", t=S)
                    V.tensor_tensor(tmp, bank[rr, held["rot_raw", (l, p2)], 0:w * S].rearrange("p (h t) -> p h t", t=S),
                                    bcast_mid(const("sin")[rr, :], w), ALU.mult).then_inc(*did("rot_sin", (l, p2)))
                    dve.wait_ge(*due("rot_sin", (l, p2)))
                    dve.wait_ge(*due("rope_cos", (l, p2)))
                    x = rope_k[rr, :].rearrange("p (h t) -> p h t", h=1) if p2 < 0 else qh[rr, 2 * p2:2 * p2 + 2, :]
                    V.tensor_tensor(x, x, tmp, ALU.add).then_inc(
                        *did("roped", (l, p2), also=[("rope_k", l)] if p2 < 0 else [("q_mla", (l, p2))]))

                def front(u):
                    kind, g, q = UNITS[u]
                    w = width(kind, q)
                    dve.wait_ge(*due("scores_raw", (l, u)))
                    if u >= 2:
                        dve.wait_ge(*due("prob_t_raw", (l, u - 2)))
                    ps = bank[:, 2 * (u % 2):2 * (u % 2) + 2, :].rearrange("p b (j k) -> p (b j) k", k=S)[:, :, 0:w]
                    if kind == "mla":
                        bias = bcast_mid(const(f"causal{q}"), HPG)
                    else:
                        name = ("cmp" if kind == "cmp" else "alibi") + str(q)
                        bias = const(name).rearrange("p (h k) -> p h k", k=w)[:, g * HPG:(g + 1) * HPG, :]
                    s_ = scores[:, u % 2, :, 0:w]
                    V.tensor_tensor(s_, ps, bias, ALU.add).then_inc(*did("biased", (l, u)))
                    dve.wait_ge(*due("biased", (l, u)))
                    V.tensor_reduce(nmax[:, u % 2, :], s_, AX.X, ALU.max, negate=True).then_inc(
                        *did("row_max", (l, u)))
                    dve.wait_ge(*due("row_max", (l, u)))
                    V.tensor_scalar(nmax[:, u % 2, :], nmax[:, u % 2, :], MAX_CLAMP, None, ALU.min).then_inc(
                        *did("neg_max", (l, u)))

                def scale(u):
                    kind, g, q = UNITS[u]
                    dve.wait_ge(*due("exps", (l, u)))
                    d = den[:, u % 2, :]
                    V.tensor_scalar(d, d, 1.0, None, ALU.max).then_inc(*did("den", (l, u)))
                    dve.wait_ge(*due("den", (l, u)))
                    V.reciprocal(d, d).then_inc(*did("rden", (l, u), also=[("prob_scale", (l, u))] if kind == "mla" else []))
                    if kind != "mla":
                        dve.wait_ge(*due("rden", (l, u)))
                        br = ("cmp", "slc", "win").index(kind)
                        gt = gates[:, q, :].rearrange("p (h b) -> p h b", b=3)[:, g * HPG:(g + 1) * HPG, br]
                        V.tensor_tensor(d, d, gt, ALU.mult).then_inc(*did("gden", (l, u), also=[("prob_scale", (l, u))]))

                def back(u):
                    kind, g, q = UNITS[u]
                    w = width(kind, q)
                    n, kk = (NCMP, 1) if kind == "cmp" else (P, q + 1)
                    dve.wait_ge(*due("prob_t_raw", (l, u)))
                    if u >= 4:
                        dve.wait_ge(*due("attn_raw", (l, PV_OF[u - 4])))
                    V.tensor_copy(prob_t[0:n, u % 4, 2:4, 0:kk, :],
                                  bank[0:n, 5, :].rearrange("p (j k q) -> p j k q", j=2, k=2)[:, :, 0:kk, :]
                                  ).then_inc(*did("prob_t_b", (l, u)))

                def out_lower(i):
                    kind, g, q, us = PV[i]
                    dve.wait_ge(*due("attn_upper", (l, i)))
                    hi, lo = oa_hl if kind == "a" else ob_hl
                    r, qs = slice(DK * g, DK * g + DK), slice(q * P, (q + 1) * P)
                    V.tensor_tensor(lo[r, :, qs], bank[r, 6 + i % 2, :].rearrange("p (j q) -> p j q", j=HPG),
                                    hi[r, :, qs].bitcast(F32), ALU.subtract).then_inc(
                        *did("attn_lower", (l, i)))

                front(0)
                front(1)
                scale(0)
                todo = []
                for u in range(NU):
                    if u + 1 < NU:
                        scale(u + 1)
                    back(u)
                    if u + 2 < NU:
                        front(u + 2)
                    if todo:
                        out_lower(todo.pop())
                    if u == PV[PV_OF[u]][3][-1]:
                        todo.append(PV_OF[u])
                out_lower(todo.pop())
                for c in range(4):
                    for name in ("w_a", "w_b"):
                        for e in range(2):
                            f = 2 * c + e
                            dve.wait_ge(*due(name + "_raw", (l, f)))
                            if f == 0:
                                dve.wait_ge(*due("merge_gate", (l, 0 if name == "w_a" else 1)))
                            if name == "w_a":
                                if f >= 2:
                                    dve.wait_ge(*due("merged", (s, f - 2)))
                                V.tensor_tensor(silu[:, e, :], gm[:, f, :], cols(held[name + "_raw", (l, f)]), ALU.mult
                                                ).then_inc(*did("w_a_gated", (l, f)))
                            else:
                                V.tensor_tensor(xn[:, f, :], gm[:, KD + f, :], cols(held[name + "_raw", (l, f)]), ALU.mult
                                                ).then_inc(*did("w_b_gated", (l, f)))
                                dve.wait_ge(*due("w_b_gated", (l, f)))
                                V.tensor_tensor(xn[:, f, :], xn[:, f, :], silu[:, e, :], ALU.add).then_inc(
                                    *did("merged", (s, f)))
                                if f:
                                    lower(xn_hl, f - 1, xn[:, f - 1, :], ("merged_upper", (s, f - 1)),
                                          ("merged_lower", (s, f - 1)))
                lower(xn_hl, KD - 1, xn[:, KD - 1, :], ("merged_upper", (s, KD - 1)),
                      ("merged_lower", (s, KD - 1)))

            mod_sum(0)
            rstd(0)
            for l in range(DEPTH):
                for s3 in range(3):
                    n = 3 * l + s3
                    if n == 0:
                        dve.wait_ge(*due("mod", 0))
                    normalise(n, xn, lambda k: mods(l, 3 * s3 + 1, k), "scaled")
                    if s3 == 1:
                        mix(l, n, n)
                    else:
                        ffn(n, l, "", n)
                    parts = ADA_AT.get(n, ())
                    if len(parts) == 2:
                        mod_sum(parts[0])
                        dve.wait_ge(*due("mod", parts[0]))
                    residual(n, lambda f: mods(l, 3 * s3 + 2, f), n + 1)
                    rstd(n + 1)
                    for part in parts[-1:]:
                        mod_sum(part)
                        dve.wait_ge(*due("mod", part))
            normalise(6, X, lambda k: vec("final_norm", k), "x_second")
            rstd("mem")

            def gained(n, src, dst, gain, parts):
                dve.wait_ge(*due("rstd", n))
                for k in range(KD + LAG):
                    if k < KD:
                        V.scalar_tensor_tensor(dst[:, k, :], src[:, k, :], gain(k), cols(4), ALU.mult,
                                               ALU.mult).then_inc(
                            *did("normed2", (n, k), also=[("rstd_read", n)] if k == KD - 1 else []))
                    if k >= LAG and parts:
                        lower(xn_hl, k - LAG, xn[:, k - LAG, :], ("normed_upper", (n, k - LAG)),
                              ("normed_lower", (n, k - LAG)))

            def added(n, gain, event="x_added"):
                dve.wait_ge(*due("rstd", n))
                for k in range(KD):
                    V.scalar_tensor_tensor(t_out[:, k, :], t_out[:, k, :], gain(k), cols(4), ALU.mult,
                                           ALU.mult).then_inc(
                        *did("mixed_n", (n, k), also=[("rstd_read", n)] if k == KD - 1 else []))
                for k in range(KD):
                    dve.wait_ge(*due("mixed_n", (n, k)))
                    V.tensor_tensor(X[:, k, :], X[:, k, :], t_out[:, k, :], ALU.add).then_inc(
                        *did(event, (n, k)))

            def ln(i, j):
                return lambda k: vec("ln", (i * 6 + j) * KD + k)

            link = [0]

            def step(ins, also=()):
                link[0] += 1
                ins.then_inc(*did("dve_chain", link[0], also=also))
                dve.wait_ge(*due("dve_chain", link[0]))

            def recurrent(i):
                lv = vec("lam", 0, KD)
                step(V.tensor_scalar(lam[:, 0, :], lv, -1.0, None, ALU.mult))
                step(V.tensor_tensor(lam[:, 1, :], lv, lam[:, 0, :], ALU.max), [("lam_abs", 0)])
                step(V.tensor_scalar(lam[:, 0, :], lam[:, 0, :], 0.0, None, ALU.max))
                dve.wait_ge(*due("lam_ln", 0))
                step(V.tensor_tensor(lam[:, 0, :], lam[:, 0, :], lam[:, 2, :], ALU.add))
                step(V.tensor_scalar(lam[:, 2, :], lam[:, 0, :], 8.0, None, ALU.mult))
                step(V.tensor_scalar(lam[:, 3, :], lam[:, 0, :], -8.0, None, ALU.mult), [("lam", 0)])
                step(V.memset(u_pad[:, :, 0:CONV - 1], 0.0))
                for k in range(KD):
                    dve.wait_ge(*due("lru_in", KD + k))
                    step(V.tensor_scalar(conv[:, k, :], u_pad[:, k, 0:S], vec("conv_w", k),
                                         vec("conv_b", k), ALU.mult, ALU.add))
                    for tap in range(1, CONV):
                        step(V.scalar_tensor_tensor(conv[:, k, :], u_pad[:, k, tap:tap + S],
                                                    vec("conv_w", tap * KD + k), conv[:, k, :],
                                                    ALU.mult, ALU.add),
                             [("conv", k)] if tap == CONV - 1 else [])
                    for done in [k - 1] * (k > 0) + [k] * (k == KD - 1):
                        lower(conv_hl, done, conv[:, done, :], ("conv_upper", done), ("conv_lower", done))
                for k in range(KD):
                    dve.wait_ge(*due("lru_gate", (1, k)))
                    V.tensor_tensor(ig[:, k, :], ig[:, k, :], conv[:, k, :], ALU.mult).then_inc(
                        *did("i_conv", k))
                for k in range(KD):
                    dve.wait_ge(*due("lru_tanh", k))
                    step(V.tensor_tensor(lru_b[:, k, :], decay[:, k, :], decay[:, k, :], ALU.mult))
                    step(V.scalar_tensor_tensor(lru_b[:, k, :], lru_b[:, k, :], 1.0, th[:, k, :],
                                                ALU.add, ALU.mult), [("lru_mult_sq", k)])
                for k in range(KD):
                    dve.wait_ge(*due("lru_mult", k))
                    step(V.tensor_tensor(lru_b[:, k, :], lru_b[:, k, :], ig[:, k, :], ALU.mult))
                    step(V.tensor_tensor_scan(lru_h[:, k, :], decay[:, k, :], lru_b[:, k, :], 0.0,
                                              ALU.mult, ALU.add))
                    V.tensor_tensor(lru_h[:, k, :], lru_h[:, k, :], y_br[:, k, :], ALU.mult).then_inc(
                        *did("lru_gated", k))
                    for done in [k - 1] * (k > 0) + [k] * (k == KD - 1):
                        lower(lru_hl, done, lru_h[:, done, :], ("lru_upper", done),
                              ("lru_lower", ((i, 0), done)))

            def cross(i):
                for q in range(QT):
                    dve.wait_ge(*due("mem_scores_raw", (i, q)))
                    ps = bank[:, 4 + 2 * q:6 + 2 * q, :].rearrange("p b (j k) -> p (b j) k", k=S)
                    V.tensor_reduce(nmax[:, q, :], ps, AX.X, ALU.max, negate=True).then_inc(
                        *did("mem_neg_max", (i, q)))
                for q in range(QT):
                    dve.wait_ge(*due("mem_exps", (i, q)))
                    V.reciprocal(den[:, q, :], den[:, q, :]).then_inc(*did("mem_rden", (i, q)))
                for q in range(QT):
                    dve.wait_ge(*due("mem_prob_t_raw", (i, q)))
                    V.tensor_copy(pt2[:, q, 2:4, :, :],
                                  bank[:, 5 + 2 * q, :].rearrange("p (j k q) -> p j k q", j=2, k=2)).then_inc(
                        *did("mem_prob_t_b", (i, q)))
                for q in range(QT):
                    dve.wait_ge(*due("mem_out_upper", (i, q)))
                    qs = slice(q * P, (q + 1) * P)
                    V.tensor_tensor(o2_hl[1][:, :, qs],
                                    bank[:, 2 * q:2 * q + 2, :].rearrange("p b (f q) -> p (b f) q", f=4),
                                    o2_hl[0][:, :, qs].bitcast(F32), ALU.subtract).then_inc(
                        *did("mem_out_lower", (i, q)))

            def mlp(i):
                for f in range(KF2 + 1):
                    if f < KF2:
                        dve.wait_ge(*due("relu", (i, f)))
                        V.tensor_tensor(silu[:, f % 2, :], silu[:, f % 2, :], silu[:, f % 2, :],
                                        ALU.mult).then_inc(*did("hidden2", (i, f)))
                    if f:
                        lower(hid2_hl, f - 1, silu[:, (f - 1) % 2, :], ("hidden2_upper", (i, f - 1)),
                              ("hidden2_lower", ((i, 2), f - 1)))

            def pair(b):
                return slice(2 * b, 2 * b + 2), bank[:, b, :].rearrange("p (k t) -> p k t", k=2)

            def widen(name, m):
                w = wide[name].rearrange("p (h n) -> p h n", n=RN)
                step(V.tensor_copy(w, bcast(stat[:, m, :], RN)), [("head_stat", name)])

            def delta_mixer(i):
                xx = slot[10]
                for k in range(KD):
                    dve.wait_ge(*due("normed2", ((i, 0), k)))
                    V.tensor_tensor(xx[:, k, 1:S], xn[:, k, 0:S - 1], xn[:, k, 1:S], ALU.subtract).then_inc(
                        *did("xx_rest", k))
                    V.tensor_scalar(xx[:, k, 0:1], xn[:, k, 0:1], -1.0, None, ALU.mult).then_inc(
                        *did("xx", k))
                for j, mu in enumerate((0, 2, 3, 1, 4, 5)):
                    if j >= 2:
                        dve.wait_ge(*due("rkv_raw", (j - 2, KD - 1)))
                    for k in range(KD):
                        dve.wait_ge(*due("xx", k))
                        V.scalar_tensor_tensor(xs_t[j % 2][:, k, :], xx[:, k, :], vec("mu", mu * KD + k),
                                               xn[:, k, :], ALU.mult, ALU.add).then_inc(*did("xs", (j, k)))
                        for done in [k - 1] * (k > 0) + [k] * (k == KD - 1) if j < 3 else []:
                            lower(xs_hl[j % 2], done, xs_t[j % 2][:, done, :], ("xs_upper", (j, done)),
                                  ("xs_lower", (j, done)))
                dve.wait_ge(*due("rkv_raw", (5, KD - 1)))
                for k in range(KD):
                    dve.wait_ge(*due("rkv", (1, k)))
                    V.tensor_scalar(kk_t[:, k, :], k_t[:, k, :], vec("k_k", k), None, ALU.mult).then_inc(
                        *did("kk", k))
                for k in range(KD):
                    dve.wait_ge(*due("lora_out", (4, k)))
                    step(V.tensor_scalar(kt_[:, k, :], aa_t[:, k, :], 1.0, vec("k_a", k), ALU.subtract,
                                         ALU.mult))
                    step(V.scalar_tensor_tensor(k_t[:, k, :], kt_[:, k, :], 1.0, k_t[:, k, :], ALU.add,
                                                ALU.mult))
                dve.wait_ge(*due("head_root", "kk"))
                step(V.tensor_scalar(stat[:, 0, :], stat[:, 0, :], 1e-12, None, ALU.max))
                step(V.reciprocal(stat[:, 0, :], stat[:, 0, :]))
                widen("kk", 0)
                dve.wait_ge(*due("delta_consts_in", 0))
                for k in range(KD):
                    dve.wait_ge(*due("lora_out", (3, k)))
                    V.tensor_tensor_scan(xn[:, k, :], const("within"), sg_t[:, k, :], 0.0, ALU.mult,
                                         ALU.add).then_inc(*did("decay_sum", k))
                dve.wait_ge(*due("decay_sum", KD - 1))
                step(V.tensor_tensor(sg_t, xn[:, :, :], sg_t, ALU.subtract), [("before_sum", 0)])
                for b in range(4):
                    dve.wait_ge(*due("head_spread", ("kk", b)))
                    ks, ps = pair(b)
                    V.tensor_tensor(kk_t[:, ks, :], kk_t[:, ks, :], ps, ALU.mult).then_inc(
                        *did("head_used", ("kk", b)))
                for k in range(KD):
                    dve.wait_ge(*due("rkv", (0, k)))
                    V.scalar_tensor_tensor(rkr_t[:, k, :], r_t[:, k, :], vec("r_k", k), k_t[:, k, :],
                                           ALU.mult, ALU.mult).then_inc(*did("rkr", k))
                dve.wait_ge(*due("head_used", ("kk", 3)))
                step(V.tensor_tensor(aa_t, kk_t, aa_t, ALU.mult))
                dve.wait_ge(*due("exp_minus", 0))
                step(V.tensor_tensor(bt, aa_t, kt_, ALU.mult), [("b_scaled", 0)])
                dve.wait_ge(*due("head_sums", "bonus"))
                step(V.tensor_copy(stat[:, 1, :], bank[:, 6, 0:QT * RH]), [("head_sums_read", "bonus")])
                widen("bonus", 1)
                for b in range(4):
                    dve.wait_ge(*due("head_spread", ("bonus", b)))
                    ks, ps = pair(b)
                    V.tensor_tensor(bonus[:, ks, :], v_t[:, ks, :], ps, ALU.mult).then_inc(
                        *did("head_used", ("bonus", b)))
                dve.wait_ge(*due("exp_plus", 0))
                step(V.tensor_tensor(ar[:, :, 1, :], r_t, exp_plus, ALU.mult))
                step(V.tensor_copy(w_end[:, :, :],
                                   exp_plus.rearrange("p k (c t) -> p k c t", t=CH)[:, :, :, CH - 1]))
                dve.wait_ge(*due("k_scaled", 0))
                step(V.scalar_tensor_tensor(ar[:, :, 0, :], kk_t, -1.0, sg_t, ALU.mult, ALU.mult),
                     [("delta_in", 0)])
                step(V.memset(state, 0.0), [("state", -1)])
                for c in range(NCH):
                    chunk(c)
                def used(name, m, out_t, src, op):
                    for b in range(4):
                        dve.wait_ge(*due("head_spread", (name, b)))
                        ks, ps = pair(b)
                        V.tensor_tensor(out_t[:, ks, :], src[:, ks, :], ps, op).then_inc(
                            *did("head_used", (name, b)))

                dve.wait_ge(*due("head_sums", "mean"))
                step(V.tensor_scalar(stat[:, 2, :], bank[:, 6, 0:QT * RH], 1.0 / RN, None, ALU.mult),
                     [("head_sums_read", "mean")])
                widen("mean", 2)
                used("mean", 2, xn, xn, ALU.subtract)
                dve.wait_ge(*due("head_sums", "var"))
                step(V.tensor_scalar(stat[:, 3, :], bank[:, 6, 0:QT * RH], 1.0 / RN, GN_EPS, ALU.mult, ALU.add),
                     [("head_var", 0), ("head_sums_read", "var")])
                dve.wait_ge(*due("head_root", "var"))
                step(V.reciprocal(stat[:, 3, :], stat[:, 3, :]))
                widen("var", 3)
                used("var", 3, xn, xn, ALU.mult)
                for k in range(KD):
                    if k % 2 == 0:
                        dve.wait_ge(*due("head_used", ("var", k // 2)))
                    step(V.scalar_tensor_tensor(xn[:, k, :], xn[:, k, :], vec("gn_g", k), bonus[:, k, :],
                                                ALU.mult, ALU.add))
                    V.scalar_tensor_tensor(xn[:, k, :], xn[:, k, :], vec("gn_b", k), g_t[:, k, :],
                                           ALU.add, ALU.mult).then_inc(*did("delta_out", k))
                    for done in [k - 1] * (k > 0) + [k] * (k == KD - 1):
                        lower(xn_hl, done, xn[:, done, :], ("delta_upper", done),
                              ("delta_lower", ((i, 0), done)))

            def chunk(c):
                lo = slice(0, CH)
                ts = slice(c * CH, (c + 1) * CH)
                for r in range(4):
                    for p in range(2):
                        dve.wait_ge(*due("mats_raw", (c, r, p)))
                        V.tensor_tensor(mats[:, p * 8 + 2 * r:p * 8 + 2 * r + 2, :],
                                        bank[lo, 6 + p, :].rearrange("p (h w) -> p h w", h=2),
                                        bcast_mid(const("earlier")[lo, :], 2), ALU.mult).then_inc(
                            *did("mats", (c, r, p)))
                eye = bcast_mid(ident[lo, 0:CH], 8)
                for n in range(LEVELS):
                    for p in range(2):
                        hs = slice(p * 8, p * 8 + 8)
                        if n == 0:
                            dve.wait_ge(*due("level", (c, 0, p)))
                            V.tensor_tensor(xit[:, hs, :], mi[:, hs, :], eye, ALU.add).then_inc(
                                *did("inv_t", (c, 0, p)))
                            dve.wait_ge(*due("y_raw", (c, 0, p)))
                            V.tensor_tensor(xi[:, hs, :], bank[lo, p, :].rearrange("p (h t) -> p h t", h=8),
                                            eye, ALU.add).then_inc(*did("inv", (c, 0, p)))
                            continue
                        if n < LEVELS - 1:
                            dve.wait_ge(*due("inv_raw", (c, n, p)))
                            V.tensor_tensor(xi[:, hs, :], bank[lo, 2 + p, :].rearrange("p (h t) -> p h t", h=8),
                                            xi[:, hs, :], ALU.add).then_inc(*did("inv", (c, n, p)))
                        dve.wait_ge(*due("inv_t_raw", (c, n, p)))
                        V.tensor_tensor(xit[:, hs, :], bank[lo, 4 + p, :].rearrange("p (h t) -> p h t", h=8),
                                        xit[:, hs, :], ALU.add).then_inc(*did("inv_t", (c, n, p)))
                dve.wait_ge(*due("q_value_raw", c))
                dve.wait_ge(*due("q_state", c))
                V.tensor_tensor(mi, bank[lo, 2:4, :].rearrange("p b (k t) -> p (b k) t", t=CH), mi,
                                ALU.add).then_inc(*did("q_sum", c))
                dve.wait_ge(*due("state_raw", c))
                ps = bank[:, 1, :].rearrange("p (k i) -> p k i", k=KD)
                step(V.tensor_tensor(state, ps, state, ALU.add), [("state_sum", c)])
                step(V.tensor_tensor(state, state, bcast(w_end[:, :, c], RN), ALU.mult), [("state", c)])
                dve.wait_ge(*due("y_chunk_raw", c))
                dve.wait_ge(*due("y_state", c))
                ps = bank[:, 0, :].rearrange("p (k t) -> p k t", k=KD)
                last = c == NCH - 1
                step(V.tensor_tensor(xn[:, :, ts], ps, xn[:, :, ts], ALU.add),
                     [("y", c)] + [("y_all", k) for k in range(KD)] * last)

            gained("mem", slot[10], mem_n, lambda k: vec("mem_norm", k), False)
            rstd((0, 0))
            for i in range(DEPTH):
                gained((i, 0), X, xn, ln(i, 0), i == 0)
                if i == 0:
                    recurrent(i)
                else:
                    delta_mixer(i)
                for k in range(1, KD - 1):
                    squares_add((i, 1), k)
                rstd((i, 1))
                added((i, 1), ln(i, 1))
                for k in range(1, KD - 1):
                    squares_add((i, 2), k)
                rstd((i, 2))
                gained((i, 2), X, xn, ln(i, 2), True)
                cross(i)
                for k in range(1, KD - 1):
                    squares_add((i, 3), k)
                rstd((i, 3))
                added((i, 3), ln(i, 3))
                for k in range(1, KD - 1):
                    squares_add((i, 4), k)
                rstd((i, 4))
                gained((i, 4), X, xn, ln(i, 4), True)
                mlp(i)
                for k in range(1, KD - 1):
                    squares_add((i, 5), k)
                rstd((i, 5))
                added((i, 5), ln(i, 5), "x_added" if i + 1 < DEPTH else "x_final")
                if i + 1 < DEPTH:
                    for k in range(1, KD - 1):
                        squares_add((i + 1, 0), k)
                    rstd((i + 1, 0))
            work_ahead(len(kinds))

        @block.scalar
        def _(act):
            led.taken = 0
            A = nc.scalar
            worked = [0]

            def work_ahead(upto):
                led.fixed = True
                for n in range(worked[0], upto):
                    worked[0] = n + 1
                    if kinds[n] == "cut":
                        j = split_no[n]
                        act.wait_ge(led.sem(f"weights_in_{n % RING}"), 16 * (n // RING + 1))
                        if j >= SPLITS:
                            act.wait_ge(*of("cut_used", j - SPLITS))
                        A.activation(w_hi[:, j % SPLITS, :], ring[:, n % RING, :], ACT.Copy).then_inc(
                            *did("weight_upper", j))
                led.fixed = False

            def due(name, key):
                event = of(name, key)
                work_ahead(ahead(led.taken))
                return event

            def upper(dst, k, src, ready, done):
                act.wait_ge(*due(*ready))
                A.activation(dst[0][:, k, :], src, ACT.Copy).then_inc(*did(*done))

            def squares(n, ready):
                for k in range(KD):
                    if ready is not None:
                        act.wait_ge(*due(*ready(k)))
                    A.activation(sq[:, k, :], X[:, k, :], ACT.Square).then_inc(*did("squares", (n, k)))

            def root_of(n, w=2):
                act.wait_ge(*due("mean_square", n))
                A.activation(root[:, 1, 0:w], root[:, 0, 0:w], ACT.Sqrt).then_inc(*did("root", n))

            def shift(n, sh):
                for k in range(KD):
                    act.wait_ge(*due("scaled", (n, k)))
                    A.activation(xn[:, k, :], xn[:, k, :], ACT.Identity, bias=sh(k)).then_inc(
                        *did("normed", (n, k)))
                    upper(xn_hl, k, xn[:, k, :], ("normed", (n, k)), ("normed_upper", (n, k)))

            def ffn(s):
                for f in range(KF + 1):
                    if f < KF:
                        act.wait_ge(*due("gate_raw", (s, f)))
                        if f >= 2:
                            act.wait_ge(*due("hidden_lower", (s, f - 2)))
                        A.activation(silu[:, f % 2, :], cols(held["gate_raw", (s, f)]), ACT.Silu).then_inc(
                            *did("silu", (s, f)))
                    if f:
                        upper(hid_hl, f - 1, silu[:, (f - 1) % 2, :], ("hidden", (s, f - 1)),
                              ("hidden_upper", (s, f - 1)))

            def mix(l, s):
                for i in range(KQ + KKV):
                    act.wait_ge(*due("in_raw", (l, i)))
                    A.activation(latent[:, i, :], cols(held["in_raw", (l, i)]), ACT.Copy).then_inc(*did("latent", (l, i)))
                    A.activation(wk[:, i, :], cols(held["in_raw", (l, i)]), ACT.Square).then_inc(*did("squares", (("m", l), i)))
                for i in range(2, 4):
                    act.wait_ge(*due("in_raw", (l, 5 + i)))
                    A.activation(kv_t[:, i, :], cols(held["in_raw", (l, 5 + i)]), ACT.Copy).then_inc(*did("kv_attn", (l, i)))
                root_of(("m", l), 4)
                for i in range(HPG):
                    act.wait_ge(*due("in_raw", (l, 9 + i)))
                    A.activation(q_t[:, i, :], cols(held["in_raw", (l, 9 + i)]), ACT.Copy, scale=DK ** -0.5).then_inc(
                        *did("q", (l, i)))
                act.wait_ge(*due("tok_raw", (l, 2)))
                A.activation(rope_k[NOPE:QH, :], bank[NOPE:QH, held["tok_raw", (l, 2)], 0:S], ACT.Copy).then_inc(
                    *did("rope_key", l))
                for t in range(QT):
                    A.activation(vsw[:, t, :], cols(held["tok_raw", (l, t)], 2 * P), ACT.Copy).then_inc(
                        *did("vsw", (l, t)))
                    A.activation(gates[:, t, :], cols(held["tok_raw", (l, t)], 3 * HEADS, 2 * P), ACT.Exp, scale=-1.0
                                 ).then_inc(*did("gate_exp", (l, t)))
                act.wait_ge(*due("cmp_raw", (l, 1, 1)))
                for g in range(GROUPS):
                    A.activation(cmp_h[:, g, :, 0:NCMP],
                                 bank[0:DK, 6 + g, 0:2 * CMP_STRIDE].rearrange("p (v n) -> p v n", v=2)[:, :, 0:NCMP],
                                 ACT.Gelu_apprx_tanh).then_inc(*did("cmp_hidden", (l, g)))
                for p2 in range(HEADS // 2):
                    act.wait_ge(*due("uk_raw", (l, p2)))
                    A.activation(kh[0:DK, 2 * p2:2 * p2 + 2, :],
                                 bank[0:DK, held["uk_raw", (l, p2)], :].rearrange("p (h t) -> p h t", h=2), ACT.Copy
                                 ).then_inc(*did("k_nope", (l, p2)))
                for p2 in range(HEADS // 2):
                    act.wait_ge(*due("uq_raw", (l, p2)))
                    A.activation(qh[0:QH, 2 * p2:2 * p2 + 2, :],
                                 bank[0:QH, held["uq_raw", (l, p2)], :].rearrange("p (h t) -> p h t", h=2), ACT.Copy,
                                 scale=QH ** -0.5).then_inc(*did("q_mla_scaled", (l, p2)))

                def exps(u):
                    kind, g, q = UNITS[u]
                    w = width(kind, q)
                    act.wait_ge(*due("neg_max", (l, u)))
                    if u >= 2:
                        act.wait_ge(*due("probs", (l, u - 2)))
                    for j in range(HPG):
                        s_ = scores[:, u % 2, j, 0:w]
                        A.activation(s_, s_, ACT.Exp, bias=nmax[:, u % 2, j:j + 1],
                                     accum_out=den[:, u % 2, j:j + 1]).then_inc(
                            *did("exp", (l, u, j), also=[("exps", (l, u))] if j == HPG - 1 else []))

                def merge(m):
                    act.wait_ge(*due("merge_raw", (l, m)))
                    A.activation(gm[:, m, :], cols(merge_bank(m)), ACT.Copy).then_inc(*did("merge", (l, m)))

                def back(u):
                    kind, g, q = UNITS[u]
                    n, kk = (NCMP, 1) if kind == "cmp" else (P, q + 1)
                    act.wait_ge(*due("prob_t_raw", (l, u)))
                    if u >= 4:
                        act.wait_ge(*due("attn_raw", (l, PV_OF[u - 4])))
                    A.activation(prob_t[0:n, u % 4, 0:2, 0:kk, :],
                                 bank[0:n, 4, :].rearrange("p (j k q) -> p j k q", j=2, k=2)[:, :, 0:kk, :],
                                 ACT.Copy).then_inc(*did("prob_t_a", (l, u)))

                def out_t(i):
                    kind, g, q, us = PV[i]
                    act.wait_ge(*due("attn_raw", (l, i)))
                    o = (oa_hl if kind == "a" else ob_hl)[0]
                    r = slice(DK * g, DK * g + DK)
                    A.activation(o[r, :, q * P:(q + 1) * P],
                                 bank[r, 6 + i % 2, :].rearrange("p (j q) -> p j q", j=HPG), ACT.Copy).then_inc(
                        *did("attn_upper", (l, i)))

                for m in range(MERGES_FIRST):
                    merge(m)
                exps(0)
                todo = []
                for u in range(NU):
                    if u + 1 < NU:
                        exps(u + 1)
                    if u + MERGES_FIRST < MERGE:
                        merge(u + MERGES_FIRST)
                    back(u)
                    if todo:
                        out_t(todo.pop())
                    if u == PV[PV_OF[u]][3][-1]:
                        todo.append(PV_OF[u])
                out_t(todo.pop())
                for e in range(2):
                    act.wait_ge(*due("merge", (l, MERGE - 1)))
                    a = gm[:, e * KD:(e + 1) * KD, :]
                    A.activation(a, a, ACT.Sigmoid).then_inc(*did("merge_gate", (l, e)))
                for f in range(KD):
                    upper(xn_hl, f, xn[:, f, :], ("merged", (s, f)), ("merged_upper", (s, f)))

            act.dma_start(X[:, :, :], dram["x"]).then_inc(*did("x_in", 0, by=16))
            act.dma_start(consts[:, :], dram["consts"]).then_inc(*did("consts_in", 0, by=16))
            act.wait_ge(*due("vecs_in", 0))
            A.activation(c_act[:, :], vec("c", 0, KD), ACT.Silu).then_inc(*did("c_act", 0))
            act.wait_ge(*due("x_in", 0))
            squares(0, None)
            root_of(0)
            for l in range(DEPTH):
                for s3 in range(3):
                    n = 3 * l + s3
                    shift(n, lambda k: mods(l, 3 * s3, k))
                    if n == 0:
                        act.dma_start(attn_consts, dram["attn_consts"]).then_inc(
                            *did("attn_consts_in", 0, by=16))
                        act.dma_start(w2[:, :, :], dram["w2"]).then_inc(*did("w2_in", 0, by=16))
                    if s3 == 1:
                        mix(l, n)
                    else:
                        ffn(n)
                    squares(n + 1, lambda k: ("residual", (n, k)))
                    root_of(n + 1)
            def squares2(n, src, ready):
                for k in range(KD):
                    if ready is not None:
                        act.wait_ge(*due(*ready(k)))
                    A.activation(t_sq[:, k, :], src[:, k, :], ACT.Square).then_inc(*did("squares", (n, k)))

            def evac(raw, key, dst, done, func=ACT.Copy, ps=None, **more):
                act.wait_ge(*due(raw, key))
                A.activation(dst, cols(held[raw, key]) if ps is None else ps, func, **more).then_inc(
                    *did(done, key))

            def mixed(s, n, bias=None):
                for f in range(KD):
                    act.wait_ge(*due("down_raw", (s, f)))
                    more = {"bias": bias(f)} if bias else {}
                    ps = cols(held["down_raw", (s, f)])
                    A.activation(t_out[:, f, :], ps, ACT.Identity, **more).then_inc(*did("mixed", (s, f)))
                    A.activation(t_sq[:, f, :], ps, ACT.Square, **more).then_inc(
                        *did("squares", (n, f), also=[("mixed_sq", (s, f))]))
                root_of(n)

            def recurrent(i):
                act.wait_ge(*due("lam_abs", 0))
                A.activation(lam[:, 2, :], lam[:, 1, :], ACT.Exp, scale=-1.0).then_inc(*did("lam_exp", 0))
                act.wait_ge(*due("lam_exp", 0))
                A.activation(lam[:, 2, :], lam[:, 2, :], ACT.Ln, bias=1.0).then_inc(*did("lam_ln", 0))
                for f in range(KD, 2 * KD + 1):
                    if f < 2 * KD:
                        evac("lru_in_raw", f, u_pad[:, f - KD, CONV - 1:], "lru_in", ACT.Identity,
                             bias=vec("b_in", f))
                    if f > KD:
                        k = f - KD - 1
                        upper(conv_hl, k, conv[:, k, :], ("conv", k), ("conv_upper", k))
                for f in range(KD):
                    evac("lru_in_raw", f, y_br[:, f, :], "lru_in", ACT.Gelu_apprx_tanh, bias=vec("b_in", f))
                for g, dst in ((0, rg), (1, ig)):
                    for f in range(KD):
                        evac("lru_gate_raw", (g, f), dst[:, f, :], "lru_gate", ACT.Sigmoid,
                             bias=vec("gate_b", g * KD + f))
                act.wait_ge(*due("lam", 0))
                act.wait_ge(*due("lru_gate", (0, KD - 1)))
                for k in range(KD):
                    A.activation(decay[:, k, :], rg[:, k, :], ACT.Exp, scale=lam[:, 3, k:k + 1]).then_inc(
                        *did("lru_decay", k))
                    A.activation(th[:, k, :], rg[:, k, :], ACT.Tanh, scale=lam[:, 2, k:k + 1]).then_inc(
                        *did("lru_tanh", k))
                keys(i, range(2))
                for k in range(KD):
                    act.wait_ge(*due("lru_mult_sq", k))
                    A.activation(lru_b[:, k, :], lru_b[:, k, :], ACT.Sqrt).then_inc(*did("lru_mult", k))
                keys(i, range(2, 4))
                for k in range(KD):
                    upper(lru_hl, k, lru_h[:, k, :], ("lru_gated", k), ("lru_upper", k))
                    if k % 2:
                        keys(i, [4 + k // 2])
                mixed((i, 0), (i, 1), lambda f: vec("b_out", f))

            def keys(i, fs=range(KD)):
                for f in fs:
                    evac("mem_k_raw", (i, f), k2[:, f, :], "mem_k")

            def cross(i):
                for f in range(KD):
                    evac("mem_q_raw", (i, f), q2[:, f, :], "mem_q", scale=256 ** -0.5)
                for q in range(QT):
                    act.wait_ge(*due("mem_neg_max", (i, q)))
                    for h in range(MH):
                        A.activation(sc2[:, q, h, :],
                                     bank[:, 4 + 2 * q + h // 2, (h % 2) * S:(h % 2 + 1) * S], ACT.Exp,
                                     bias=nmax[:, q, h:h + 1], accum_out=den[:, q, h:h + 1]).then_inc(
                            *did("mem_exp", (i, q, h), also=[("mem_exps", (i, q))] if h == MH - 1 else []))
                for e in range(2):
                    act.wait_ge(*due("mem_v_raw", (i, e)))
                    b = held["mem_v_raw", (i, e)]
                    A.activation(v2[:, :, e * 512:(e + 1) * 512], bank[:, b:b + 2, :], ACT.Copy).then_inc(
                        *did("mem_v", (i, e)))
                for q in range(QT):
                    act.wait_ge(*due("mem_prob_t_raw", (i, q)))
                    A.activation(pt2[:, q, 0:2, :, :],
                                 bank[:, 4 + 2 * q, :].rearrange("p (j k q) -> p j k q", j=2, k=2),
                                 ACT.Copy).then_inc(*did("mem_prob_t_a", (i, q)))
                for q in range(QT):
                    act.wait_ge(*due("mem_out_raw", (i, q)))
                    A.activation(o2_hl[0][:, :, q * P:(q + 1) * P],
                                 bank[:, 2 * q:2 * q + 2, :].rearrange("p b (f q) -> p (b f) q", f=4),
                                 ACT.Copy).then_inc(*did("mem_out_upper", (i, q)))
                mixed((i, 1), (i, 3))

            def mlp(i):
                for f in range(KF2 + 1):
                    if f < KF2:
                        act.wait_ge(*due("relu_raw", (i, f)))
                        if f >= 2:
                            act.wait_ge(*due("hidden2_lower", ((i, 2), f - 2)))
                        A.activation(silu[:, f % 2, :], cols(held["relu_raw", (i, f)]), ACT.Relu).then_inc(
                            *did("relu", (i, f)))
                    if f:
                        upper(hid2_hl, f - 1, silu[:, (f - 1) % 2, :], ("hidden2", (i, f - 1)),
                              ("hidden2_upper", (i, f - 1)))
                mixed((i, 2), (i, 5))

            def delta_mixer(i):
                act.dma_start(delta_consts[:, :], dram["delta_consts"]).then_inc(
                    *did("delta_consts_in", 0, by=16))

                def xs_upper(j):
                    for k in range(KD):
                        upper(xs_hl[j % 2], k, xs_t[j % 2][:, k, :], ("xs", (j, k)), ("xs_upper", (j, k)))

                xs_upper(0)
                xs_upper(1)
                for j, dst in enumerate((r_t, k_t, v_t)):
                    for f in range(KD):
                        evac("rkv_raw", (j, f), dst[:, f, :], "rkv")
                    if j == 0:
                        xs_upper(2)
                for j, wd, fn, dst, fn2, b in ((3, RN, ACT.Tanh, sg_t, ACT.Sigmoid, "w0"),
                                               (4, RN, ACT.Copy, aa_t, ACT.Sigmoid, "a0"),
                                               (5, P, ACT.Sigmoid, g_t, ACT.Copy, None)):
                    act.wait_ge(*due("rkv_raw", (j, KD - 1)))
                    if j == 5:
                        act.wait_ge(*due("lora_raw", (3, KD - 1)))
                    A.activation(silu[0:wd, j % 2, :], bank[0:wd, held["rkv_raw", (j, KD - 1)], 0:S],
                                 fn).then_inc(*did("lora", j))
                    for f in range(KD):
                        more = {"bias": vec(b, f)} if b else {}
                        evac("lora_raw", (j, f), dst[:, f, :], "lora_out", fn2, **more)
                for k in range(KD):
                    act.wait_ge(*due("kk", k))
                    A.activation(bt[:, k, :], kk_t[:, k, :], ACT.Square).then_inc(*did("kk_sq", k))
                act.wait_ge(*due("head_sums", "kk"))
                A.activation(stat[:, 0, :], bank[:, 6, 0:QT * RH], ACT.Sqrt).then_inc(
                    *did("head_root", "kk", also=[("head_sums_read", "kk")]))
                act.wait_ge(*due("before_sum", 0))
                A.activation(kt_, xn[:, :, :], ACT.Exp, scale=E_HALF).then_inc(*did("exp_minus", 0))
                A.activation(exp_plus, xn[:, :, :], ACT.Exp, scale=-E_HALF)
                A.activation(sg_t, sg_t, ACT.Exp, scale=-E_HALF).then_inc(*did("exp_plus", 0))
                for c in range(NCH):
                    chunk(c)
                for b in range(4):
                    act.wait_ge(*due("head_used", ("mean", b)))
                    A.activation(slot[3][:, 2 * b:2 * b + 2, :], xn[:, 2 * b:2 * b + 2, :], ACT.Square
                                 ).then_inc(*did("yc_sqs", b, also=[("yc_sq", 2 * b), ("yc_sq", 2 * b + 1)]))
                act.wait_ge(*due("head_var", 0))
                A.activation(stat[:, 3, :], stat[:, 3, :], ACT.Sqrt).then_inc(*did("head_root", "var"))
                for k in range(KD):
                    upper(xn_hl, k, xn[:, k, :], ("delta_out", k), ("delta_upper", k))
                keys(i)
                mixed((i, 0), (i, 1))

            def chunk(c):
                lo = slice(0, CH)
                ts = slice(c * CH, (c + 1) * CH)
                for m in range(3):
                    for e in range(2):
                        act.wait_ge(*due("tm_raw", (c, m, e)))
                        if c:
                            act.wait_ge(*due("y_chunk_raw", c - 1))
                        A.activation(tm[:, m, e * 512:(e + 1) * 512], bank[lo, 2 * m + e, :], ACT.Copy
                                     ).then_inc(*did("tm", (c, m, e)))
                for n in range(1, LEVELS):
                    for p in range(2):
                        act.wait_ge(*due("y_raw", (c, n, p)))
                        A.activation(yi[:, p * 8:p * 8 + 8, :],
                                     bank[lo, p, :].rearrange("p (h t) -> p h t", h=8), ACT.Copy).then_inc(
                            *did("y_inv", (c, n, p)))
                act.wait_ge(*due("q_state_raw", c))
                A.activation(mi, bank[lo, 0:2, :].rearrange("p b (k t) -> p (b k) t", t=CH), ACT.Copy
                             ).then_inc(*did("q_state", c))
                act.wait_ge(*due("sa_raw", c))
                A.activation(yi, bank[lo, 4:6, :].rearrange("p b (k t) -> p (b k) t", t=CH), ACT.Copy
                             ).then_inc(*did("sa", c))
                act.wait_ge(*due("y_state_raw", c))
                for p in range(2):
                    r = slice(RN * p, RN * p + RN)
                    A.activation(xn[r, :, ts], bank[r, 6 + p, :].rearrange("p (k t) -> p k t", k=KD),
                                 ACT.Copy).then_inc(*did("y_half", (c, p), also=[("y_state", c)] if p else []))

            act.dma_start(slot[10], dram["mem"]).then_inc(*did("mem_in", 0, by=16))
            act.wait_ge(*due("mem_in", 0))
            squares2("mem", slot[10], None)
            root_of("mem")
            squares2((0, 0), X, lambda k: ("x_second", (6, k)))
            root_of((0, 0))

            def normed_upper(n):
                for k in range(KD):
                    upper(xn_hl, k, xn[:, k, :], ("normed2", (n, k)), ("normed_upper", (n, k)))

            normed_upper((0, 0))
            for i in range(DEPTH):
                if i == 0:
                    recurrent(i)
                else:
                    delta_mixer(i)
                squares2((i, 2), X, lambda k: ("x_added", ((i, 1), k)))
                root_of((i, 2))
                normed_upper((i, 2))
                cross(i)
                squares2((i, 4), X, lambda k: ("x_added", ((i, 3), k)))
                root_of((i, 4))
                normed_upper((i, 4))
                mlp(i)
                if i + 1 < DEPTH:
                    squares2((i + 1, 0), X, lambda k: ("x_added", ((i, 5), k)))
                    root_of((i + 1, 0))
            work_ahead(len(kinds))

        @block.gpsimd
        def _(pool):
            led.taken = 0
            G = nc.gpsimd
            rr = slice(NOPE, QH)

            def ada_products(chunks):
                for i in chunks:
                    n = slot_of[i]
                    pool.wait_ge(led.sem(f"weights_in_{n % RING}"), 16 * (n // RING + 1))
                    w = ring[:, n % RING, :].rearrange("p (k c) -> p k c", k=KD)
                    G.tensor_tensor(w, w, bcast(c_act[:, :], P), ALU.mult).then_inc(
                        *did("ada_product", i))

            def ada_of(s):
                return [i for step in range(KF + KD) for i, _ in ada_chunks(s, step)]

            pool.wait_ge(*of("c_act", 0))
            ada_products([i for i in beside if i < ADA_PARTS[0][1]])
            for l in range(DEPTH):
                ada_products(ada_of(3 * l))
                if l == 0:
                    pool.wait_ge(*of("attn_consts_in", 0))
                for p2 in range(-1, HEADS // 2):
                    w = 1 if p2 < 0 else 2
                    pool.wait_ge(*of("rot_raw", (l, p2)))
                    x = rope_k[rr, :].rearrange("p (h t) -> p h t", h=1) if p2 < 0 else qh[rr, 2 * p2:2 * p2 + 2, :]
                    G.tensor_tensor(x, x, bcast_mid(const("cos")[rr, :], w), ALU.mult).then_inc(
                        *did("rope_cos", (l, p2)))
                    if p2 == 0:
                        pool.wait_ge(*of("rope_k", l))
                        G.tensor_copy(kh[rr, :, :], bcast_mid(rope_k[rr, :], HEADS)).then_inc(*did("k_mla", l))
                for u in range(NU):
                    kind, g, q = UNITS[u]
                    w = width(kind, q)
                    pool.wait_ge(*of("prob_scale", (l, u)))
                    s_ = scores[:, u % 2, :, 0:w]
                    G.tensor_tensor(s_, s_, bcast(den[:, u % 2, :], w), ALU.mult).then_inc(*did("probs", (l, u)))
                ada_products(ada_of(3 * l + 2))
            for i in range(DEPTH):
                if i == 1:
                    pool.wait_ge(*of("b_scaled", 0))
                    G.tensor_tensor(kt_, kt_, k_t, ALU.mult).then_inc(*did("k_scaled", 0))
                    for c in range(NCH):
                        for n in range(LEVELS):
                            for p in range(2):
                                if n == 0:
                                    for r in range(4):
                                        pool.wait_ge(*of("mats", (c, r, p)))
                                    if c:
                                        pool.wait_ge(*of("sa_raw", c - 1))
                                else:
                                    pool.wait_ge(*of("y_raw", (c, n - 1, p)))
                                    pool.wait_ge(*of("inv_t", (c, 0, p)))
                                lv = const("levels")[0:CH, n * CH:(n + 1) * CH]
                                G.tensor_tensor(mi[:, p * 8:p * 8 + 8, :], mats[:, p * 8:p * 8 + 8, 0:CH],
                                                bcast_mid(lv, 8), ALU.mult).then_inc(*did("level", (c, n, p)))
                for q in range(QT):
                    pool.wait_ge(*of("mem_rden", (i, q)))
                    G.tensor_tensor(sc2[:, q], sc2[:, q], bcast(den[:, q, :], S), ALU.mult).then_inc(
                        *did("mem_probs", (i, q)))

    return led.events, order


def tiles(w):
    k, f = w.shape
    t = w.reshape(k // P, P, f // P, P).transpose(2, 0, 1, 3)
    return np.ascontiguousarray(t.reshape(-1, TILES, P, P).transpose(0, 2, 1, 3)).reshape(-1, P, CW)


def columns(v):
    return v.reshape(-1, P).T


def laid_out(x):
    a = {k: np.asarray(v) for k, v in x.items()}
    L = range(DEPTH)
    cut = np.cumsum([0, 512, 128, 128, 128, 128, 128, 128, 24, QRANK, KVRANK, ROPE, 2 * D])
    q, kc, vc, ks, vs, kw, vw, gn, cq, ckv, kr, gm = (slice(cut[i], cut[i + 1]) for i in range(12))
    pair = np.concatenate([np.arange((g * HPG + j) * DK, (g * HPG + j + 1) * DK)
                           for j in range(HPG) for g in range(GROUPS)])
    d = {}
    d["x"] = a["x"][0].T.reshape(KD, P, S).transpose(1, 0, 2)
    d["consts"] = np.concatenate([CONSTS[k] for k in CONSTS if k not in ATTN + DELTA], 1)
    d["delta_consts"] = np.concatenate([CONSTS[k] for k in DELTA], 1)
    d["attn_consts"] = np.concatenate([CONSTS[k] for k in ATTN], 1)
    pe = np.stack([np.concatenate([a[n][l].T] * 2, 0) for l in L for n in ("cmpk_pe", "cmpv_pe")], 1)
    d["vecs"] = np.concatenate(
        [columns(a["b_ada"].reshape(-1)), columns(a["c"][0]), columns(a["final_norm"]),
         columns(a["mla_q_norm"].reshape(-1)), columns(a["mla_kv_norm"].reshape(-1)),
         pe.reshape(P, -1), columns(a["ln_gains_2"].reshape(-1)),
         *(columns(a[n].reshape(-1)) for n in (
             "mem_norm_2", "a_conv_w_2", "a_conv_b_2", "a_b_in_2", "a_gate_b_2", "a_lambda_2",
             "a_b_out_2", "b_mu_2", "b_w0_2", "b_a0_2", "b_k_k_2", "b_k_a_2", "b_r_k_2",
             "b_gn_g_2", "b_gn_b_2"))], 1)
    d["w2"] = np.stack([a[n][l] for l in L for n in ("cmpk_w2", "cmpv_w2")], 1)
    each = lambda f: np.concatenate([f(l) for l in L])
    d["w_ada"] = each(lambda l: tiles(a["w_ada"][l]))
    for n in ("ffn1_gate", "ffn1_up", "ffn1_down", "ffn2_gate", "ffn2_up", "ffn2_down", "w_out"):
        d[n] = each(lambda l: tiles(a[n][l]))
    w = a["w_in"]
    d["w_in"] = each(lambda l: tiles(np.concatenate(
        [w[l][:, cq], w[l][:, ckv], w[l][:, kc], w[l][:, vc], w[l][:, ks], w[l][:, kw],
         w[l][:, q][:, pair], w[l][:, gm]], 1)))
    tok = [np.concatenate([w[l][:, s] for s in (vs, vw, gn, kr)], 1).reshape(KD, P, TOKW) for l in L]
    pad = np.zeros((1, P, TOKW), np.float32)
    d["w_tok"] = np.stack([np.concatenate([t, pad])[3 * c:3 * c + 3].transpose(1, 0, 2).reshape(P, -1)
                           for t in tok for c in range(3)])
    w1 = [a[n][l].reshape(2, CMP_STRIDE, DK, DK).transpose(0, 2, 1, 3).reshape(2, DK, -1)
          for l in L for n in ("cmpk_w1", "cmpv_w1")]
    d["cmp_w1"] = np.concatenate([np.concatenate([v, v], 1) for v in w1])
    for n in ("w_uk", "w_uv"):
        d[n] = a["mla_" + n].reshape(DEPTH, KKV, P, 512).transpose(0, 2, 1, 3).reshape(DEPTH, P, -1)
    uq = a["mla_w_uq"].reshape(DEPTH, KQ, P, HEADS, QH).transpose(0, 3, 1, 2, 4)
    d["w_uq"] = uq.reshape(DEPTH * 3, TILES, P, QH).transpose(0, 2, 1, 3).reshape(DEPTH * 3, P, -1)
    d["w_a"] = each(lambda l: tiles(a["w_branch_a"][l][pair]))
    d["w_b"] = each(lambda l: tiles(a["w_branch_b"][l][pair]))
    d["mem"] = a["mem_2"][0].T.reshape(KD, P, S).transpose(1, 0, 2)
    d["a_w_in"] = tiles(a["a_w_in_2"][0])
    gw = a["a_gate_w_2"][0].reshape(2 * LRU_HEADS, 2, P, 2, P).transpose(0, 3, 1, 2, 4)
    d["a_gate_w"] = gw.reshape(-1, TILES, P, P).transpose(0, 2, 1, 3).reshape(-1, P, CW)
    d["a_w_out"] = tiles(a["a_w_out_2"][0])
    d["b_w_rkv"] = np.concatenate([tiles(a["b_w_rkv_2"][0][j]) for j in range(3)])
    d["b_w_o"] = tiles(a["b_w_o_2"][0])
    lora = [a[n][0].reshape(KD, P, -1).transpose(1, 0, 2).reshape(P, -1)
            for n in ("b_w1_2", "b_a1_2", "b_g1_2")]
    d["lora1"] = np.stack([np.pad(v, ((0, 0), (0, CW - v.shape[1]))) for v in lora])
    lora = [a[n][0] for n in ("b_w2_2", "b_a2_2", "b_g2_2")]
    d["lora2"] = np.stack([np.pad(v, ((0, P - v.shape[0]), (0, 0))) for v in lora])
    for n in ("c_w_q", "c_w_o", "m_w_up", "m_w_down"):
        d[n] = each(lambda l: tiles(a[n + "_2"][l]))
    d["c_w_kv"] = each(lambda l: tiles(a["c_w_kv_2"][l][:, 0:D]))
    d["c_w_v"] = a["c_w_kv_2"][:, :, D:].reshape(DEPTH, KD // 2, 2, P, 2, 512).transpose(
        0, 4, 1, 3, 2, 5).reshape(-1, P, CW)
    return {k: np.ascontiguousarray(v) for k, v in d.items()}


def build(scrap, nc, shapes):
    seen, stream = None, []
    for target in (*scrap, nc):
        dram = {k: target.dram_tensor(k + "_dram", s, F32, kind="ExternalInput").ap()
                for k, s in shapes.items()}
        out = target.dram_tensor("out_dram", (P, KD, S), F32, kind="ExternalOutput").ap()
        seen, stream = program(target, dram, out, seen, stream)
    return nc


def kernel(**inputs):
    import concourse.bacc as bacc
    from concourse.bass_utils import run_bass_kernel_spmd as run

    arrays = laid_out(inputs)
    *scrap, nc = (bacc.Bacc("TRN2", target_bir_lowering=False, num_devices=1) for _ in range(4))
    build(scrap, nc, {k: v.shape for k, v in arrays.items()})
    r = run(nc, [{k + "_dram": v for k, v in arrays.items()}], core_ids=[0])
    y = r.results[0]["out_dram"]
    return y.transpose(1, 0, 2).reshape(D, S).T.reshape(1, S, D).copy()
```
